# Optimizing a Trainium2 kernel written in Bass

```python
import jax, jax.numpy as jnp
from jax import lax
import numpy as np
import math

D_MODEL = 1024
BATCH = 1
SEQ = 512
DEPTH = 1

GRID_W = 64
CTX_LEN = 256
EPS = 1e-6
N_MOD = 6
SGU_WIDTH = 1024
SGU_CHUNK = 128
SGU_GROUPS = 8
SGU_GROUP_DIM = SGU_WIDTH // SGU_GROUPS
GLA_HEADS = 4
GLA_KEY_DIM = D_MODEL // 2
GLA_VAL_DIM = D_MODEL
GLA_HEAD_K = GLA_KEY_DIM // GLA_HEADS
GLA_HEAD_V = GLA_VAL_DIM // GLA_HEADS
GLA_RANK = 16
GLA_GATE_NORMALIZER = 16.0
GLA_CHUNK = 64
D_FF = 2816
CONV_K = 3

IN_SPLITS = (SGU_WIDTH, SGU_WIDTH, GLA_KEY_DIM, GLA_VAL_DIM, D_MODEL, D_MODEL, GLA_KEY_DIM, GLA_VAL_DIM, 2 * GLA_RANK)
D_IN = sum(IN_SPLITS)
OFF_KVG = sum(IN_SPLITS[:6])


def _split(z, sizes):
    offs = [int(o) for o in np.cumsum(sizes)[:-1]]
    return jnp.split(z, offs, axis=-1)

def _rms_norm(x, g):
    xf = x.astype(jnp.float32)
    y = xf * lax.rsqrt(jnp.mean(xf * xf, axis=-1, keepdims=True) + EPS)
    return (y * g.astype(jnp.float32)).astype(x.dtype)

def _layer_norm(x, g, b):
    xf = x.astype(jnp.float32)
    mu = jnp.mean(xf, axis=-1, keepdims=True)
    var = jnp.mean(jnp.square(xf - mu), axis=-1, keepdims=True)
    y = (xf - mu) * lax.rsqrt(var + EPS)
    return (y * g.astype(jnp.float32) + b.astype(jnp.float32)).astype(x.dtype)

def _modulate(h, shift, scale):
    return h * (1 + scale) + shift

def _spatial_gating(u, vs, ln_g, ln_b, w_s, b_s):
    bsz, length, _ = u.shape
    n = length // SGU_CHUNK
    vn = _layer_norm(vs, ln_g, ln_b).reshape(bsz, n, SGU_CHUNK, SGU_GROUPS, SGU_GROUP_DIM)
    s = jnp.einsum('gpq,bnqgc->bnpgc', w_s, vn) + b_s.T[:, :, None]
    return u * s.reshape(bsz, length, SGU_WIDTH)

def _heads(a, hd):
    return a.reshape(a.shape[0], a.shape[1], GLA_HEADS, hd).astype(jnp.float32)

def _log_decay(lr, w2, b2):
    z = (lr @ w2 + b2).astype(jnp.float32)
    la = jax.nn.log_sigmoid(z) / GLA_GATE_NORMALIZER
    return la.reshape(lr.shape[0], lr.shape[1], GLA_HEADS, GLA_HEAD_K)

def _gla_direction(q, k, v, log_a, s0):
    bsz, t, h, _ = k.shape
    n = t // GLA_CHUNK

    def chunks(a):
        return a.reshape(bsz, n, GLA_CHUNK, h, a.shape[-1])

    k, v, log_a = chunks(k), chunks(v), chunks(log_a)
    b = jnp.cumsum(log_a, axis=2)
    b_last = b[:, :, -1:]
    k_dec = k * jnp.exp(b_last - b)
    cm = lambda a: jnp.moveaxis(a, 1, 0)
    xs_state = (cm(k_dec), cm(v), cm(jnp.exp(b_last[:, :, 0])))

    if q is None:
        def step_state(s, xs):
            kd, vv, dec = xs
            return dec[..., None] * s + jnp.einsum('bchk,bchv->bhkv', kd, vv), None
        s_final, _ = lax.scan(step_state, s0, xs_state)
        return None, s_final

    q = chunks(q)
    q_dec = q * jnp.exp(b)
    k_inv = k * jnp.exp(-b)
    mask = jnp.tril(jnp.ones((GLA_CHUNK, GLA_CHUNK), dtype=bool))
    scores = jnp.where(mask, jnp.einsum('bnchk,bnshk->bnhcs', q_dec, k_inv), 0.0)
    o_intra = jnp.einsum('bnhcs,bnshv->bnchv', scores, v)

    def step(s, xs):
        qd, kd, vv, dec = xs
        o = jnp.einsum('bchk,bhkv->bchv', qd, s)
        return dec[..., None] * s + jnp.einsum('bchk,bchv->bhkv', kd, vv), o

    s_final, o_inter = lax.scan(step, s0, (cm(q_dec),) + xs_state)
    o = o_intra + jnp.moveaxis(o_inter, 0, 1)
    return o.reshape(bsz, t, h, -1), s_final

def _gla_bidir(q, k, v, lr, w2, b2, s0f, s0b):
    la_f = _log_decay(lr[..., :GLA_RANK], w2[0], b2[0])
    la_b = _log_decay(lr[..., GLA_RANK:], w2[1], b2[1])
    flip = lambda a: None if a is None else a[:, ::-1]
    o_f, s_f = _gla_direction(q, k, v, la_f, s0f)
    o_b, s_b = _gla_direction(flip(q), flip(k), flip(v), flip(la_b), s0b)
    o = None if q is None else o_f + flip(o_b)
    return o, s_f, s_b

def _token_mixer(h, w_in, sgu_ln_g, sgu_ln_b, sgu_w, sgu_b, gla_w2, gla_b2, gla_norm_g,
                 w_br_a, w_br_b, w_o, s0f, s0b):
    z = h @ w_in
    u, vs, q, r, ga, gb, k, v, lr = _split(z, IN_SPLITS)
    a = _spatial_gating(jax.nn.gelu(u, approximate=False), jax.nn.gelu(vs, approximate=False),
                        sgu_ln_g, sgu_ln_b, sgu_w, sgu_b)
    qh = _heads(q, GLA_HEAD_K) * (GLA_HEAD_K ** -0.5)
    o, s_f, s_b = _gla_bidir(qh, _heads(k, GLA_HEAD_K), _heads(v, GLA_HEAD_V), lr, gla_w2, gla_b2, s0f, s0b)
    o = o * lax.rsqrt(jnp.mean(o * o, axis=-1, keepdims=True) + EPS)
    o = o.reshape(h.shape[0], h.shape[1], GLA_VAL_DIM) * gla_norm_g.astype(jnp.float32)
    ob = o.astype(h.dtype) * jax.nn.silu(r)
    merged = jax.nn.sigmoid(ga) * (a @ w_br_a) + jax.nn.sigmoid(gb) * (ob @ w_br_b)
    return merged @ w_o, s_f, s_b

def _context_states(hc, w_in, gla_w2, gla_b2, s0):
    k, v, lr = _split(hc @ w_in[:, OFF_KVG:], IN_SPLITS[6:])
    _, s_f, s_b = _gla_bidir(None, _heads(k, GLA_HEAD_K), _heads(v, GLA_HEAD_V), lr, gla_w2, gla_b2, s0, s0)
    return s_f, s_b

def _conv_ffn(h, rows, w_up, conv_w, conv_b, w_down):
    bsz, length, _ = h.shape
    a, val = _split(h @ w_up, (D_FF, D_FF))
    img = a.reshape(bsz, rows, length // rows, D_FF)
    a = lax.conv_general_dilated(img, conv_w[:, :, None, :], (1, 1), 'SAME',
                                 dimension_numbers=('NHWC', 'HWIO', 'NHWC'),
                                 feature_group_count=D_FF) + conv_b
    return (jax.nn.gelu(a.reshape(bsz, length, D_FF), approximate=False) * val) @ w_down

def first_inputs(seed: int = 0) -> dict:
    key = jax.random.key(seed)
    ks = jax.random.split(key, 32)

    def nrm(k, shape, scale):
        return jax.random.normal(k, shape, jnp.float32) * scale

    def gain(k, shape):
        return 1.0 + nrm(k, shape, 0.1)

    D = D_MODEL
    return {
        "x": nrm(ks[0], (BATCH, SEQ, D), 1.0),
        "c": nrm(ks[1], (BATCH, D), 1.0),
        "ctx": nrm(ks[2], (BATCH, CTX_LEN, D), 1.0),
        "c_ctx": nrm(ks[3], (D,), 1.0),
        "w_ada": nrm(ks[4], (DEPTH, D, N_MOD * D), 0.5 * D ** -0.5),
        "b_ada": nrm(ks[5], (DEPTH, N_MOD * D), 0.01),
        "norm1_g": gain(ks[6], (DEPTH, D)),
        "norm2_g": gain(ks[7], (DEPTH, D)),
        "w_in": nrm(ks[8], (DEPTH, D, D_IN), D ** -0.5),
        "sgu_ln_g": gain(ks[9], (DEPTH, SGU_WIDTH)),
        "sgu_ln_b": nrm(ks[10], (DEPTH, SGU_WIDTH), 0.01),
        "sgu_w": nrm(ks[11], (DEPTH, SGU_GROUPS, SGU_CHUNK, SGU_CHUNK), 0.5 * SGU_CHUNK ** -0.5),
        "sgu_b": gain(ks[12], (DEPTH, SGU_GROUPS, SGU_CHUNK)),
        "gla_w2": nrm(ks[13], (DEPTH, 2, GLA_RANK, GLA_KEY_DIM), GLA_RANK ** -0.5),
        "gla_b2": nrm(ks[14], (DEPTH, 2, GLA_KEY_DIM), 0.1),
        "gla_norm_g": gain(ks[15], (DEPTH, GLA_VAL_DIM)),
        "w_br_a": nrm(ks[16], (DEPTH, SGU_WIDTH, D), SGU_WIDTH ** -0.5),
        "w_br_b": nrm(ks[17], (DEPTH, GLA_VAL_DIM, D), GLA_VAL_DIM ** -0.5),
        "w_o": nrm(ks[18], (DEPTH, D, D), D ** -0.5),
        "ffn_w_up": nrm(ks[19], (DEPTH, D, 2 * D_FF), D ** -0.5),
        "ffn_conv_w": nrm(ks[20], (DEPTH, CONV_K, CONV_K, D_FF), 1.0 / CONV_K),
        "ffn_conv_b": nrm(ks[21], (DEPTH, D_FF), 0.01),
        "ffn_w_down": nrm(ks[22], (DEPTH, D_FF, D), D_FF ** -0.5),
        "final_norm_g": gain(ks[23], (D,)),
    }

def first_block(x, c, ctx, c_ctx, w_ada, b_ada, norm1_g, norm2_g, w_in, sgu_ln_g, sgu_ln_b, sgu_w, sgu_b,
              gla_w2, gla_b2, gla_norm_g, w_br_a, w_br_b, w_o, ffn_w_up, ffn_conv_w, ffn_conv_b,
              ffn_w_down, final_norm_g):
    bsz, seq, _ = x.shape
    rows = seq // GRID_W
    s0 = jnp.zeros((bsz, GLA_HEADS, GLA_HEAD_K, GLA_HEAD_V), jnp.float32)
    for l in range(DEPTH):
        last = l == DEPTH - 1
        sh1x, sc1x, g1x, sh2x, sc2x, g2x = jnp.split((jax.nn.silu(c) @ w_ada[l] + b_ada[l])[:, None, :], N_MOD, axis=-1)
        sh1c, sc1c, g1c, sh2c, sc2c, g2c = jnp.split(jax.nn.silu(c_ctx) @ w_ada[l] + b_ada[l], N_MOD, axis=-1)
        tm = (w_in[l], sgu_ln_g[l], sgu_ln_b[l], sgu_w[l], sgu_b[l], gla_w2[l], gla_b2[l], gla_norm_g[l],
              w_br_a[l], w_br_b[l], w_o[l])
        hc = _modulate(_rms_norm(ctx, norm1_g[l]), sh1c, sc1c)
        if last:
            s_f, s_b = _context_states(hc, w_in[l], gla_w2[l], gla_b2[l], s0)
        else:
            y_c, s_f, s_b = _token_mixer(hc, *tm, s0, s0)
        hx = _modulate(_rms_norm(x, norm1_g[l]), sh1x, sc1x)
        y_x, _, _ = _token_mixer(hx, *tm, s_f, s_b)
        x = x + g1x * y_x
        hx2 = _modulate(_rms_norm(x, norm2_g[l]), sh2x, sc2x)
        x = x + g2x * _conv_ffn(hx2, rows, ffn_w_up[l], ffn_conv_w[l], ffn_conv_b[l], ffn_w_down[l])
        if not last:
            ctx = ctx + g1c * y_c
            hc2 = _modulate(_rms_norm(ctx, norm2_g[l]), sh2c, sc2c)
            ctx = ctx + g2c * _conv_ffn(hc2, 1, ffn_w_up[l], ffn_conv_w[l], ffn_conv_b[l], ffn_w_down[l])
    return _rms_norm(x, final_norm_g)


HY_WIDTH = 512
HY_GROUPS = 8
HY_ORDER = 2
HY_EMB = 33
HY_BANDS = (HY_EMB - 1) // 2
HY_FILT_HIDDEN = 64
HY_FAST_DECAY = 0.3
HY_SLOW_DECAY = 1.5
HY_DECAY_TARGET = 1e-2
HY_MAX_DECAY = math.log(HY_DECAY_TARGET) / HY_FAST_DECAY
HY_MIN_DECAY = math.log(HY_DECAY_TARGET) / HY_SLOW_DECAY
HY_COLS = 3 * HY_WIDTH

RW_WIDTH = 512
RW_HEAD = 64
RW_HEADS = RW_WIDTH // RW_HEAD
RW_LORA_W = 64
RW_LORA_A = 64
RW_LORA_G = 128
RW_GN_EPS = 64e-5
RW_SIZES = [RW_WIDTH, RW_WIDTH, RW_WIDTH, RW_LORA_W, RW_LORA_W, RW_LORA_A, RW_LORA_A, RW_LORA_G]
RW_OFFSETS = [sum(RW_SIZES[:i + 1]) for i in range(len(RW_SIZES) - 1)]
RW_COLS = sum(RW_SIZES)

GATE_COLS = 2 * D_MODEL
IN_COLS = HY_COLS + RW_COLS + GATE_COLS

FFN_HIDDEN = ((8 * D_MODEL + 3 * 256 - 1) // (3 * 256)) * 256

DN_ALPHA = (2.0 * DEPTH) ** 0.25
DN_BETA = (8.0 * DEPTH) ** -0.25
LN_EPS = 1e-5


def layer_norm(x, w, b):
    xf = x.astype(jnp.float32)
    mu = jnp.mean(xf, axis=-1, keepdims=True)
    var = jnp.mean(jnp.square(xf - mu), axis=-1, keepdims=True)
    return ((xf - mu) * lax.rsqrt(var + LN_EPS) * w + b).astype(x.dtype)

def shift_prev(z):
    return jnp.pad(z[:, :-1], ((0, 0), (1, 0), (0, 0)))

def shift_next(z):
    return jnp.pad(z[:, 1:], ((0, 0), (0, 1), (0, 0)))

def short_conv3(z, w, b):
    return w[0] * shift_prev(z) + w[1] * z + w[2] * shift_next(z) + b

def hyena_filters(L, fw1, fb1, fw2, fb2, fw3, fb3, fw4, sin_freq):
    f32 = jnp.float32
    t = jnp.linspace(0.0, 1.0, L, dtype=f32)[:, None]
    w = 2.0 * math.pi * jnp.arange(L, dtype=f32) / L
    f = jnp.linspace(1e-4, HY_BANDS - 1, HY_BANDS, dtype=f32)
    ang = w[:, None] * f[None, :]
    feats = jnp.concatenate([t, jnp.cos(ang), -jnp.sin(ang)], axis=-1)
    sf = sin_freq.astype(f32)
    h = jnp.sin(sf[0] * (feats @ fw1.astype(f32) + fb1.astype(f32)))
    h = jnp.sin(sf[1] * (h @ fw2.astype(f32) + fb2.astype(f32)))
    h = jnp.sin(sf[2] * (h @ fw3.astype(f32) + fb3.astype(f32)))
    h = (h @ fw4.astype(f32)).reshape(L, HY_ORDER, 2, HY_WIDTH)
    deltas = jnp.abs(jnp.linspace(HY_MIN_DECAY, HY_MAX_DECAY, HY_WIDTH, dtype=f32))
    window = jnp.exp(-t * deltas[None, :])
    return h * window[:, None, None, :]

def long_conv(z, h_fwd, h_bwd, d_skip):
    L = z.shape[1]
    n = 2 * L
    zf = jnp.fft.rfft(z, n=n, axis=1)
    hf = jnp.fft.rfft(h_fwd, n=n, axis=0) + jnp.conj(jnp.fft.rfft(h_bwd, n=n, axis=0))
    y = jnp.fft.irfft(zf * hf[None], n=n, axis=1)[:, :L]
    return y + z * d_skip

def hyena_mixer(u, conv_w, conv_b, fw1, fb1, fw2, fb2, fw3, fb3, fw4, sin_freq, skip):
    L = u.shape[1]
    u = short_conv3(u, conv_w, conv_b).astype(jnp.float32)
    v, x1, x2 = jnp.split(u, 3, axis=-1)
    h = hyena_filters(L, fw1, fb1, fw2, fb2, fw3, fb3, fw4, sin_freq)
    sk = skip.astype(jnp.float32)
    z = x1 * long_conv(v, h[:, 0, 0], h[:, 0, 1], sk[0])
    z = x2 * long_conv(z, h[:, 1, 0], h[:, 1, 1], sk[1])
    return z

def rwkv_step(S, inp):
    r, w, k, v, kk, a = inp
    sa = jnp.einsum('dbhvk,dbhk->dbhv', S, -kk)
    S = S * w[..., None, :] + sa[..., :, None] * (kk * a)[..., None, :] + v[..., :, None] * k[..., None, :]
    y = jnp.einsum('dbhvk,dbhk->dbhv', S, r)
    return S, y

def rwkv_mixer(u, mu, w0, w2, a0, a2, g2, k_k, k_a, r_k, gn_w, gn_b):
    f32 = jnp.float32
    B, L, _ = u.shape
    u = u + mu * (0.5 * (shift_prev(u) + shift_next(u)) - u)
    r, k, v, wd_f, wd_b, ad_f, ad_b, gd = jnp.split(u.astype(f32), RW_OFFSETS, axis=-1)
    d = w0.astype(f32)[:, None, None, :] + jnp.einsum('dblr,drc->dblc', jnp.tanh(jnp.stack([wd_f, wd_b])), w2.astype(f32))
    decay = jnp.exp(-math.exp(-0.5) * jax.nn.sigmoid(d))
    a = jax.nn.sigmoid(a0.astype(f32)[:, None, None, :] + jnp.einsum('dblr,drc->dblc', jnp.stack([ad_f, ad_b]), a2.astype(f32)))
    g = jax.nn.sigmoid(gd) @ g2.astype(f32)

    def heads(z):
        return z.reshape(z.shape[:-1] + (RW_HEADS, RW_HEAD))

    kk = heads(k * k_k.astype(f32))
    kk = kk / jnp.maximum(jnp.sqrt(jnp.sum(kk * kk, axis=-1, keepdims=True)), 1e-12)
    kd = heads(k[None] * (1.0 + (a - 1.0) * k_a.astype(f32)))
    r_h, v_h, w_h, a_h = heads(r), heads(v), heads(decay), heads(a)

    def dirs(z_f, z_b):
        return jnp.moveaxis(jnp.stack([z_f, z_b[:, ::-1]]), 2, 0)

    xs = (dirs(r_h, r_h), dirs(w_h[0], w_h[1]), dirs(kd[0], kd[1]),
          dirs(v_h, v_h), dirs(kk, kk), dirs(a_h[0], a_h[1]))
    S0 = jnp.zeros((2, B, RW_HEADS, RW_HEAD, RW_HEAD), f32)
    _, ys = lax.scan(rwkv_step, S0, xs)
    ys = jnp.moveaxis(ys, 0, 2)
    y = ys[0] + ys[1][:, ::-1]
    mu_y = jnp.mean(y, axis=-1, keepdims=True)
    var_y = jnp.mean(jnp.square(y - mu_y), axis=-1, keepdims=True)
    y = (y - mu_y) * lax.rsqrt(var_y + RW_GN_EPS) * heads(gn_w.astype(f32)) + heads(gn_b.astype(f32))
    bonus = jnp.sum(r_h[None] * kd * r_k.astype(f32), axis=-1, keepdims=True) * v_h[None]
    y = y + jnp.sum(bonus, axis=0)
    return y.reshape(B, L, RW_WIDTH) * g

def hybrid_layer(x, w_in, hy_conv_w, hy_conv_b, hy_filt_w1, hy_filt_b1, hy_filt_w2, hy_filt_b2,
                 hy_filt_w3, hy_filt_b3, hy_filt_w4, hy_sin_freq, hy_skip, rw_mu, rw_w0, rw_w2,
                 rw_a0, rw_a2, rw_g2, rw_k_k, rw_k_a, rw_r_k, rw_gn_w, rw_gn_b, w_hy_out, w_rw_out,
                 w_o, ln1_w, ln1_b, ffn_w_gate, ffn_w_up, ffn_w_down, ln2_w, ln2_b):
    dt = x.dtype
    proj = x @ w_in
    u_h, u_r, gates = jnp.split(proj, [HY_COLS, HY_COLS + RW_COLS], axis=-1)
    y_h = hyena_mixer(u_h, hy_conv_w, hy_conv_b, hy_filt_w1, hy_filt_b1, hy_filt_w2, hy_filt_b2,
                      hy_filt_w3, hy_filt_b3, hy_filt_w4, hy_sin_freq, hy_skip).astype(dt) @ w_hy_out
    y_r = rwkv_mixer(u_r, rw_mu, rw_w0, rw_w2, rw_a0, rw_a2, rw_g2, rw_k_k, rw_k_a, rw_r_k,
                     rw_gn_w, rw_gn_b).astype(dt) @ w_rw_out
    g_h, g_r = jnp.split(jax.nn.sigmoid(gates), 2, axis=-1)
    mix = (g_h * y_h + g_r * y_r) @ w_o
    x = layer_norm(DN_ALPHA * x + mix, ln1_w, ln1_b)
    ffn = (jax.nn.silu(x @ ffn_w_gate) * (x @ ffn_w_up)) @ ffn_w_down
    return layer_norm(DN_ALPHA * x + ffn, ln2_w, ln2_b)

def second_inputs(seed: int = 0) -> dict:
    key = jax.random.key(seed)
    keys = iter(jax.random.split(key, 48))

    def nrm(shape, scale):
        return jax.random.normal(next(keys), shape, jnp.float32) * scale

    Ld = DEPTH
    return {
        "x": nrm((BATCH, SEQ, D_MODEL), 1.0),
        "w_in": nrm((Ld, D_MODEL, IN_COLS), D_MODEL ** -0.5),
        "hy_conv_w": nrm((Ld, 3, HY_COLS), 3 ** -0.5),
        "hy_conv_b": nrm((Ld, HY_COLS), 0.02),
        "hy_filt_w1": nrm((Ld, HY_EMB, HY_FILT_HIDDEN), HY_EMB ** -0.5),
        "hy_filt_b1": nrm((Ld, HY_FILT_HIDDEN), 0.1),
        "hy_filt_w2": nrm((Ld, HY_FILT_HIDDEN, HY_FILT_HIDDEN), HY_FILT_HIDDEN ** -0.5),
        "hy_filt_b2": nrm((Ld, HY_FILT_HIDDEN), 0.1),
        "hy_filt_w3": nrm((Ld, HY_FILT_HIDDEN, HY_FILT_HIDDEN), HY_FILT_HIDDEN ** -0.5),
        "hy_filt_b3": nrm((Ld, HY_FILT_HIDDEN), 0.1),
        "hy_filt_w4": nrm((Ld, HY_FILT_HIDDEN, HY_ORDER * 2 * HY_WIDTH), 0.1 * HY_FILT_HIDDEN ** -0.5),
        "hy_sin_freq": 1.0 + nrm((Ld, 3, HY_FILT_HIDDEN), 0.05),
        "hy_skip": nrm((Ld, HY_ORDER, HY_WIDTH), 0.5),
        "rw_mu": 0.5 + nrm((Ld, RW_COLS), 0.1),
        "rw_w0": -0.5 + nrm((Ld, 2, RW_WIDTH), 0.5),
        "rw_w2": nrm((Ld, 2, RW_LORA_W, RW_WIDTH), 0.5 * RW_LORA_W ** -0.5),
        "rw_a0": nrm((Ld, 2, RW_WIDTH), 0.1),
        "rw_a2": nrm((Ld, 2, RW_LORA_A, RW_WIDTH), 0.5 * RW_LORA_A ** -0.5),
        "rw_g2": nrm((Ld, RW_LORA_G, RW_WIDTH), RW_LORA_G ** -0.5),
        "rw_k_k": 0.85 + nrm((Ld, RW_WIDTH), 0.05),
        "rw_k_a": 1.0 + nrm((Ld, RW_WIDTH), 0.05),
        "rw_r_k": nrm((Ld, RW_HEADS, RW_HEAD), 0.1),
        "rw_gn_w": 1.0 + nrm((Ld, RW_WIDTH), 0.05),
        "rw_gn_b": nrm((Ld, RW_WIDTH), 0.02),
        "w_hy_out": nrm((Ld, HY_WIDTH, D_MODEL), HY_WIDTH ** -0.5),
        "w_rw_out": nrm((Ld, RW_WIDTH, D_MODEL), RW_WIDTH ** -0.5),
        "w_o": nrm((Ld, D_MODEL, D_MODEL), DN_BETA * D_MODEL ** -0.5),
        "ln1_w": 1.0 + nrm((Ld, D_MODEL), 0.05),
        "ln1_b": nrm((Ld, D_MODEL), 0.02),
        "ffn_w_gate": nrm((Ld, D_MODEL, FFN_HIDDEN), D_MODEL ** -0.5),
        "ffn_w_up": nrm((Ld, D_MODEL, FFN_HIDDEN), D_MODEL ** -0.5),
        "ffn_w_down": nrm((Ld, FFN_HIDDEN, D_MODEL), DN_BETA * FFN_HIDDEN ** -0.5),
        "ln2_w": 1.0 + nrm((Ld, D_MODEL), 0.05),
        "ln2_b": nrm((Ld, D_MODEL), 0.02),
    }

def second_block(x, w_in, hy_conv_w, hy_conv_b, hy_filt_w1, hy_filt_b1, hy_filt_w2, hy_filt_b2,
              hy_filt_w3, hy_filt_b3, hy_filt_w4, hy_sin_freq, hy_skip, rw_mu, rw_w0, rw_w2,
              rw_a0, rw_a2, rw_g2, rw_k_k, rw_k_a, rw_r_k, rw_gn_w, rw_gn_b, w_hy_out, w_rw_out,
              w_o, ln1_w, ln1_b, ffn_w_gate, ffn_w_up, ffn_w_down, ln2_w, ln2_b):
    for l in range(DEPTH):
        x = hybrid_layer(x, w_in[l], hy_conv_w[l], hy_conv_b[l], hy_filt_w1[l], hy_filt_b1[l],
                         hy_filt_w2[l], hy_filt_b2[l], hy_filt_w3[l], hy_filt_b3[l], hy_filt_w4[l],
                         hy_sin_freq[l], hy_skip[l], rw_mu[l], rw_w0[l], rw_w2[l], rw_a0[l],
                         rw_a2[l], rw_g2[l], rw_k_k[l], rw_k_a[l], rw_r_k[l], rw_gn_w[l], rw_gn_b[l],
                         w_hy_out[l], w_rw_out[l], w_o[l], ln1_w[l], ln1_b[l], ffn_w_gate[l],
                         ffn_w_up[l], ffn_w_down[l], ln2_w[l], ln2_b[l])
    return x


def setup_inputs(seed=0):
    out = dict(first_inputs(seed))
    for name, value in second_inputs(seed + 1).items():
        if name != "x":
            out[name + "_2"] = value
    return out


def reference(
    x, c, ctx, c_ctx, w_ada, b_ada, norm1_g, norm2_g, w_in, sgu_ln_g, sgu_ln_b, sgu_w, sgu_b,
    gla_w2, gla_b2, gla_norm_g, w_br_a, w_br_b, w_o, ffn_w_up, ffn_conv_w, ffn_conv_b,
    ffn_w_down, final_norm_g, w_in_2, hy_conv_w_2, hy_conv_b_2, hy_filt_w1_2, hy_filt_b1_2,
    hy_filt_w2_2, hy_filt_b2_2, hy_filt_w3_2, hy_filt_b3_2, hy_filt_w4_2, hy_sin_freq_2,
    hy_skip_2, rw_mu_2, rw_w0_2, rw_w2_2, rw_a0_2, rw_a2_2, rw_g2_2, rw_k_k_2, rw_k_a_2,
    rw_r_k_2, rw_gn_w_2, rw_gn_b_2, w_hy_out_2, w_rw_out_2, w_o_2, ln1_w_2, ln1_b_2,
    ffn_w_gate_2, ffn_w_up_2, ffn_w_down_2, ln2_w_2, ln2_b_2,
):
    x = first_block(
        x, c, ctx, c_ctx, w_ada, b_ada, norm1_g, norm2_g, w_in, sgu_ln_g, sgu_ln_b, sgu_w,
        sgu_b, gla_w2, gla_b2, gla_norm_g, w_br_a, w_br_b, w_o, ffn_w_up, ffn_conv_w,
        ffn_conv_b, ffn_w_down, final_norm_g,
    )
    return second_block(
        x, w_in_2, hy_conv_w_2, hy_conv_b_2, hy_filt_w1_2, hy_filt_b1_2, hy_filt_w2_2,
        hy_filt_b2_2, hy_filt_w3_2, hy_filt_b3_2, hy_filt_w4_2, hy_sin_freq_2, hy_skip_2,
        rw_mu_2, rw_w0_2, rw_w2_2, rw_a0_2, rw_a2_2, rw_g2_2, rw_k_k_2, rw_k_a_2, rw_r_k_2,
        rw_gn_w_2, rw_gn_b_2, w_hy_out_2, w_rw_out_2, w_o_2, ln1_w_2, ln1_b_2, ffn_w_gate_2,
        ffn_w_up_2, ffn_w_down_2, ln2_w_2, ln2_b_2,
    )


_drawn_inputs = setup_inputs


def setup_inputs(seed=0):
    import zlib

    import numpy as np

    out = dict(_drawn_inputs(seed))
    spreads = {}
    factors = {'ctx': 3.727,
     'c_ctx': 5.653,
     'b_ada': 4.603,
     'sgu_ln_g': 8.0,
     'sgu_ln_b': 64.0,
     'sgu_b': 4.295,
     'gla_b2': 8.0,
     'gla_norm_g': 4.638,
     'ffn_conv_b': 8.0,
     'hy_conv_b_2': 8.0,
     'hy_filt_b1_2': 3.051,
     'hy_filt_b2_2': 3.416,
     'hy_filt_b3_2': 2.886,
     'hy_sin_freq_2': 8.0,
     'rw_w2_2': 5.973,
     'rw_a0_2': 7.964,
     'rw_a2_2': 2.73,
     'rw_k_k_2': 26.127,
     'rw_k_a_2': 4.957,
     'rw_gn_w_2': 8.0,
     'rw_gn_b_2': 28.816,
     'ln1_b_2': 2.793,
     'ln2_b_2': 2.881}
    for name, (base, spread) in spreads.items():
        noise = np.random.default_rng([zlib.crc32(name.encode()), seed]).standard_normal(out[name].shape)
        drawn = base * np.exp(spread * noise) if base else spread * noise
        out[name] = __import__('jax').numpy.asarray(drawn.astype(out[name].dtype))
    for name, factor in factors.items():
        out[name] = (out[name] * factor).astype(out[name].dtype)
    return out
```

```python
import math
from contextlib import ExitStack

import numpy as np

import concourse.bass as bass
from concourse import mybir

F32 = mybir.dt.float32
ACT = mybir.ActivationFunctionType
ALU = mybir.AluOpType

P = 128
D = 1024
L = 512
LC = 256
DT = D // P
TT = L // P
TC = LC // P
HEADS = 4
DK, DV = 128, 256
RANK = 16
SGU_G = 8
FF = 2816
FT = FF // P
GRID = 64
ROWS = L // GRID
HW = 512
HT = HW // P
RH = 64
BLK = 256
RING = 3
BANKS = 8
EPS, LN_EPS, GN_EPS = 1e-6, 1e-5, 64e-5
ALPHA = 2.0 ** 0.25
DECAY = -math.exp(-0.5)
LEVELS = [2, 4, 8, 16, 32]
BIG = 1e30
U = 4096
CUM = P + 4

COLUMNS = [
    ("c", 8), ("c_ctx", 8), ("b_ada", 48), ("norm1_g", 8), ("norm2_g", 8), ("gla_norm_g", 8),
    ("final_norm_g", 8), ("conv_w", 9 * FT), ("conv_b", FT), ("hy_conv_w", 36), ("hy_conv_b", 12),
    ("rw_mu", 15), ("a0", 8), ("k_k", 4), ("k_a", 4), ("r_k", 4), ("gn_w", 4), ("gn_b", 4),
    ("ln1_w", 8), ("ln1_b", 8), ("ln2_w", 8), ("ln2_b", 8), ("filt_b", 3), ("filt_sf", 3),
]
COL = {}
for _name, _n in COLUMNS:
    COL[_name] = sum(n for _, n in COLUMNS[:len(COL)])
NCOL = sum(n for _, n in COLUMNS)

ADA_FIRST, ADA_REST = 8, 16
STREAM = [
    ("ada1", ADA_FIRST), ("k", 2), ("v", 4), ("lr", 1), ("q", 2), ("ada2", ADA_REST), ("r", 4), ("gb", 4),
    ("br_b", 4), ("ga", 4), ("vs", 4), ("u", 4), ("br_a", 4), ("w_o", 4), ("up", 22), ("down", 12),
    ("rw_in", 8), ("hy_in", 6), ("gates", 8), ("rw_out", 2), ("hy_out", 2), ("w_o2", 4), ("up2", 22), ("down2", 12),
]
FIRST_BLOCK = {}
for _name, _n in STREAM:
    FIRST_BLOCK[_name] = sum(n for _, n in STREAM[:len(FIRST_BLOCK)])
NBLOCKS = sum(n for _, n in STREAM)

RW_ORDER = (6, 2, 3, 0, 1, 4, 5, 7)
RW_TILES = [t for _b in RW_ORDER for t in (2 * _b, 2 * _b + 1) if t < 15]

CONSTS = [
    ("ident", P), ("ones", P), ("headones", P), ("gla_cum", 2 * CUM), ("rw_cum", 2 * CUM), ("incl", 2 * P),
    ("pair_mask", 4 * P), ("level_mask", 2 * 6 * P),
]
CONST = {}
for _name, _n in CONSTS:
    CONST[_name] = sum(n for _, n in CONSTS[:len(CONST)])
NCONST = sum(n for _, n in CONSTS)


class Progress:

    def __init__(self, known):
        self.known = known
        self.found = {}
        self.signals = {}

    def stage(self, nc, ctx, name):
        self.signals[name] = Signal(self, name, ctx.enter_context(nc.semaphore(name)))
        return self.signals[name]

    def after(self, *what):
        name, count = self.known[what] if self.known is not None else (next(iter(self.signals)), 1)
        return self.signals[name].sem, count


class Signal:

    def __init__(self, progress, name, sem):
        self.progress, self.name, self.sem, self.count = progress, name, sem, 0

    def did(self, *what):
        self.count += 1
        if what:
            self.note(what)
        return self.sem, 1

    def both(self, *whats):
        self.count += 1
        for what in whats:
            self.note(what)
        return self.sem, 1

    def note(self, what):
        found = self.progress.found
        assert what not in found or what[0] in ("y", "rexp"), what
        found[what] = (self.name, self.count)

    def loaded(self, *what):
        self.count += 16
        self.progress.found[what] = (self.name, self.count)
        return self.sem, 16


def build(nc, io, known):
    progress = Progress(known)
    ctx = ExitStack()
    with ctx:
        _build(nc, io, progress, ctx)
    return progress.found


def _build(nc, io, progress, ctx):
    after = progress.after

    def sb(name, shape):
        return ctx.enter_context(nc.sbuf_tensor(name, shape, F32))

    cols = sb("cols", [P, NCOL])
    consts = sb("consts", [P, NCONST])
    ring = sb("ring", [P, RING, 8 * BLK])
    arena = sb("arena", [P, 10 * U])
    small = sb("small", [P, 1280])
    scratch = sb("scratch", [P, 8 * CUM])
    banks = ctx.enter_context(nc.psum_tensor("banks", [P, BANKS, 512], F32))

    def at(unit, size, offset=0):
        start = unit * U + offset
        return arena[:, start:start + size]

    def tiles(unit, n, width=L, offset=0):
        return at(unit, n * width, offset).rearrange("p (n t) -> p n t", n=n)

    def col(name, i=0, rows=slice(0, P)):
        return cols[rows, COL[name] + i:COL[name] + i + 1]

    def const(name, n, i=0):
        return consts[:, CONST[name] + i * n:CONST[name] + (i + 1) * n]

    ident, ones, headones = const("ident", P), const("ones", P), const("headones", P)
    gla_cum = [const("gla_cum", CUM, d) for d in range(2)]
    rw_cum = [const("rw_cum", CUM, d) for d in range(2)]
    incl = [const("incl", P, d) for d in range(2)]
    pair_mask = [const("pair_mask", 2 * P, d) for d in range(2)]
    level_mask = [[const("level_mask", P, 6 * d + i) for i in range(6)] for d in range(2)]

    csil = small[:, 0:16].rearrange("p (k n) -> p k n", n=2)
    mod = small[:, 16:80]
    modc = small[:, 80:96]
    gs1, gs1c, gs2 = small[:, 96:104], small[:, 104:112], small[:, 112:120]
    eps_cols = small[:, 120:124]
    bn = small[:, 124:124 + 48].rearrange("p (t h s) -> p t h s", t=4, h=2)
    mv = small[:, 172:180].rearrange("p (t s) -> p t s", t=4)
    ln_r = small[:, 180:184]
    stats_x = small[:, 184:184 + 96].rearrange("p (d h c s) -> p d h c s", d=2, h=4, c=4)
    stats_c = small[:, 280:280 + 48].rearrange("p (d h c s) -> p d h c s", d=2, h=4, c=2)
    mix_half, mix_one = small[:, 328:343], small[:, 343:358]
    half_ka, rest_ka, half_a0 = small[:, 358:362], small[:, 362:366], small[:, 366:374]
    filt_sb = small[:, 374:377]
    ones_row = small[0:1, 384:512]
    state = small[:, 512:640].rearrange("p (b v) -> p b v", b=2)
    state_t = small[:, 640:704]
    state_m = small[:, 1048:1176]
    ub = small[:, 768:896].rearrange("p (h v) -> p h v", h=2)
    sab = small[:, 896:1024].rearrange("p (h v) -> p h v", h=2)
    job_stats = small[:, 1024:1048].rearrange("p (b c s) -> p b c s", b=2, c=4)

    psum_full = progress.stage(nc, ctx, "psum_full")
    slot_loaded = [progress.stage(nc, ctx, f"slot_loaded{i}") for i in range(RING)]
    names = ["start", "ada", "gla", "mix", "ffn", "rwkv", "hyena", "ffn2"]
    dve_in = {n: progress.stage(nc, ctx, f"dve_{n}") for n in names}
    act_in = {n: progress.stage(nc, ctx, f"act_{n}") for n in names}
    pool_in = {n: progress.stage(nc, ctx, f"pool_{n}") for n in names}
    loads = {n: progress.stage(nc, ctx, f"load_{n}") for n in
             ("cols", "consts", "x", "ctx", "gla_w2", "ln_g", "ln_b", "w_s", "b_s", "rw_small", "w0",
              "filters", "dft", "dftT", "window", "skip")}
    out_stored = progress.stage(nc, ctx, "out_stored")

    xT = tiles(0, DT)
    hT = tiles(1, DT)
    ctxT = tiles(2, DT, LC, 0)
    hcT = tiles(2, DT, LC, 2048)
    sq = tiles(3, DT)
    rstd = tiles(4, 2)
    kT, kcT = tiles(4, HEADS), tiles(4, HEADS, LC, 2048)
    lrT, lrcT = at(4, L, 3072)[0:33], at(4, LC, 3584)[0:33]
    v_tok = tiles(5, TT, D)
    vc_tok = tiles(6, TC, D)
    qT = tiles(6, HEADS, L, 2048)
    la = [tiles(7, TT, L, 2048 * d) for d in range(2)]
    lac = [tiles(3, TC, L, 1024 * d) for d in range(2)]
    gla_w2 = at(8, 1024)[0:33].rearrange("p (d n) -> p d n", d=2)
    soft = [at(9, L, 512 * i) for i in range(8)]
    q_dec = [tiles(8, HEADS, L, 2048 * d) for d in range(2)]
    k_inv = [tiles(9, HEADS, L, 2048 * d) for d in range(2)]
    kc_inv = [tiles(3, HEADS, LC, 2048 + 1024 * d) for d in range(2)]
    k_tok = [tiles(2, TT, L, 2048 * d) for d in range(2)]
    kc_tok = [tiles(3, TC, L, 1024 * d) for d in range(2)]
    s_gla = [at(6, DV, 2048 + 256 * i) for i in range(8)]
    sm = [[[at(7 if d == 0 else 4, DV, 256 * (4 * h + c)) for c in range(TT)] for h in range(HEADS)]
          for d in range(2)]
    sc = tiles(3, TT, L, 2048)
    oT = tiles(2, DT)
    osq = tiles(3, 4)
    silu_r = tiles(5, DT)
    sga, sgb = tiles(6, DT), tiles(7, DT)
    vs_tok = tiles(8, TT, D)
    guT = tiles(4, DT)
    ln_g, ln_b = at(9, D), at(9, D, 1024)
    w_sT = tiles(9, SGU_G, P, 2048)
    b_s = at(9, D, 3072)[0:1]
    gT = tiles(2, FT)
    pads = at(8, 4 * (ROWS + 2) * (GRID + 2)).rearrange("p (b y x) -> p b y x", b=4, y=ROWS + 2)
    acc = tiles(9, 4)
    sq5 = tiles(5, DT)
    exps = scratch[:, :].rearrange("p (k c j) -> p k c j", k=4, c=2)
    work = [scratch[:, L * i:L * (i + 1)] for i in range(2)]
    rstd2 = tiles(9, 2, L, 2048)

    x2T = tiles(1, DT)
    raw = at(0, 3 * (L + 2), 2048).rearrange("p (b t) -> p b t", b=3)
    pair_sum = tiles(5, 2)
    rT, rkT = tiles(8, HT), tiles(8, HT, L, 2048)
    rvT = tiles(9, HT)
    wdT, adT, gdT = (at(9, L, 2048 + L * i) for i in range(3))
    mixed = [rT[:, i, :] for i in range(4)] + [rkT[:, i, :] for i in range(4)] + [rvT[:, i, :] for i in range(4)] + [wdT, adT, gdT]
    lw = [tiles(6, TT, L, 2048), tiles(0, TT)]
    rv_tok = tiles(7, TT)
    nkkT = tiles(7, HT, L, 2048)
    kk_sq, kk_n = (tiles(5, 2, L, 1024 * i) for i in (1, 2))
    w0_row = at(5, 2 * L, 3072)[0:1]
    yT = tiles(2, HT)
    rw_a2, rw_g2 = (at(2, L, 2048 + L * i) for i in range(2))
    rw_w2 = tiles(3, 2)
    job_t, kd_sum = at(2, L, 3584), at(9, L, 3584)
    sets = []
    for s in range(2):
        base = 7168 * s
        sets.append(dict(
            nqb=at(3, 2048, base).rearrange("p (s a t) -> p s a t", s=8, a=2),
            mqk=at(3, 2048, base + 2048).rearrange("p (s a t) -> p s a t", s=8, a=2),
            g=at(3, 1024, base + 4096).rearrange("p (s t) -> p s t", s=8),
            ar=at(3, 1024, base + 5120).rearrange("p (c a t) -> p c a t", c=4, a=2),
            b_tok=at(3, 512, base + 6144).rearrange("p (c f) -> p c f", c=4),
            k_tok=at(3, 512, base + 6656).rearrange("p (c f) -> p c f", c=4)))
    X, Y = (at(0, 1024, 2048 + 1024 * i).rearrange("p (s t) -> p s t", s=8) for i in range(2))
    job_slot = ring[:, (FIRST_BLOCK["hy_in"] + 1) % RING, :].rearrange("p (n t) -> p n t", n=4)
    aT, kdT, bkT = job_slot[:, 0, :], job_slot[:, 1, :], job_slot[:, 2:4, :]
    y_sq, gn_s = tiles(3, HT), tiles(5, 2)
    zT = tiles(4, HT)
    hyT = tiles(3, 12)
    xv_tok, x1_tok = tiles(5, TT), tiles(5, TT, L, 2048)
    featsT = at(6, L)[0:33]
    fw1 = at(6, 64, 512)[0:33]
    fw23 = [at(6, 64, 576 + 64 * i)[0:64] for i in range(2)]
    fw4 = at(6, 2048, 704)[0:64].rearrange("p (o d n) -> p o d n", o=2, d=2)
    fsd = at(7, 2048)[0:64].rearrange("p (o d n) -> p o d n", o=2, d=2)
    filt_h, filt_k, filt_a = (at(7, L, 2048 + L * i)[0:64] for i in range(3))
    skip_row = at(6, 1024, 2816)[0:1]
    window = tiles(4, TT, L, 2048)
    ht = [[tiles(8 + o, TT, L, 2048 * s) for s in range(2)] for o in range(2)]
    dft = [tiles(0, TT), tiles(0, TT, L, 2048)]
    dftT = [tiles(6, TT), tiles(6, TT, L, 2048)]
    Hcs = [[tiles((7, 3)[o], TT, L, 2048 * s) for s in range(2)] for o in range(2)]
    Ycs = [tiles(8, TT), tiles(8, TT, L, 2048)]
    prod = tiles(9, 8)
    gate_h, gate_r = tiles(0, DT), tiles(7, DT)
    lnc, lnsq = tiles(3, DT), tiles(4, DT)
    gT2 = tiles(3, FT)
    silu_g = tiles(6, 4)
    norm_s = tiles(9, 2)

    block = ctx.enter_context(nc.Block())
    bank_of, block_done = {}, {}
    bank_user = {}
    order = [(0, 1, 2, 3), (3, 2, 1, 0)]
    JOBS = [(hp, d) for hp in range(HT) for d in range(2)]
    LO, HI = slice(0, 64), slice(64, 128)

    def bank(*name):
        return banks[:, bank_of[name], :]

    @block.tensor
    def _(pe):
        taken = [0]

        def take(*name):
            b = taken[0] % BANKS
            taken[0] += 1
            if b in bank_user:
                pe.wait_ge(*after(*("free",) + bank_user[b]))
            bank_user[b] = name
            bank_of[name] = b
            return banks[:, b, :]

        def weights(name, i):
            n = FIRST_BLOCK[name] + i
            pe.wait_ge(*after("block", n))
            return ring[:, n % RING, :].rearrange("p (k c) -> p k c", c=BLK)

        def weights_done(name, i, *group):
            block_done[FIRST_BLOCK[name] + i] = group

        def linear(name, b, rhs, rhs_ready, group, tiles_of=(0, 1), kt=DT):
            w = weights(name, b)
            for j in tiles_of:
                t = 2 * b + j
                ps = take(group, t)
                for k in range(kt):
                    pe.wait_ge(*after(rhs_ready, k))
                    mm = pe.matmul(ps, w[:, k, j * P:(j + 1) * P], rhs[:, k, :], start=k == 0, stop=k == kt - 1)
                mm.then_inc(*psum_full.did("psum", group, t))
            weights_done(name, b, group, t)

        def feature_sum(group, src, ready, weight, n=L, kt=DT):
            ps = take(group)
            for k in range(kt):
                pe.wait_ge(*after(ready, k))
                mm = pe.matmul(ps[:, 0:n], weight, src[:, k, :], start=k == 0, stop=k == kt - 1)
            mm.then_inc(*psum_full.did("psum", group))

        pe.wait_ge(*after("consts"))
        feature_sum("ss_c", sq5[:, :, 0:LC], "sqc", ones, LC)
        feature_sum("ss_x", sq, "sq", ones)

        def modulation(name, nb):
            ps = take(name)
            pe.wait_ge(*after("csil"))
            for b in range(nb):
                w = weights(name, b)
                for j in range(2):
                    at_col = 2 * (2 * b + j)
                    for k in range(DT):
                        mm = pe.matmul(ps[:, at_col:at_col + 2], w[:, k, j * P:(j + 1) * P], csil[:, k, :],
                                       start=k == 0, stop=k == DT - 1)
                mm.then_inc(*psum_full.did("psum", name, b))
                weights_done(name, b, name, b)

        modulation("ada1", ADA_FIRST)

        for b in range(2):
            w = weights("k", b)
            for j in range(2):
                t = 2 * b + j
                for group, src, ready, n in (("kc", hcT, "hcT", LC), ("k", hT, "hT", L)):
                    ps = take(group, t)
                    for k in range(DT):
                        pe.wait_ge(*after(ready, k))
                        mm = pe.matmul(ps[:, 0:n], w[:, k, j * P:(j + 1) * P], src[:, k, :],
                                       start=k == 0, stop=k == DT - 1)
                    mm.then_inc(*psum_full.did("psum", group, t))
            weights_done("k", b, "k", t)

        def token_major(group, w, b, src, half):
            ps = take(group, b, half)
            for i in range(2):
                tt = 2 * half + i
                for k in range(DT):
                    mm = pe.matmul(ps[:, i * BLK:(i + 1) * BLK], src[:, k, tt * P:(tt + 1) * P], w[:, k, :],
                                   start=k == 0, stop=k == DT - 1)
            mm.then_inc(*psum_full.did("psum", group, b, half))

        for b in range(4):
            w = weights("v", b)
            token_major("vc", w, b, hcT, 0)
            token_major("v", w, b, hT, 0)
            token_major("v", w, b, hT, 1)
            weights_done("v", b, "v", b, 1)
        w = weights("lr", 0)
        for group, src, n in (("lrc", hcT, LC), ("lr", hT, L)):
            ps = take(group)
            for k in range(DT):
                mm = pe.matmul(ps[0:32, 0:n], w[:, k, 0:32], src[:, k, :], start=k == 0, stop=k == DT - 1)
            mm.then_inc(*psum_full.did("psum", group))
        weights_done("lr", 0, "lr")
        for b in range(2):
            linear("q", b, hT, "hT", "q")

        pe.wait_ge(*after("gla_w2"))
        pe.wait_ge(*after("lrcT"))
        pe.wait_ge(*after("lr_ones"))
        for d in range(2):
            for tt in range(TC):
                ps = take("zc", d, tt)
                pe.matmul(ps, lrcT[:, tt * P:(tt + 1) * P], gla_w2[:, d, :], start=True, stop=True).then_inc(
                    *psum_full.did("psum", "zc", d, tt))
        pe.wait_ge(*after("lrT"))
        for d in range(2):
            for tt in range(TT):
                ps = take("z", d, tt)
                pe.matmul(ps, lrT[:, tt * P:(tt + 1) * P], gla_w2[:, d, :], start=True, stop=True).then_inc(
                    *psum_full.did("psum", "z", d, tt))
        modulation("ada2", ADA_REST)

        def cumulate(group, log_decay, ready, d, h, cp):
            ps = take(group, d, h, cp)
            for i in range(2):
                c = 2 * cp + i
                pe.wait_ge(*after(ready, d, c))
                mm = pe.matmul(ps[:, i * CUM:(i + 1) * CUM], log_decay[d][:, c, h * P:(h + 1) * P], gla_cum[d],
                               start=True, stop=True)
            mm.then_inc(*psum_full.did("psum", group, d, h, cp))

        for d in range(2):
            for h in range(HEADS):
                cumulate("cumc", lac, "lac", d, h, 0)
        for d in range(2):
            for h in range(HEADS):
                for cp in range(2):
                    cumulate("cum", la, "la", d, h, cp)

        for group, src, ready, chunks in (("ktc", kc_inv, "kc_inv", TC), ("kt", k_inv, "k_inv", TT)):
            for d in range(2):
                for c in range(chunks):
                    ps = take(group, d, c)
                    for h in range(HEADS):
                        pe.wait_ge(*after(ready, d, h, c // 2))
                        mm = pe.transpose(ps[:, h * P:(h + 1) * P], src[d][:, h, c * P:(c + 1) * P], ident)
                    mm.then_inc(*psum_full.did("psum", group, d, c))

        for step in range(5):
            for d in range(2):
                if step < 2:
                    c, keys, vals, ready = (step, 1 - step)[d], kc_tok[d], vc_tok, ("kc_tok", d, (step, 1 - step)[d])
                else:
                    c = order[d][step - 2]
                    keys, vals, ready = k_tok[d], v_tok, ("k_tok", d, c)
                pe.wait_ge(*after(*ready))
                for hp in range(2):
                    ps = take("su", step, d, hp)
                    for i in range(2):
                        h = 2 * hp + i
                        for b in range(4):
                            pe.wait_ge(*after(*(("vc_tok", b) if step < 2 else ("v_tok", b))))
                        mm = pe.matmul(ps[:, i * DV:(i + 1) * DV], keys[:, c, h * P:(h + 1) * P],
                                       vals[:, c, h * DV:(h + 1) * DV], start=True, stop=True)
                    mm.then_inc(*psum_full.did("psum", "su", step, d, hp))

        for c in range(TT):
            for d in range(2):
                ps = take("sc", d, c)
                for h in range(HEADS):
                    pe.wait_ge(*after("q_dec", d, h, c // 2))
                    mm = pe.matmul(ps[:, h * P:(h + 1) * P], k_inv[d][:, h, c * P:(c + 1) * P],
                                   q_dec[d][:, h, c * P:(c + 1) * P], start=True, stop=True)
                mm.then_inc(*psum_full.did("psum", "sc", d, c))

        def out_sum(h):
            ps = take("oss", h)
            for vt in range(2):
                pe.wait_ge(*after("osq", 2 * h + vt))
                mm = pe.matmul(ps, ones, osq[:, (2 * h + vt) % 4, :], start=vt == 0, stop=vt == 1)
            mm.then_inc(*psum_full.did("psum", "oss", h))

        for h in range(HEADS):
            for vt in range(2):
                ps = take("o", 2 * h + vt)
                vcols = slice(h * DV + vt * P, h * DV + (vt + 1) * P)
                for c in range(TT):
                    pe.wait_ge(*after("sc", c))
                    pe.wait_ge(*after("sm", 0, h, c))
                    pe.wait_ge(*after("sm", 1, h, c))
                    out = ps[:, c * P:(c + 1) * P]
                    pe.matmul(out, v_tok[:, c, vcols], sc[:, c, h * P:(h + 1) * P], start=True, stop=False)
                    for d in range(2):
                        mm = pe.matmul(out, sm[d][h][c][:, vt * P:(vt + 1) * P], q_dec[d][:, h, c * P:(c + 1) * P],
                                       start=False, stop=d == 1)
                mm.then_inc(*psum_full.did("psum", "o", 2 * h + vt))
            if h >= 1:
                out_sum(h - 1)
        for b in range(4):
            linear("r", b, hT, "hT", "r")
            if b == 0:
                out_sum(HEADS - 1)
        for b in range(4):
            linear("gb", b, hT, "hT", "gb")
        for b in range(4):
            linear("br_b", b, oT, "ob", "br_b")
        for b in range(4):
            linear("ga", b, hT, "hT", "ga")

        for b in range(4):
            w = weights("vs", b)
            token_major("vs", w, b, hT, 0)
            token_major("vs", w, b, hT, 1)
            weights_done("vs", b, "vs", b, 1)
        for b in range(4):
            linear("u", b, hT, "hT", "u")
        pe.wait_ge(*after("w_s"))
        pe.wait_ge(*after("b_s"))
        pe.wait_ge(*after("ones_row"))
        for g in range(SGU_G):
            ps = take("s", g)
            pe.matmul(ps, ones_row, b_s[:, g * P:(g + 1) * P].unsqueeze(1).to_broadcast([1, TT, P]), start=True,
                      stop=False)
            for n in range(TT):
                pe.wait_ge(*after("vn", n))
                mm = pe.matmul(ps[:, n * P:(n + 1) * P], vs_tok[:, n, g * P:(g + 1) * P], w_sT[:, g, :],
                               start=False, stop=n == TT - 1)
            mm.then_inc(*psum_full.did("psum", "s", g))
        for b in range(4):
            linear("br_a", b, guT, "aT", "br_a")
        for b in range(4):
            linear("w_o", b, sga, "merged", "w_o")

        feature_sum("ss2", sq5, "sq2", ones)
        for b in range(FT // 2):
            for group, base in (("fa", 0), ("fv", 1)):
                w = weights("up", 2 * b + base)
                for j in range(2):
                    ps = take(group, 2 * b + j)
                    for k in range(DT):
                        pe.wait_ge(*after("h2T", k))
                        mm = pe.matmul(ps, w[:, k, j * P:(j + 1) * P], hT[:, k, :], start=k == 0, stop=k == DT - 1)
                    mm.then_inc(*psum_full.did("psum", group, 2 * b + j))
                weights_done("up", 2 * b + base, group, 2 * b + 1)

        def down(name, group, src, ready):
            for b in range(4):
                ps = [take(group, 2 * b + j) for j in range(2)]
                for part in range(3):
                    w = weights(name, 3 * b + part)
                    kt = min(8, FT - 8 * part)
                    for j in range(2):
                        for k in range(kt):
                            pe.wait_ge(*after(ready, 8 * part + k))
                            mm = pe.matmul(ps[j], w[:, k, j * P:(j + 1) * P], src[:, 8 * part + k, :],
                                           start=part == 0 and k == 0, stop=part == 2 and k == kt - 1)
                        if part == 2:
                            mm.then_inc(*psum_full.did("psum", group, 2 * b + j))
                    if part < 2:
                        mm.then_inc(*psum_full.did("psum", group, "part", b, part))
                        weights_done(name, 3 * b + part, group, "part", b, part)
                weights_done(name, 3 * b + 2, group, 2 * b + 1)

        down("down", "down", gT, "gT")
        feature_sum("ss3", sq5, "sq3", ones)

        def key_norms(hps):
            for hp in hps:
                ps = take("kk", hp)
                pe.wait_ge(*after("kk_sq", hp))
                pe.matmul(ps, headones, kk_sq[:, hp % 2, :], start=True, stop=True).then_inc(
                    *psum_full.did("psum", "kk", hp))

        def rwkv_projection(i):
            b = RW_ORDER[i]
            w = weights("rw_in", i)
            for t in (2 * b, 2 * b + 1):
                if t < 15:
                    ps = take("rw", t)
                    for k in range(DT):
                        pe.wait_ge(*after("x2T", k))
                        mm = pe.matmul(ps, w[:, k, (t % 2) * P:(t % 2 + 1) * P], x2T[:, k, :],
                                       start=k == 0, stop=k == DT - 1)
                    mm.then_inc(*psum_full.did("psum", "rw", t))
                    last = t
                if t in (0, 1):
                    key_norms((2 * t, 2 * t + 1))
            weights_done("rw_in", i, "rw", last)
            if i in (2, 3):
                d = i - 2
                pe.wait_ge(*after("wd_tanh"))
                pe.wait_ge(*after("rw_w2"))
                pe.wait_ge(*after("w0"))
                for tt in range(TT):
                    ps = take("w", d, tt)
                    pe.matmul(ps, wdT[:, tt * P:(tt + 1) * P], rw_w2[:, d, :], start=True, stop=False)
                    pe.matmul(ps, ones_row, w0_row[:, d * L:(d + 1) * L], start=False, stop=True).then_inc(
                        *psum_full.did("psum", "w", d, tt))

        for i in range(7):
            rwkv_projection(i)

        def inputs(j):
            hp, d = JOBS[j]
            ps = take("a", j)
            rows = (LO, HI)[d]
            pe.wait_ge(*after("mixed", 13))
            pe.matmul(ps, rw_a2[rows, hp * P:(hp + 1) * P], adT[rows, :], start=True, stop=True).then_inc(
                *psum_full.did("psum", "a", j))
            for cp in range(2):
                ps = take("rcum", j, cp)
                for i in range(2):
                    c = 2 * cp + i
                    pe.wait_ge(*after("lw", d, c))
                    mm = pe.matmul(ps[:, i * CUM:(i + 1) * CUM], lw[d][:, c, hp * P:(hp + 1) * P], rw_cum[d],
                                   start=True, stop=True)
                mm.then_inc(*psum_full.did("psum", "rcum", j, cp))

        def tokens(j):
            for what, i in (("job_b", 0), ("job_k", 1)):
                ps = take("tok", j, i)
                pe.wait_ge(*after(what, j))
                for c in range(TT):
                    mm = pe.transpose(ps[:, c * P:(c + 1) * P], bkT[:, i, c * P:(c + 1) * P], ident)
                mm.then_inc(*psum_full.did("psum", "tok", j, i))

        def gram(j, i, cp):
            s = sets[j % 2]
            pe.wait_ge(*after("job_a", j))
            pe.wait_ge(*after("job_r", j))
            for h in range(2):
                ps = take("gram", j, i, cp, h)
                rows = (LO, HI)[h]
                for n in range(2):
                    c = 2 * cp + n
                    mm = pe.matmul(ps[:, n * 2 * P:(n + 1) * 2 * P], bkT[rows, i, c * P:(c + 1) * P],
                                   s["ar"][rows, c, :, :], start=True, stop=True)
                mm.then_inc(*psum_full.did("psum", "gram", j, i, cp, h))

        def bonus(j):
            hp, d = JOBS[j]
            if d == 1:
                ps = take("bonus", hp)
                pe.wait_ge(*after("bonus_in", hp))
                pe.matmul(ps, headones, kd_sum, start=True, stop=True).then_inc(*psum_full.did("psum", "bonus", hp))

        def inverse_start(j, half):
            ps = take("x0", j, half)
            pe.wait_ge(*after("g0", j))
            for i in range(4):
                mm = pe.transpose(ps[:, i * P:(i + 1) * P], sets[j % 2]["g"][:, 4 * half + i, :], ident)
            mm.then_inc(*psum_full.did("psum", "x0", j, half))

        def invert_y(j, lv, half):
            s = sets[j % 2]
            ps = take("iy", j, lv, half)
            pe.wait_ge(*after("x", j, lv, half))
            pe.wait_ge(*after("lt", j))
            for i in range(4):
                n = 4 * half + i
                mm = pe.matmul(ps[:, i * P:(i + 1) * P], s["nqb"][:, n, 0, :], X[:, n, :], start=True, stop=True)
            mm.then_inc(*psum_full.did("psum", "iy", j, lv, half))

        def invert_xg(j, lv, half):
            s = sets[j % 2]
            pe.wait_ge(*after("yi", j, lv, half))
            pe.wait_ge(*after(*(("g", j, lv, half) if lv else ("g0", j))))
            for what in ("ix", "ig"):
                ps = take(what, j, lv, half)
                for i in range(4):
                    n = 4 * half + i
                    out = ps[:, i * P:(i + 1) * P]
                    if what == "ix":
                        mm = pe.matmul(out, s["g"][:, n, :], Y[:, n, :], start=True, stop=True)
                    else:
                        mm = pe.matmul(out, Y[:, n, :], s["g"][:, n, :], start=True, stop=True)
                mm.then_inc(*psum_full.did("psum", what, j, lv, half))

        def invert_last(j, stage):
            s = sets[j % 2]
            d = JOBS[j][1]
            first, second = (LO, HI) if d == 0 else (HI, LO)
            ps = take("il", j, stage)
            if stage == 0:
                pe.wait_ge(*after("x", j, 5, 0))
                pe.wait_ge(*after("x", j, 5, 1))
                for n in range(8):
                    mm = pe.matmul(ps[second, n * 64:(n + 1) * 64], s["nqb"][first, n, 0, second],
                                   X[first, n, first], start=True, stop=True)
            else:
                pe.wait_ge(*after("y_last", j))
                pe.wait_ge(*after("g", j, 5, 0))
                pe.wait_ge(*after("g", j, 5, 1))
                for n in range(8):
                    mm = pe.matmul(ps[first, n * 64:(n + 1) * 64], Y[second, n, first], s["g"][second, n, second],
                                   start=True, stop=True)
            mm.then_inc(*psum_full.did("psum", "il", j, stage))

        def chain_u(j, step):
            hp, d = JOBS[j]
            s = sets[j % 2]
            c = order[d][step]
            pe.wait_ge(*after("rv_tok", c))
            ps = take("cu", j, step)
            for h in range(2):
                out = ps[:, h * 64:(h + 1) * 64]
                mm = pe.matmul(out, s["mqk"][:, 2 * c + h, 0, :], rv_tok[:, c, hp * P + h * 64:hp * P + (h + 1) * 64],
                               start=step == 0 or h == 0, stop=step == 0)
            if step:
                pe.wait_ge(*after("state_m", j, step))
                mm = pe.matmul(ps[:, 0:P], s["ar"][:, c, 0, :], state_m, start=False, stop=True)
            mm.then_inc(*psum_full.did("psum", "cu", j, step))

        def chain_sa(j, step):
            s = sets[j % 2]
            c = order[JOBS[j][1]][step]
            pe.wait_ge(*after("u", j, step))
            pe.wait_ge(*after("g_done", j))
            ps = take("cs", j, step)
            for h in range(2):
                mm = pe.matmul(ps[:, h * 64:(h + 1) * 64], s["g"][:, 2 * c + h, :], ub[:, h, :], start=True, stop=True)
            mm.then_inc(*psum_full.did("psum", "cs", j, step))

        def chain_out(j, step):
            hp, d = JOBS[j]
            s = sets[j % 2]
            c = order[d][step]
            pe.wait_ge(*after("sa", j, step))
            if step < 3:
                ps = take("ch", j, step)
                for h in range(2):
                    rows = (LO, HI)[h]
                    pe.matmul(ps[rows, 0:64], s["b_tok"][:, c, rows], sab[:, h, :], start=True, stop=False)
                    mm = pe.matmul(ps[rows, 0:64], s["k_tok"][:, c, rows],
                                   rv_tok[:, c, hp * P + h * 64:hp * P + (h + 1) * 64], start=False, stop=True)
                mm.then_inc(*psum_full.did("psum", "ch", j, step))
            ps = take("cy", j, step)
            for h in range(2):
                rows = (LO, HI)[h]
                out = ps[rows, 0:P]
                pe.matmul(out, sab[:, h, :], s["nqb"][:, 2 * c + h, 1, :], start=True, stop=False)
                mm = pe.matmul(out, rv_tok[:, c, hp * P + h * 64:hp * P + (h + 1) * 64],
                               s["mqk"][:, 2 * c + h, 1, :], start=False, stop=step == 0)
            if step:
                mm = pe.matmul(ps[:, 0:P], state_m, s["ar"][:, c, 1, :], start=False, stop=True)
            mm.then_inc(*psum_full.did("psum", "cy", j, step))

        inputs(0)
        rwkv_projection(7)
        for c in range(TT):
            ps = take("vt", c)
            for hp in range(HT):
                pe.wait_ge(*after("mixed", 8 + hp))
                mm = pe.transpose(ps[:, hp * P:(hp + 1) * P], rvT[:, hp, c * P:(c + 1) * P], ident)
            mm.then_inc(*psum_full.did("psum", "vt", c))
        tokens(0)
        gram(0, 0, 0)
        gram(0, 0, 1)
        for j in range(len(JOBS) + 1):
            new, old, ahead = j < len(JOBS), j > 0, j + 1 < len(JOBS)
            if old:
                chain_u(j - 1, 0)
            if new:
                gram(j, 1, 0)
            if old:
                chain_sa(j - 1, 0)
            if new:
                gram(j, 1, 1)
                inverse_start(j, 0)
                bonus(j)
                inverse_start(j, 1)
            if old:
                chain_out(j - 1, 0)
            if ahead:
                inputs(j + 1)
            for lv in range(5):
                chained = old and lv < 3
                if new:
                    for half in range(2):
                        invert_y(j, lv, half)
                if chained:
                    chain_u(j - 1, lv + 1)
                if new:
                    invert_xg(j, lv, 0)
                if chained:
                    chain_sa(j - 1, lv + 1)
                if new:
                    invert_xg(j, lv, 1)
                if chained:
                    chain_out(j - 1, lv + 1)
            if new:
                invert_last(j, 0)
            if ahead:
                tokens(j + 1)
                gram(j + 1, 0, 0)
            if new:
                invert_last(j, 1)
            if ahead:
                gram(j + 1, 0, 1)

        for hp in range(HT):
            ps = take("ym", hp)
            pe.wait_ge(*after("y", 2 * hp + 1))
            pe.matmul(ps, headones, yT[:, hp, :], start=True, stop=True).then_inc(*psum_full.did("psum", "ym", hp))
        for hp in range(HT):
            ps = take("yv", hp)
            pe.wait_ge(*after("y_sq", hp))
            pe.matmul(ps, headones, y_sq[:, hp, :], start=True, stop=True).then_inc(*psum_full.did("psum", "yv", hp))
        pe.wait_ge(*after("gd_sig"))
        for hp in range(HT):
            ps = take("g", hp)
            pe.matmul(ps, rw_g2[:, hp * P:(hp + 1) * P], gdT, start=True, stop=True).then_inc(
                *psum_full.did("psum", "g", hp))

        for b in range(6):
            linear("hy_in", b, x2T, "x2T", "hy")
            if b >= 2 and b < 5:
                n = b - 2
                fw, src = ((fw1, featsT), (fw23[0], filt_h), (fw23[1], filt_h))[n]
                ps = take("filt", n)
                pe.wait_ge(*after("filters"))
                if n:
                    pe.wait_ge(*after("filt_h", n - 1))
                pe.matmul(ps[0:64, :], fw, src, start=True, stop=True).then_inc(*psum_full.did("psum", "filt", n))
        for what, dst in (("hvt", 0), ("hxt", 4)):
            for c in range(TT):
                ps = take(what, c)
                for i in range(HT):
                    pe.wait_ge(*after("hyT", dst + i))
                    mm = pe.transpose(ps[:, i * P:(i + 1) * P], hyT[:, dst + i, c * P:(c + 1) * P], ident)
                mm.then_inc(*psum_full.did("psum", what, c))
        for o in range(2):
            for sd in range(2):
                for tt in range(TT):
                    pe.wait_ge(*after("fsd", o, sd))
                    pe.wait_ge(*after("filt_h", 2))
                    ps = take("hf", o, sd, tt)
                    pe.matmul(ps, filt_h[:, tt * P:(tt + 1) * P], fsd[:, o, sd, :], start=True, stop=True).then_inc(
                        *psum_full.did("psum", "hf", o, sd, tt))
        pe.wait_ge(*after("dft"))

        def transform(group, tag, src, ready, cs):
            for ft in range(TT):
                ps = take(group, *tag, ft)
                for k in range(TT):
                    pe.wait_ge(*after(*ready(k)))
                    mm = pe.matmul(ps, dft[cs][:, k, ft * P:(ft + 1) * P], src[:, k, :], start=k == 0, stop=k == TT - 1)
                mm.then_inc(*psum_full.did("psum", group, *tag, ft))

        for o in range(2):
            for sd in range(2):
                transform("H", (o, sd), ht[o][sd], lambda k: ("ht", o, sd, k), sd)
        for o in range(2):
            z, ready = xv_tok, (lambda k: ("xv_tok", k)) if o == 0 else (lambda k: ("z2", k))
            for ft in range(TT):
                for cs in range(2):
                    ps = take("Z", o, cs, ft)
                    for k in range(TT):
                        pe.wait_ge(*after(*ready(k)))
                        mm = pe.matmul(ps, dft[cs][:, k, ft * P:(ft + 1) * P], z[:, k, :], start=k == 0, stop=k == TT - 1)
                    mm.then_inc(*psum_full.did("psum", "Z", o, cs, ft))
            pe.wait_ge(*after("dftT"))
            for tt in range(TT):
                ps = take("conv", o, tt)
                for cs in range(2):
                    for k in range(TT):
                        pe.wait_ge(*after("Y", o, cs, k))
                        if o == 0:
                            a, b = dftT[cs][:, k, tt * P:(tt + 1) * P], Ycs[cs][:, k, :]
                        else:
                            a, b = Ycs[cs][:, k, tt * P:(tt + 1) * P], dftT[cs][:, k, :]
                        mm = pe.matmul(ps, a, b, start=cs == 0 and k == 0, stop=cs == 1 and k == TT - 1)
                mm.then_inc(*psum_full.did("psum", "conv", o, tt))

        for b in range(8):
            linear("gates", b, x2T, "x2T", "gate")

        def half_width(name, group, src, ready):
            for b in range(2):
                n = FIRST_BLOCK[name] + b
                pe.wait_ge(*after("block", n))
                w = ring[:, n % RING, :].rearrange("p (k c) -> p k c", c=2 * BLK)
                for j in range(4):
                    ps = take(group, 4 * b + j)
                    for k in range(HT):
                        pe.wait_ge(*after(ready, k))
                        mm = pe.matmul(ps, w[:, k, j * P:(j + 1) * P], src[:, k, :], start=k == 0, stop=k == HT - 1)
                    mm.then_inc(*psum_full.did("psum", group, 4 * b + j))
                weights_done(name, b, group, 4 * b + j)

        half_width("rw_out", "rwo", yT, "yT")
        half_width("hy_out", "hyo", zT, "zT")
        for b in range(4):
            linear("w_o2", b, gate_h, "merged2", "w_o2")
        feature_sum("lm0", x2T, "res0", ones)
        feature_sum("lv0", lnsq, "lnsq0", ones)
        for b in range(FT // 2):
            for group, base in (("fg", 0), ("fu", 1)):
                w = weights("up2", 2 * b + base)
                for j in range(2):
                    ps = take(group, 2 * b + j)
                    for k in range(DT):
                        pe.wait_ge(*after("x3T", k))
                        mm = pe.matmul(ps, w[:, k, j * P:(j + 1) * P], x2T[:, k, :], start=k == 0, stop=k == DT - 1)
                    mm.then_inc(*psum_full.did("psum", group, 2 * b + j))
                weights_done("up2", 2 * b + base, group, 2 * b + 1)
        down("down2", "down2", gT2, "gT2")
        feature_sum("lm1", x2T, "res1", ones)
        feature_sum("lv1", lnsq, "lnsq1", ones)

    @block.vector
    def _(dve):
        V = nc.vector

        def mul(out, a, b):
            return V.tensor_tensor(out, a, b, ALU.mult)

        def stt(out, a, scalar, b, op0, op1):
            return V.scalar_tensor_tensor(out, a, scalar, b, op0, op1)

        def gate_values(t):
            dve.wait_ge(*after("gelu", t))
            dve.wait_ge(*after("psum", "fv", t))
            mul(gT[:, t, :], bank("fv", t), acc[:, t % 4, :]).then_inc(*now.both(("gT", t), ("free", "fv", t)))

        now = dve_in["start"]
        V.memset(eps_cols[:, 0:1], EPS).then_inc(*now.did())
        V.memset(eps_cols[:, 1:2], LN_EPS).then_inc(*now.did())
        V.memset(eps_cols[:, 2:3], GN_EPS).then_inc(*now.did())
        V.memset(eps_cols[:, 3:4], 1.0).then_inc(*now.did())
        V.memset(ones_row, 1.0).then_inc(*now.both(("eps",), ("ones_row",)))
        V.memset(lrcT[32:33, :], 1.0).then_inc(*now.did())
        V.memset(lrT[32:33, :], 1.0).then_inc(*now.did("lr_ones"))
        for which, i, n in (("c", 1, LC), ("x", 0, L)):
            dve.wait_ge(*after("rms", which))
            V.reciprocal(rstd[:, i, 0:n], rstd[:, i, 0:n]).then_inc(*now.did("rstd", which))
        dve.wait_ge(*after("psum", "ada1", ADA_FIRST - 1))
        dve.wait_ge(*after("cols"))
        ps = bank("ada1")[:, 0:32].rearrange("p (t n) -> p t n", n=2)
        V.tensor_tensor(modc, ps[:, :, 1], cols[:, COL["b_ada"]:COL["b_ada"] + 16], ALU.add).then_inc(*now.did("modc"))
        V.tensor_tensor(mod[:, 0:16], ps[:, :, 0], cols[:, COL["b_ada"]:COL["b_ada"] + 16], ALU.add).then_inc(
            *now.both(("mod1",), ("free", "ada1")))
        g1 = cols[:, COL["norm1_g"]:COL["norm1_g"] + 8]
        dve.wait_ge(*after("modc"))
        stt(gs1c, modc[:, 8:16], 1.0, g1, ALU.add, ALU.mult).then_inc(*now.did("gs1c"))
        dve.wait_ge(*after("mod1"))
        stt(gs1, mod[:, 8:16], 1.0, g1, ALU.add, ALU.mult).then_inc(*now.did("gs1"))
        dve.wait_ge(*after("gs1c"))
        dve.wait_ge(*after("rstd", "c"))
        dve.wait_ge(*after("ctx"))
        for k in range(DT):
            stt(hcT[:, k, :], ctxT[:, k, :], gs1c[:, k:k + 1], rstd[:, 1, 0:LC], ALU.mult, ALU.mult).then_inc(
                *now.did("hcT_scaled", k))
        dve.wait_ge(*after("gs1"))
        dve.wait_ge(*after("rstd", "x"))
        dve.wait_ge(*after("x"))
        for k in range(DT):
            stt(hT[:, k, :], xT[:, k, :], gs1[:, k:k + 1], rstd[:, 0, :], ALU.mult, ALU.mult).then_inc(
                *now.did("hT_scaled", k))

        now = dve_in["gla"]
        i = 0
        for group, out, n in (("zc", lac, TC), ("z", la, TT)):
            for d in range(2):
                for tt in range(n):
                    dve.wait_ge(*after("soft", group, d, tt))
                    stt(out[d][:, tt, :], bank(group, d, tt), 0.0, soft[i % 8], ALU.min, ALU.subtract).then_inc(
                        *now.both(("la" if group == "z" else "lac", d, tt), ("free", group, d, tt)))
                    i += 1
        dve.wait_ge(*after("psum", "ada2", ADA_REST - 1))
        V.tensor_tensor(mod[:, 16:48], bank("ada2")[:, 0:64].rearrange("p (t n) -> p t n", n=2)[:, :, 0],
                        cols[:, COL["b_ada"] + 16:COL["b_ada"] + 48], ALU.add).then_inc(
            *now.both(("mod2",), ("free", "ada2")))
        dve.wait_ge(*after("mod2"))
        stt(gs2, mod[:, 32:40], 1.0, cols[:, COL["norm2_g"]:COL["norm2_g"] + 8], ALU.add, ALU.mult).then_inc(
            *now.did("gs2"))
        e = 0
        for group, cps in (("cumc", 1), ("cum", 2)):
            for d in range(2):
                inc = slice(1, P + 1) if d == 0 else slice(0, P)
                for h in range(HEADS):
                    for cp in range(cps):
                        plus, minus = exps[:, e % 2], exps[:, 2 + e % 2]
                        dve.wait_ge(*after("exp", group, d, h, cp))
                        st = stats_c if group == "cumc" else stats_x
                        V.tensor_copy(st[:, d, h, 2 * cp:2 * cp + 2, :], plus[:, :, P + 1:CUM]).then_inc(
                            *now.did("stats", group, d, h, cp))
                        span = slice(2 * cp * P, 2 * (cp + 1) * P)
                        src, dst = (kcT, kc_inv) if group == "cumc" else (kT, k_inv)
                        dve.wait_ge(*after("kcT" if group == "cumc" else "kT", h))
                        if group == "cum":
                            dve.wait_ge(*after("qT", h))
                            mul(q_dec[d][:, h, span].rearrange("p (c t) -> p c t", c=2),
                                qT[:, h, span].rearrange("p (c t) -> p c t", c=2), plus[:, :, inc]).then_inc(
                                *now.did("q_dec", d, h, cp))
                        mul(dst[d][:, h, span].rearrange("p (c t) -> p c t", c=2),
                            src[:, h, span].rearrange("p (c t) -> p c t", c=2), minus[:, :, 0:P]).then_inc(
                            *now.both(("kc_inv" if group == "cumc" else "k_inv", d, h, cp), ("exp_used", e)))
                        e += 1
        for step in range(5):
            for d in range(2):
                if step < 2:
                    c, st, group = (step, 1 - step)[d], stats_c, "cumc"
                else:
                    c, st, group = order[d][step - 2], stats_x, "cum"
                for hp in range(2):
                    dve.wait_ge(*after("psum", "su", step, d, hp))
                    ps = bank("su", step, d, hp)
                    for i in range(2):
                        h = 2 * hp + i
                        s = s_gla[4 * d + h]
                        add = ps[:, i * DV:(i + 1) * DV]
                        freed = [("free", "su", step, d, hp)] if i else []
                        dve.wait_ge(*after("stats", group, d, h, c // 2))
                        if step == 0:
                            V.tensor_scalar(s, add, st[:, d, h, c, 2:3], None, ALU.mult).then_inc(
                                *now.both(("s", step, d, h), *freed))
                        else:
                            if step >= 2:
                                dve.wait_ge(*after("sm", d, h, order[d][step - 2]))
                            t = work[0][:, i * DV:(i + 1) * DV]
                            dve.wait_ge(now.sem, now.count)
                            V.tensor_scalar(t, add, st[:, d, h, c, 2:3], None, ALU.mult).then_inc(
                                *now.both(("s_add", step, d, h), *freed))
                            dve.wait_ge(*after("s_add", step, d, h))
                            stt(s, s, st[:, d, h, c, 1:2], t, ALU.mult, ALU.add).then_inc(*now.did("s", step, d, h))
        for c in range(TT):
            for d in range(2):
                dve.wait_ge(now.sem, now.count)
                dve.wait_ge(*after("psum", "sc", d, c))
                V.tensor_scalar(work[0], bank("sc", d, c), BIG, -BIG, ALU.min, ALU.max).then_inc(
                    *now.both(("clamped", d, c), ("free", "sc", d, c)))
                dve.wait_ge(*after("clamped", d, c))
                out = sc[:, c, :] if d == 0 else work[1]
                mul(out.rearrange("p (h t) -> p h t", h=4), work[0].rearrange("p (h t) -> p h t", h=4),
                    incl[d].unsqueeze(1).to_broadcast([P, 4, P])).then_inc(*now.did("masked", d, c))
                dve.wait_ge(*after("masked", d, c))
            V.tensor_tensor(sc[:, c, :], sc[:, c, :], work[1], ALU.add).then_inc(*now.did("sc", c))
            dve.wait_ge(*after("sc", c))
        for h in range(HEADS):
            dve.wait_ge(*after("o_rms", h))
            r = work[h % 2]
            V.reciprocal(r, r).then_inc(*now.did("o_rstd", h))
            dve.wait_ge(*after("o_rstd", h))
            for vt in range(2):
                t = 2 * h + vt
                dve.wait_ge(*after("oT", t))
                stt(oT[:, t, :], oT[:, t, :], col("gla_norm_g", t), r, ALU.mult, ALU.mult).then_inc(
                    *now.did("o_normed", t))

        now = dve_in["mix"]
        for t in range(DT):
            dve.wait_ge(*after("silu_r", t))
            dve.wait_ge(*after("o_normed", t))
            mul(oT[:, t, :], oT[:, t, :], silu_r[:, t, :]).then_inc(*now.did("ob", t))
        for t in range(DT):
            dve.wait_ge(*after("psum", "br_b", t))
            dve.wait_ge(*after("sgb", t))
            mul(sgb[:, t, :], bank("br_b", t), sgb[:, t, :]).then_inc(*now.both(("mb", t), ("free", "br_b", t)))
        for n in range(TT):
            for b in range(4):
                dve.wait_ge(*after("vs", b, n // 2))
            for half in range(2):
                V.bn_stats(bn[:, n, half, :], vs_tok[:, n, half * 512:(half + 1) * 512]).then_inc(
                    *now.did("bn", n, half))
            dve.wait_ge(*after("bn", n, 1))
            V.bn_aggr(mv[:, n, :], bn[:, n, :, :].rearrange("p h s -> p (h s)")).then_inc(*now.did("mv", n))
        dve.wait_ge(*after("ln_std"))
        V.reciprocal(ln_r, ln_r).then_inc(*now.did("ln_r"))
        dve.wait_ge(*after("ln_r"))
        dve.wait_ge(*after("ln_g"))
        dve.wait_ge(*after("ln_b"))
        for n in range(TT):
            V.tensor_scalar(vs_tok[:, n, :], vs_tok[:, n, :], mv[:, n, 0:1], ln_r[:, n:n + 1], ALU.subtract,
                            ALU.mult).then_inc(*now.did("vn0", n))
            dve.wait_ge(*after("vn0", n))
            mul(vs_tok[:, n, :], vs_tok[:, n, :], ln_g).then_inc(*now.did("vn1", n))
            dve.wait_ge(*after("vn1", n))
            V.tensor_tensor(vs_tok[:, n, :], vs_tok[:, n, :], ln_b, ALU.add).then_inc(*now.did("vn", n))
        for g in range(SGU_G):
            dve.wait_ge(*after("psum", "s", g))
            dve.wait_ge(*after("guT", g))
            mul(guT[:, g, :], bank("s", g), guT[:, g, :]).then_inc(*now.both(("aT", g), ("free", "s", g)))
        for t in range(DT):
            dve.wait_ge(*after("psum", "br_a", t))
            dve.wait_ge(*after("sga", t))
            mul(sga[:, t, :], bank("br_a", t), sga[:, t, :]).then_inc(*now.both(("ma", t), ("free", "br_a", t)))
            dve.wait_ge(*after("ma", t))
            dve.wait_ge(*after("mb", t))
            V.tensor_tensor(sga[:, t, :], sga[:, t, :], sgb[:, t, :], ALU.add).then_inc(*now.did("merged", t))
        for t in range(DT):
            dve.wait_ge(*after("psum", "w_o", t))
            dve.wait_ge(*after("mod2"))
            stt(xT[:, t, :], bank("w_o", t), mod[:, 16 + t:17 + t], xT[:, t, :], ALU.mult, ALU.add).then_inc(
                *now.both(("x1", t), ("free", "w_o", t)))

        now = dve_in["ffn"]
        V.memset(pads, 0.0).then_inc(*now.did("pads"))
        dve.wait_ge(*after("rms", "2"))
        V.reciprocal(rstd2[:, 0, :], rstd2[:, 0, :]).then_inc(*now.did("rstd2"))
        dve.wait_ge(*after("rstd2"))
        dve.wait_ge(*after("gs2"))
        for k in range(DT):
            stt(hT[:, k, :], xT[:, k, :], gs2[:, k:k + 1], rstd2[:, 0, :], ALU.mult, ALU.mult).then_inc(
                *now.did("h2T_scaled", k))
        for t in range(FT):
            a = acc[:, t % 4, :].rearrange("p (y x) -> p y x", x=GRID)
            dve.wait_ge(*after("conv", t, 0))
            for tap in range(1, 9):
                ky, kx = tap // 3, tap % 3
                stt(a, pads[:, t % 4, ky:ky + ROWS, kx:kx + GRID], col("conv_w", tap * FT + t), a, ALU.mult,
                    ALU.add).then_inc(*now.did("conv", t, tap))
                dve.wait_ge(*after("conv", t, tap))
            if t:
                gate_values(t - 1)
        gate_values(FT - 1)
        for t in range(DT):
            dve.wait_ge(*after("psum", "down", t))
            stt(xT[:, t, :], bank("down", t), mod[:, 40 + t:41 + t], xT[:, t, :], ALU.mult, ALU.add).then_inc(
                *now.both(("x2", t), ("free", "down", t)))
        dve.wait_ge(*after("rms", "3"))
        V.reciprocal(rstd2[:, 1, :], rstd2[:, 1, :]).then_inc(*now.did("rstd3"))
        dve.wait_ge(*after("rstd3"))
        for k in range(DT):
            stt(x2T[:, k, :], xT[:, k, :], col("final_norm_g", k), rstd2[:, 1, :], ALU.mult, ALU.mult).then_inc(
                *now.did("x2T", k))

        now = dve_in["rwkv"]
        dve.wait_ge(dve_in["ffn"].sem, dve_in["ffn"].count)
        mu = cols[:, COL["rw_mu"]:COL["rw_mu"] + 15]
        ka = cols[:, COL["k_a"]:COL["k_a"] + 4]
        V.tensor_scalar(mix_half, mu, 0.5, None, ALU.mult).then_inc(*now.did("mix_half"))
        V.tensor_scalar(mix_one, mu, -1.0, 1.0, ALU.mult, ALU.add).then_inc(*now.did("mix_one"))
        V.tensor_scalar(half_ka, ka, 0.5, None, ALU.mult).then_inc(*now.did())
        V.tensor_scalar(rest_ka, ka, -0.5, 1.0, ALU.mult, ALU.add).then_inc(*now.did())
        V.tensor_scalar(half_a0, cols[:, COL["a0"]:COL["a0"] + 8], 0.5, None, ALU.mult).then_inc(*now.did("half"))
        V.memset(state_m, 0.0).then_inc(*now.did())
        V.memset(raw[:, :, 0:1], 0.0).then_inc(*now.did())
        V.memset(raw[:, :, L + 1:L + 2], 0.0).then_inc(*now.did("raw_zero"))
        dve.wait_ge(*after("mix_half"))
        def key_squares(hp):
            if hp >= 2:
                dve.wait_ge(*after("psum", "kk", hp - 2))
            V.tensor_scalar(nkkT[:, hp, :], rkT[:, hp, :], col("k_k", hp), None, ALU.mult).then_inc(
                *now.did("kk_raw", hp))
            dve.wait_ge(*after("kk_raw", hp))
            mul(kk_sq[:, hp % 2, :], nkkT[:, hp, :], nkkT[:, hp, :]).then_inc(*now.did("kk_sq", hp))

        def keys_normalised(hp):
            n = kk_n[:, hp % 2, :]
            dve.wait_ge(*after("kk_norm", hp))
            V.tensor_scalar(n, n, 1e-12, None, ALU.max).then_inc(*now.did("kk_max", hp))
            dve.wait_ge(*after("kk_max", hp))
            V.reciprocal(n, n).then_inc(*now.did("kk_inv", hp))
            dve.wait_ge(*after("kk_inv", hp))
            stt(nkkT[:, hp, :], nkkT[:, hp, :], -1.0, n, ALU.mult, ALU.mult).then_inc(*now.did("nkk", hp))

        def mix(i):
            t = RW_TILES[i]
            dve.wait_ge(*after("raw", t))
            V.tensor_tensor(pair_sum[:, i % 2, :], raw[:, i % 3, 0:L], raw[:, i % 3, 2:L + 2], ALU.add).then_inc(
                *now.did("pair_sum", t))
            dve.wait_ge(*after("pair_sum", t))
            dve.wait_ge(*after("mixed0", t))
            stt(mixed[t], pair_sum[:, i % 2, :], mix_half[:, t:t + 1], mixed[t], ALU.mult, ALU.add).then_inc(
                *now.did("mixed", t))
            dve.wait_ge(*after("mixed", t))
            if t == 7:
                key_squares(0)
                key_squares(1)
            if t == 0:
                key_squares(2)
                key_squares(3)
            if t in (1, 2, 3, 8):
                keys_normalised((1, 2, 3, 8).index(t))

        for i in range(14):
            mix(i)

        def as_chunks(ap):
            return ap.rearrange("p (c t) -> p c t", c=TT)

        def prepare(j, part):
            hp, d = JOBS[j]
            s = sets[j % 2]
            inc, exc = (slice(1, P + 1), slice(0, P)) if d == 0 else (slice(0, P), slice(1, P + 1))
            plus = exps[:, 0:2].rearrange("p a c j -> p (a c) j")
            minus = exps[:, 2:4].rearrange("p a c j -> p (a c) j")
            dve.wait_ge(now.sem, now.count)
            if part == 0:
                dve.wait_ge(*after("a", j))
                V.tensor_scalar(job_t, aT, half_ka[:, hp:hp + 1], rest_ka[:, hp:hp + 1], ALU.mult, ALU.add).then_inc(
                    *now.did("job_t", j))
                dve.wait_ge(*after("job_t", j))
                mul(kdT, job_t, rkT[:, hp, :]).then_inc(*now.did("kd", j))
            if part == 1:
                V.tensor_scalar(job_t, aT, -0.5, -0.5, ALU.mult, ALU.add).then_inc(*now.did("job_t2", j))
                dve.wait_ge(*after("job_t2", j))
                mul(job_t, job_t, nkkT[:, hp, :]).then_inc(*now.did("kka", j))
                if d == 0:
                    V.tensor_copy(kd_sum, kdT).then_inc(*now.did("kd_sum", hp))
                else:
                    V.tensor_tensor(kd_sum, kd_sum, kdT, ALU.add).then_inc(*now.did("kd_sum2", hp))
            if part == 2:
                dve.wait_ge(*after("rexp", j))
                mul(as_chunks(bkT[:, 0, :]), as_chunks(job_t), minus[:, :, 0:P]).then_inc(*now.did("job_b", j))
                mul(as_chunks(bkT[:, 1, :]), as_chunks(kdT), minus[:, :, 0:P]).then_inc(*now.did("job_k", j))
                if d == 1:
                    stt(kd_sum, kd_sum, col("r_k", hp), rT[:, hp, :], ALU.mult, ALU.mult).then_inc(
                        *now.did("bonus_in", hp))
            if part == 3:
                mul(s["ar"][:, :, 0, :], as_chunks(nkkT[:, hp, :]), plus[:, :, exc]).then_inc(*now.did("job_a", j))
                mul(s["ar"][:, :, 1, :], as_chunks(rT[:, hp, :]), plus[:, :, inc]).then_inc(*now.did("job_r", j))
                V.tensor_copy(job_stats[:, j % 2, :, :], plus[:, :, P + 1:CUM]).then_inc(*now.did("job_stats", j))

        def gram(j, i, cp):
            d = JOBS[j][1]
            dst = sets[j % 2][("nqb", "mqk")[i]]
            for h in range(2):
                dve.wait_ge(*after("psum", "gram", j, i, cp, h))
                mul(dst[:, 4 * cp + h:4 * cp + h + 3:2, :, :].rearrange("p n a t -> p n (a t)"),
                    bank("gram", j, i, cp, h).rearrange("p (n t) -> p n t", n=2),
                    pair_mask[d].unsqueeze(1).to_broadcast([P, 2, 2 * P])).then_inc(
                    *now.both(("gram", j, i, cp, h), ("free", "gram", j, i, cp, h)))

        def inverse_start(j):
            s = sets[j % 2]
            dve.wait_ge(*after("gram", j, 0, 1, 1))
            lt = s["nqb"][:, :, 0, :]
            V.tensor_tensor(lt, lt, ident.unsqueeze(1).to_broadcast([P, 8, P]), ALU.add).then_inc(*now.did("lt", j))
            dve.wait_ge(*after("lt", j))
            mul(s["g"], lt, level_mask[1 - JOBS[j][1]][0].unsqueeze(1).to_broadcast([P, 8, P])).then_inc(
                *now.did("g0", j))

        def bonus(j):
            hp, d = JOBS[j]
            if d == 1:
                dve.wait_ge(*after("psum", "bonus", hp))
                mul(rvT[:, hp, :], bank("bonus", hp), rvT[:, hp, :]).then_inc(
                    *now.both(("bonus", hp), ("free", "bonus", hp)))

        def invert_y(j, lv, half):
            dve.wait_ge(*after("psum", "iy", j, lv, half))
            dve.wait_ge(now.sem, now.count)
            mul(Y[:, 4 * half:4 * half + 4, :], bank("iy", j, lv, half).rearrange("p (s t) -> p s t", s=4),
                level_mask[JOBS[j][1]][lv + 1].unsqueeze(1).to_broadcast([P, 4, P])).then_inc(
                *now.both(("yi", j, lv, half), ("free", "iy", j, lv, half)))

        def chain_start(j, step):
            if step:
                c = order[JOBS[j][1]][step]
                dve.wait_ge(*after("state", j, step))
                for h, rows in enumerate((LO, HI)):
                    V.tensor_scalar(state_m[rows, h * RH:(h + 1) * RH], state[rows, j % 2, :],
                                    job_stats[rows, j % 2, c, 0:1], None, ALU.mult).then_inc(
                        *(now.did("state_m", j, step) if h else now.did()))

        def chain_sa(j, step):
            dve.wait_ge(now.sem, now.count)
            dve.wait_ge(*after("psum", "cs", j, step))
            V.tensor_copy(sab, bank("cs", j, step)[:, 0:P].rearrange("p (h v) -> p h v", h=2)).then_inc(
                *now.both(("sa", j, step), ("free", "cs", j, step)))

        def chain_end(j, step):
            hp, d = JOBS[j]
            c = order[d][step]
            dve.wait_ge(now.sem, now.count)
            if step < 3:
                dve.wait_ge(*after("psum", "ch", j, step))
                st = job_stats[:, j % 2, c, :]
                s = state[:, j % 2, :]
                if step == 0:
                    V.tensor_scalar(s, bank("ch", j, step)[:, 0:64], st[:, 2:3], None, ALU.mult).then_inc(
                        *now.both(("state", j, 1), ("free", "ch", j, step)))
                else:
                    V.tensor_scalar(state_t, bank("ch", j, step)[:, 0:64], st[:, 2:3], None, ALU.mult).then_inc(
                        *now.both(("state_t", j, step), ("free", "ch", j, step)))
                    dve.wait_ge(*after("state_t", j, step))
                    stt(s, s, st[:, 1:2], state_t, ALU.mult, ALU.add).then_inc(*now.did("state", j, step + 1))
            dve.wait_ge(*after("psum", "cy", j, step))
            y = yT[:, hp, c * P:(c + 1) * P]
            if d == 0:
                ins = V.tensor_copy(y, bank("cy", j, step)[:, 0:P])
            else:
                dve.wait_ge(*after("y_chunk", j - 1, c))
                ins = V.tensor_tensor(y, bank("cy", j, step)[:, 0:P], y, ALU.add)
            ins.then_inc(*now.both(("y_chunk", j, c), ("y", j), ("free", "cy", j, step)))

        for part in range(4):
            prepare(0, part)
        mix(14)
        gram(0, 0, 0)
        gram(0, 0, 1)
        inverse_start(0)
        for j in range(len(JOBS) + 1):
            new, old, ahead = j < len(JOBS), j > 0, j + 1 < len(JOBS)
            if new:
                gram(j, 1, 0)
            if old:
                chain_sa(j - 1, 0)
            if new:
                gram(j, 1, 1)
                bonus(j)
            if old:
                chain_end(j - 1, 0)
            for lv in range(5):
                chained = old and lv < 3
                if chained:
                    chain_start(j - 1, lv + 1)
                if new:
                    invert_y(j, lv, 0)
                    invert_y(j, lv, 1)
                if chained:
                    chain_sa(j - 1, lv + 1)
                    chain_end(j - 1, lv + 1)
                if ahead and lv < 4:
                    prepare(j + 1, lv)
            if new:
                first, second = (LO, HI) if JOBS[j][1] == 0 else (HI, LO)
                dve.wait_ge(*after("psum", "il", j, 0))
                V.tensor_copy(Y[second, :, first], bank("il", j, 0)[second, :].rearrange("p (s t) -> p s t", s=8)
                              ).then_inc(*now.both(("y_last", j), ("free", "il", j, 0)))
            if ahead:
                gram(j + 1, 0, 0)
            if new:
                dve.wait_ge(*after("psum", "il", j, 1))
                V.tensor_copy(sets[j % 2]["g"][first, :, second],
                              bank("il", j, 1)[first, :].rearrange("p (s t) -> p s t", s=8)).then_inc(
                    *now.both(("g_done", j), ("free", "il", j, 1)))
            if ahead:
                gram(j + 1, 0, 1)
                inverse_start(j + 1)

        dve.wait_ge(now.sem, now.count)
        for hp in range(HT):
            dve.wait_ge(*after("psum", "ym", hp))
            dve.wait_ge(*after("y", 2 * hp + 1))
            stt(yT[:, hp, :], bank("ym", hp), -1.0 / RH, yT[:, hp, :], ALU.mult, ALU.add).then_inc(
                *now.both(("yc", hp), ("free", "ym", hp)))
            dve.wait_ge(*after("yc", hp))
            mul(y_sq[:, hp, :], yT[:, hp, :], yT[:, hp, :]).then_inc(*now.did("y_sq", hp))
        for hp in range(HT):
            r = gn_s[:, hp % 2, :]
            dve.wait_ge(*after("gn_std", hp))
            V.reciprocal(r, r).then_inc(*now.did("gn_r", hp))
            dve.wait_ge(*after("gn_r", hp))
            stt(yT[:, hp, :], yT[:, hp, :], col("gn_w", hp), r, ALU.mult, ALU.mult).then_inc(*now.did("yn", hp))
            dve.wait_ge(*after("yn", hp))
            dve.wait_ge(*after("bonus", hp))
            stt(yT[:, hp, :], yT[:, hp, :], col("gn_b", hp), rvT[:, hp, :], ALU.add, ALU.add).then_inc(
                *now.did("yb", hp))
            dve.wait_ge(*after("yb", hp))
            dve.wait_ge(*after("psum", "g", hp))
            mul(yT[:, hp, :], bank("g", hp), yT[:, hp, :]).then_inc(*now.both(("yT", hp), ("free", "g", hp)))

        now = dve_in["hyena"]
        dve.wait_ge(dve_in["rwkv"].sem, dve_in["rwkv"].count)
        V.memset(raw[:, :, 0:1], 0.0).then_inc(*now.did())
        V.memset(raw[:, :, L + 1:L + 2], 0.0).then_inc(*now.did("raw_zero2"))
        dve.wait_ge(*after("filters"))
        for o in range(2):
            V.tensor_tensor(fsd[:, o, 0, :], fw4[:, o, 0, :], fw4[:, o, 1, :], ALU.add).then_inc(
                *now.did("fsd", o, 0))
            V.tensor_tensor(fsd[:, o, 1, :], fw4[:, o, 0, :], fw4[:, o, 1, :], ALU.subtract).then_inc(
                *now.did("fsd", o, 1))
        mul(filt_sb[0:64, :], cols[0:64, COL["filt_b"]:COL["filt_b"] + 3],
            cols[0:64, COL["filt_sf"]:COL["filt_sf"] + 3]).then_inc(*now.did("filt_sb"))
        turn = 2.0 * math.pi
        parts = [6.28125, 0.0019340515136718750, turn - 6.28125 - 0.0019340515136718750]
        magic = 1.5 * 2.0 ** 23
        def sine_argument(n):
            dve.wait_ge(now.sem, now.count)
            dve.wait_ge(*after("filt_a", n))
            V.tensor_scalar(filt_k, filt_a, 1.0 / turn, magic, ALU.mult, ALU.add).then_inc(*now.did("fk", n))
            dve.wait_ge(*after("fk", n))
            V.tensor_scalar(filt_k, filt_k, -magic, None, ALU.add).then_inc(*now.did("fr", n, -1))
            dve.wait_ge(*after("fr", n, -1))
            for i, part in enumerate(parts):
                stt(filt_a, filt_k, -part, filt_a, ALU.mult, ALU.add).then_inc(*now.did("fr", n, i))
                dve.wait_ge(*after("fr", n, i))
            V.tensor_scalar(filt_a, filt_a, 3.1415925, -3.1415925, ALU.min, ALU.max).then_inc(*now.did("filt_r", n))

        for t in range(12):
            dve.wait_ge(*after("hy0", t))
            stt(hyT[:, t, :], raw[:, t % 3, 0:L], col("hy_conv_w", t), hyT[:, t, :], ALU.mult, ALU.add).then_inc(
                *now.did("hy1", t))
            dve.wait_ge(*after("hy1", t))
            stt(hyT[:, t, :], raw[:, t % 3, 2:L + 2], col("hy_conv_w", 24 + t), hyT[:, t, :], ALU.mult,
                ALU.add).then_inc(*now.did("hyT", t))
            if t in (5, 7, 9):
                sine_argument((t - 5) // 2)
        for o in range(2):
            for sd in range(2):
                for tt in range(TT):
                    dve.wait_ge(*after("psum", "hf", o, sd, tt))
                    dve.wait_ge(*after("window"))
                    mul(ht[o][sd][:, tt, :], bank("hf", o, sd, tt), window[:, tt, :]).then_inc(
                        *now.both(("ht0" if (sd, tt) == (0, 0) else "ht", o, sd, tt), ("free", "hf", o, sd, tt)))
                    if (sd, tt) == (0, 0):
                        dve.wait_ge(*after("ht0", o, 0, 0))
                        dve.wait_ge(*after("skip"))
                        first = ht[o][0][0:1, 0, :]
                        V.tensor_tensor(first, first, skip_row[:, o * HW:(o + 1) * HW], ALU.add).then_inc(
                            *now.both(("ht", o, 0, 0), ("skip_added", o)))
        for o in range(2):
            Hc, Hs = Hcs[o]
            for ft in range(TT):
                p = [prod[:, 4 * (ft % 2) + i, :] for i in range(4)]
                dve.wait_ge(now.sem, now.count)
                dve.wait_ge(*after("psum", "Z", o, 0, ft))
                dve.wait_ge(*after("H", o, 0, ft))
                dve.wait_ge(*after("H", o, 1, ft))
                zc = bank("Z", o, 0, ft)
                mul(p[0], zc, Hc[:, ft, :]).then_inc(*now.did("p", o, ft, 0))
                mul(p[2], zc, Hs[:, ft, :]).then_inc(*now.both(("p", o, ft, 2), ("free", "Z", o, 0, ft)))
                dve.wait_ge(*after("psum", "Z", o, 1, ft))
                zs = bank("Z", o, 1, ft)
                mul(p[1], zs, Hs[:, ft, :]).then_inc(*now.did("p", o, ft, 1))
                mul(p[3], zs, Hc[:, ft, :]).then_inc(*now.both(("p", o, ft, 3), ("free", "Z", o, 1, ft)))
                dve.wait_ge(*after("p", o, ft, 1))
                V.tensor_tensor(Ycs[0][:, ft, :], p[0], p[1], ALU.subtract).then_inc(*now.did("Y", o, 0, ft))
                dve.wait_ge(*after("p", o, ft, 3))
                V.tensor_tensor(Ycs[1][:, ft, :], p[2], p[3], ALU.add).then_inc(*now.did("Y", o, 1, ft))
            for tt in range(TT):
                dve.wait_ge(*after("psum", "conv", o, tt))
                if o == 0:
                    dve.wait_ge(*after("x1_tok", tt))
                    out, gate, name = xv_tok[:, tt, :], x1_tok[:, tt, :], ("z2", tt)
                else:
                    out, gate, name = zT[:, tt, :], hyT[:, 8 + tt, :], ("zT", tt)
                stt(out, bank("conv", o, tt), 1.0 / L, gate, ALU.mult, ALU.mult).then_inc(
                    *now.both(name, ("free", "conv", o, tt)))

        now = dve_in["ffn2"]
        dve.wait_ge(dve_in["hyena"].sem, dve_in["hyena"].count)
        for t in range(DT):
            dve.wait_ge(*after("psum", "rwo", t))
            dve.wait_ge(*after("gate", 8 + t))
            mul(gate_r[:, t, :], bank("rwo", t), gate_r[:, t, :]).then_inc(*now.both(("mr", t), ("free", "rwo", t)))
        for t in range(DT):
            dve.wait_ge(*after("psum", "hyo", t))
            dve.wait_ge(*after("gate", t))
            mul(gate_h[:, t, :], bank("hyo", t), gate_h[:, t, :]).then_inc(*now.both(("mh", t), ("free", "hyo", t)))
            dve.wait_ge(*after("mh", t))
            dve.wait_ge(*after("mr", t))
            V.tensor_tensor(gate_h[:, t, :], gate_h[:, t, :], gate_r[:, t, :], ALU.add).then_inc(
                *now.did("merged2", t))
        for n, group in enumerate(("w_o2", "down2")):
            for t in range(DT):
                dve.wait_ge(*after("psum", group, t))
                stt(x2T[:, t, :], x2T[:, t, :], ALPHA, bank(group, t), ALU.mult, ALU.add).then_inc(
                    *now.both(("res%d" % n, t), ("free", group, t)))
            dve.wait_ge(now.sem, now.count)
            dve.wait_ge(*after("psum", "lm%d" % n))
            mean = norm_s[:, 1, :]
            V.tensor_scalar(mean, bank("lm%d" % n), 1.0 / D, None, ALU.mult).then_inc(
                *now.both(("mean", n), ("free", "lm%d" % n)))
            dve.wait_ge(*after("mean", n))
            for t in range(DT):
                V.tensor_tensor(lnc[:, t, :], x2T[:, t, :], mean, ALU.subtract).then_inc(*now.did("lnc", n, t))
            dve.wait_ge(*after("ln_std2", n))
            r = norm_s[:, 0, :]
            V.reciprocal(r, r).then_inc(*now.did("ln_rstd", n))
            dve.wait_ge(*after("ln_rstd", n))
            for t in range(DT):
                stt(lnc[:, t, :], lnc[:, t, :], col("ln%d_w" % (n + 1), t), r, ALU.mult, ALU.mult).then_inc(
                    *now.did("lnn", n, t))
            if n == 0:
                for t in range(FT):
                    dve.wait_ge(*after("psum", "fu", t))
                    dve.wait_ge(*after("silu_g", t))
                    mul(gT2[:, t, :], bank("fu", t), silu_g[:, t % 4, :]).then_inc(
                        *now.both(("gT2", t), ("free", "fu", t)))

    @block.scalar
    def _(act):

        def run(out, src, func, **kw):
            return nc.scalar.activation(out, src, func, **kw)

        def eps(i, rows=slice(0, P)):
            return eps_cols[rows, i:i + 1]

        now = act_in["start"]
        act.dma_start(ctxT, io["ctxT"]).then_inc(*loads["ctx"].loaded("ctx"))
        act.dma_start(cols[:, :], io["cols"]).then_inc(*loads["cols"].loaded("cols"))
        act.dma_start(consts[:, :], io["consts"]).then_inc(*loads["consts"].loaded("consts"))
        act.dma_start(xT, io["xT"]).then_inc(*loads["x"].loaded("x"))
        act.wait_ge(*after("ctx"))
        for k in range(DT):
            run(sq5[:, k, 0:LC], ctxT[:, k, :], ACT.Square).then_inc(*now.did("sqc", k))
        act.wait_ge(*after("x"))
        for k in range(DT):
            run(sq[:, k, :], xT[:, k, :], ACT.Square).then_inc(*now.did("sq", k))
        act.wait_ge(*after("cols"))
        run(csil[:, :, 0], cols[:, COL["c"]:COL["c"] + 8], ACT.Silu).then_inc(*now.did())
        run(csil[:, :, 1], cols[:, COL["c_ctx"]:COL["c_ctx"] + 8], ACT.Silu).then_inc(*now.did("csil"))
        act.wait_ge(*after("eps"))
        for which, i, n in (("c", 1, LC), ("x", 0, L)):
            act.wait_ge(*after("psum", "ss_" + which))
            run(rstd[:, i, 0:n], bank("ss_" + which)[:, 0:n], ACT.Sqrt, scale=1.0 / D, bias=eps(0)).then_inc(
                *now.both(("rms", which), ("free", "ss_" + which)))
        for k in range(DT):
            act.wait_ge(*after("hcT_scaled", k))
            run(hcT[:, k, :], hcT[:, k, :], ACT.Identity, bias=modc[:, k:k + 1]).then_inc(*now.did("hcT", k))
        for k in range(DT):
            act.wait_ge(*after("hT_scaled", k))
            run(hT[:, k, :], hT[:, k, :], ACT.Identity, bias=mod[:, k:k + 1]).then_inc(*now.did("hT", k))

        now = act_in["gla"]
        for t in range(HEADS):
            act.wait_ge(*after("psum", "kc", t))
            run(kcT[:, t, :], bank("kc", t)[:, 0:LC], ACT.Copy).then_inc(*now.both(("kcT", t), ("free", "kc", t)))
            act.wait_ge(*after("psum", "k", t))
            run(kT[:, t, :], bank("k", t), ACT.Copy).then_inc(*now.both(("kT", t), ("free", "k", t)))

        def evacuate_tokens(group, b, half, dst, func, name):
            act.wait_ge(*after("psum", group, b, half))
            run(dst[:, 2 * half:2 * half + 2, b * BLK:(b + 1) * BLK],
                bank(group, b, half).rearrange("p (i c) -> p i c", i=2), func).then_inc(
                *now.both(name, ("free", group, b, half)))

        for b in range(4):
            evacuate_tokens("vc", b, 0, vc_tok, ACT.Copy, ("vc_tok", b))
            evacuate_tokens("v", b, 0, v_tok, ACT.Copy, ("v_tok0", b))
            evacuate_tokens("v", b, 1, v_tok, ACT.Copy, ("v_tok", b))
        act.wait_ge(*after("psum", "lrc"))
        run(lrcT[0:32, :], bank("lrc")[0:32, 0:LC], ACT.Copy).then_inc(*now.both(("lrcT",), ("free", "lrc")))
        act.wait_ge(*after("psum", "lr"))
        run(lrT[0:32, :], bank("lr")[0:32, :], ACT.Copy).then_inc(*now.both(("lrT",), ("free", "lr")))
        for t in range(HEADS):
            act.wait_ge(*after("psum", "q", t))
            run(qT[:, t, :], bank("q", t), ACT.Copy, scale=DK ** -0.5).then_inc(*now.both(("qT", t), ("free", "q", t)))

        zs = [("zc", d, tt) for d in range(2) for tt in range(TC)] + [("z", d, tt) for d in range(2) for tt in range(TT)]
        for i, (group, d, tt) in enumerate(zs):
            buf = soft[i % 8]
            act.wait_ge(*after("psum", group, d, tt))
            if i >= 8:
                act.wait_ge(*after(*("free",) + zs[i - 8]))
            run(buf, bank(group, d, tt), ACT.Abs).then_inc(*now.did("abs", i))
            act.wait_ge(*after("abs", i))
            run(buf, buf, ACT.Exp, scale=-1.0).then_inc(*now.did("exp_z", i))
            act.wait_ge(*after("exp_z", i))
            run(buf, buf, ACT.Ln, bias=eps(3)).then_inc(*now.did("soft", group, d, tt))
        e = 0
        for group, cps in (("cumc", 1), ("cum", 2)):
            for d in range(2):
                inc = slice(1, P + 1) if d == 0 else slice(0, P)
                for h in range(HEADS):
                    for cp in range(cps):
                        act.wait_ge(*after("psum", group, d, h, cp))
                        if e >= 2:
                            act.wait_ge(*after("exp_used", e - 2))
                        ps = bank(group, d, h, cp)[:, 0:2 * CUM].rearrange("p (c j) -> p c j", c=2)
                        run(exps[:, e % 2], ps, ACT.Exp).then_inc(*now.did())
                        run(exps[:, 2 + e % 2, :, 0:P], ps[:, :, inc], ACT.Exp, scale=-1.0).then_inc(
                            *now.both(("exp", group, d, h, cp), ("free", group, d, h, cp)))
                        e += 1
        for group, dst, chunks, name in (("ktc", kc_tok, TC, "kc_tok"), ("kt", k_tok, TT, "k_tok")):
            for d in range(2):
                for c in range(chunks):
                    act.wait_ge(*after("psum", group, d, c))
                    run(dst[d][:, c, :], bank(group, d, c), ACT.Copy).then_inc(
                        *now.both((name, d, c), ("free", group, d, c)))
        act.wait_ge(*after("k_inv", 1, 3, 1))
        for i in range(TT):
            for d in range(2):
                c = order[d][i]
                for h in range(HEADS):
                    act.wait_ge(*after("s", 1 + i, d, h))
                    run(sm[d][h][c], s_gla[4 * d + h], ACT.Copy, scale=stats_x[:, d, h, c, 0:1]).then_inc(
                        *now.did("sm", d, h, c))

        def output_rms(h):
            act.wait_ge(*after("psum", "oss", h))
            if h >= 2:
                act.wait_ge(*after("o_normed", 2 * (h - 2) + 1))
            run(work[h % 2], bank("oss", h), ACT.Sqrt, scale=1.0 / DV, bias=eps(0)).then_inc(
                *now.both(("o_rms", h), ("free", "oss", h)))

        for h in range(HEADS):
            for t in (2 * h, 2 * h + 1):
                act.wait_ge(*after("psum", "o", t))
                run(oT[:, t, :], bank("o", t), ACT.Copy).then_inc(*now.did("oT", t))
                if h >= 2:
                    act.wait_ge(*after("psum", "oss", h - 2))
                run(osq[:, t % 4, :], bank("o", t), ACT.Square).then_inc(*now.both(("osq", t), ("free", "o", t)))
            if h >= 1:
                output_rms(h - 1)

        now = act_in["mix"]

        def evacuate(group, t, dst, func, name, **kw):
            act.wait_ge(*after("psum", group, t))
            run(dst, bank(group, t), func, **kw).then_inc(*now.both((name, t), ("free", group, t)))

        for t in range(DT):
            evacuate("r", t, silu_r[:, t, :], ACT.Silu, "silu_r")
            if t == 1:
                output_rms(HEADS - 1)
        for t in range(DT):
            evacuate("gb", t, sgb[:, t, :], ACT.Sigmoid, "sgb")
        for t in range(DT):
            evacuate("ga", t, sga[:, t, :], ACT.Sigmoid, "sga")
        for b in range(4):
            for half in range(2):
                evacuate_tokens("vs", b, half, vs_tok, ACT.Gelu, ("vs", b, half))
        for t in range(DT):
            evacuate("u", t, guT[:, t, :], ACT.Gelu, "guT")
            if t == 3:
                act.wait_ge(*after("mv", 3))
                run(ln_r, mv[:, :, 1], ACT.Sqrt, bias=eps(0)).then_inc(*now.did("ln_std"))
        for k in range(DT):
            act.wait_ge(*after("x1", k))
            run(sq5[:, k, :], xT[:, k, :], ACT.Square).then_inc(*now.did("sq2", k))
        act.wait_ge(*after("psum", "ss2"))
        run(rstd2[:, 0, :], bank("ss2"), ACT.Sqrt, scale=1.0 / D, bias=eps(0)).then_inc(
            *now.both(("rms", "2"), ("free", "ss2")))

        now = act_in["ffn"]
        for k in range(DT):
            act.wait_ge(*after("h2T_scaled", k))
            run(hT[:, k, :], hT[:, k, :], ACT.Identity, bias=mod[:, 24 + k:25 + k]).then_inc(*now.did("h2T", k))
        act.wait_ge(*after("pads"))

        def gelu(t):
            act.wait_ge(*after("conv", t, 8))
            run(acc[:, t % 4, :], acc[:, t % 4, :], ACT.Gelu).then_inc(*now.did("gelu", t))

        for t in range(FT):
            act.wait_ge(*after("psum", "fa", t))
            if t >= 4:
                act.wait_ge(*after("conv", t - 4, 8))
            run(pads[:, t % 4, 1:1 + ROWS, 1:1 + GRID], bank("fa", t).rearrange("p (y x) -> p y x", x=GRID),
                ACT.Copy).then_inc(*now.both(("pad", t), ("free", "fa", t)))
            act.wait_ge(*after("pad", t))
            if t >= 4:
                act.wait_ge(*after("gT", t - 4))
            run(acc[:, t % 4, :].rearrange("p (y x) -> p y x", x=GRID), pads[:, t % 4, 0:ROWS, 0:GRID], ACT.Identity,
                scale=col("conv_w", t), bias=col("conv_b", t)).then_inc(*now.did("conv", t, 0))
            if t:
                gelu(t - 1)
        gelu(FT - 1)
        for k in range(DT):
            act.wait_ge(*after("x2", k))
            run(sq5[:, k, :], xT[:, k, :], ACT.Square).then_inc(*now.did("sq3", k))
        act.wait_ge(*after("psum", "ss3"))
        run(rstd2[:, 1, :], bank("ss3"), ACT.Sqrt, scale=1.0 / D, bias=eps(0)).then_inc(
            *now.both(("rms", "3"), ("free", "ss3")))

        now = act_in["rwkv"]
        act.wait_ge(*after("raw_zero"))
        act.wait_ge(*after("mix_one"))
        def key_norm(hp):
            if hp >= 2:
                act.wait_ge(*after("nkk", hp - 2))
            evacuate("kk", hp, kk_n[:, hp % 2, :], ACT.Sqrt, "kk_norm")

        def project(i):
            t = RW_TILES[i]
            if i >= 3:
                act.wait_ge(*after("mixed", RW_TILES[i - 3]))
            evacuate("rw", t, raw[:, i % 3, 1:L + 1], ACT.Copy, "raw")
            act.wait_ge(*after("raw", t))
            run(mixed[t], raw[:, i % 3, 1:L + 1], ACT.Copy, scale=mix_one[:, t:t + 1]).then_inc(
                *now.did("mixed0", t))
            if t == 4:
                act.wait_ge(*after("mixed", 12))
                run(wdT, wdT, ACT.Tanh).then_inc(*now.did("wd_tanh"))
            if t == 1:
                key_norm(0)
                key_norm(1)
            if t in (7, 2):
                d = (7, 2).index(t)
                for tt in range(TT):
                    act.wait_ge(*after("psum", "w", d, tt))
                    run(lw[d][:, tt, :], bank("w", d, tt), ACT.Sigmoid).then_inc(
                        *now.both(("lw", d, tt), ("free", "w", d, tt)))
            if t in (2, 3):
                key_norm(t)

        for i in range(14):
            project(i)
        act.wait_ge(*after("half"))

        def inputs(j):
            hp, d = JOBS[j]
            inc = slice(1, P + 1) if d == 0 else slice(0, P)
            if j:
                act.wait_ge(*after("job_stats", j - 1))
            evacuate("a", j, aT, ACT.Tanh, "a", scale=0.5, bias=half_a0[:, 4 * d + hp:4 * d + hp + 1])
            for cp in range(2):
                act.wait_ge(*after("psum", "rcum", j, cp))
                ps = bank("rcum", j, cp)[:, 0:2 * CUM].rearrange("p (c j) -> p c j", c=2)
                run(exps[:, cp], ps, ACT.Exp).then_inc(*now.did())
                run(exps[:, 2 + cp, :, 0:P], ps[:, :, inc], ACT.Exp, scale=-1.0).then_inc(
                    *now.both(("rexp", j), ("free", "rcum", j, cp)))

        def tokens(j):
            for i, dst in ((0, "b_tok"), (1, "k_tok")):
                act.wait_ge(*after("psum", "tok", j, i))
                run(sets[j % 2][dst], bank("tok", j, i).rearrange("p (c f) -> p c f", c=4), ACT.Copy).then_inc(
                    *now.both(("tok", j, i), ("free", "tok", j, i)))

        def inverse_start(j, half):
            act.wait_ge(*after("psum", "x0", j, half))
            run(X[:, 4 * half:4 * half + 4, :], bank("x0", j, half).rearrange("p (s t) -> p s t", s=4),
                ACT.Copy).then_inc(*now.both(("x", j, 0, half), ("free", "x0", j, half)))

        def invert_xg(j, lv, half):
            for what, dst, name in (("ix", X, "x"), ("ig", sets[j % 2]["g"], "g")):
                act.wait_ge(*after("psum", what, j, lv, half))
                run(dst[:, 4 * half:4 * half + 4, :], bank(what, j, lv, half).rearrange("p (s t) -> p s t", s=4),
                    ACT.Copy).then_inc(*now.both((name, j, lv + 1, half), ("free", what, j, lv, half)))

        def chain_u(j, step):
            act.wait_ge(*after("psum", "cu", j, step))
            run(ub, bank("cu", j, step)[:, 0:P].rearrange("p (h v) -> p h v", h=2), ACT.Copy).then_inc(
                *now.both(("u", j, step), ("free", "cu", j, step)))

        inputs(0)
        project(14)
        for c in range(TT):
            evacuate("vt", c, rv_tok[:, c, :], ACT.Copy, "rv_tok")
        tokens(0)
        act.wait_ge(*after("mixed", 14))
        run(gdT, gdT, ACT.Sigmoid).then_inc(*now.did("gd_sig"))
        for j in range(len(JOBS) + 1):
            new, old, ahead = j < len(JOBS), j > 0, j + 1 < len(JOBS)
            if old:
                chain_u(j - 1, 0)
            if new:
                inverse_start(j, 0)
                inverse_start(j, 1)
            if ahead:
                inputs(j + 1)
            for lv in range(5):
                if old and lv < 3:
                    chain_u(j - 1, lv + 1)
                if new:
                    invert_xg(j, lv, 0)
                    invert_xg(j, lv, 1)
            if ahead:
                tokens(j + 1)
        for hp in range(HT):
            act.wait_ge(*after("psum", "yv", hp))
            if hp >= 2:
                act.wait_ge(*after("yn", hp - 2))
            run(gn_s[:, hp % 2, :], bank("yv", hp), ACT.Sqrt, scale=1.0 / RH, bias=eps(2)).then_inc(
                *now.both(("gn_std", hp), ("free", "yv", hp)))

        now = act_in["hyena"]
        act.wait_ge(*after("raw_zero2"))
        def filter_layer(n):
            act.wait_ge(*after("filt_sb"))
            act.wait_ge(*after("psum", "filt", n))
            run(filt_a, bank("filt", n)[0:64, :], ACT.Identity, scale=col("filt_sf", n, slice(0, 64)),
                bias=filt_sb[0:64, n:n + 1]).then_inc(*now.both(("filt_a", n), ("free", "filt", n)))
            act.wait_ge(*after("filt_r", n))
            run(filt_h, filt_a, ACT.Sin).then_inc(*now.did("filt_h", n))

        for t in range(12):
            if t >= 3:
                act.wait_ge(*after("hyT", t - 3))
            evacuate("hy", t, raw[:, t % 3, 1:L + 1], ACT.Copy, "hraw")
            act.wait_ge(*after("hraw", t))
            run(hyT[:, t, :], raw[:, t % 3, 1:L + 1], ACT.Identity, scale=col("hy_conv_w", 12 + t),
                bias=col("hy_conv_b", t)).then_inc(*now.did("hy0", t))
            if t in (5, 7, 9):
                filter_layer((t - 5) // 2)
        for c in range(TT):
            evacuate("hvt", c, xv_tok[:, c, :], ACT.Copy, "xv_tok")
        for c in range(TT):
            evacuate("hxt", c, x1_tok[:, c, :], ACT.Copy, "x1_tok")
        for o in range(2):
            for sd in range(2):
                for ft in range(TT):
                    act.wait_ge(*after("psum", "H", o, sd, ft))
                    run(Hcs[o][sd][:, ft, :], bank("H", o, sd, ft), ACT.Copy).then_inc(
                        *now.both(("H", o, sd, ft), ("free", "H", o, sd, ft)))

        now = act_in["ffn2"]
        for t in range(2 * DT):
            evacuate("gate", t, (gate_h if t < DT else gate_r)[:, t % DT, :], ACT.Sigmoid, "gate")
        for n in range(2):
            for t in range(DT):
                act.wait_ge(*after("lnc", n, t))
                run(lnsq[:, t, :], lnc[:, t, :], ACT.Square).then_inc(*now.did("lnsq%d" % n, t))
            act.wait_ge(*after("psum", "lv%d" % n))
            run(norm_s[:, 0, :], bank("lv%d" % n), ACT.Sqrt, scale=1.0 / D, bias=eps(1)).then_inc(
                *now.both(("ln_std2", n), ("free", "lv%d" % n)))
            for t in range(DT):
                act.wait_ge(*after("lnn", n, t))
                run(x2T[:, t, :], lnc[:, t, :], ACT.Identity, bias=col("ln%d_b" % (n + 1), t)).then_inc(
                    *now.did("x3T" if n == 0 else "out", t))
            if n == 0:
                for t in range(FT):
                    if t >= 4:
                        act.wait_ge(*after("gT2", t - 4))
                    evacuate("fg", t, silu_g[:, t % 4, :], ACT.Silu, "silu_g")

    @block.gpsimd
    def _(pool):

        def load(name, dst, src=None):
            pool.dma_start(dst, io[name] if src is None else src).then_inc(*loads[name].loaded(name))

        load("gla_w2", gla_w2)
        pool.wait_ge(*after("psum", "sc", 1, 3))
        pool.wait_ge(*after("psum", "kt", 1, 3))
        pool.wait_ge(*after("la", 1, 3))
        load("ln_g", ln_g, io["ln_g"].partition_broadcast(P))
        load("ln_b", ln_b, io["ln_b"].partition_broadcast(P))
        load("w_s", w_sT)
        load("b_s", b_s)
        pool.wait_ge(*after("psum", "ss3"))
        load("rw_small", at(2, 2 * L, 2048).rearrange("p (n c) -> p n c", n=2))
        pool.dma_start(rw_w2, io["rw_w2"]).then_inc(*loads["rw_small"].loaded("rw_w2"))
        load("w0", w0_row)
        last = len(JOBS) - 1
        pool.wait_ge(*after("y", last))
        pool.wait_ge(*after("gn_r", HT - 1))
        pool.wait_ge(*after("psum", "yv", HT - 1))
        for name, dst in (("featsT", featsT), ("fw1", fw1), ("fw2", fw23[0]), ("fw3", fw23[1]), ("fw4", fw4)):
            pool.dma_start(dst, io[name]).then_inc(*loads["filters"].loaded("filters"))
        load("skip", skip_row)
        load("window", window)
        pool.wait_ge(*after("hyT", 11))
        pool.wait_ge(*after("hy0", 11))
        pool.dma_start(at(0, U), io["dft"][0]).then_inc(*loads["dft"].loaded("dft"))
        pool.wait_ge(*after("psum", "hf", 1, 1, 3))
        pool.wait_ge(*after("skip_added", 1))
        pool.wait_ge(*after("fsd", 1, 1))
        pool.dma_start(at(6, U), io["dft"][1]).then_inc(*loads["dftT"].loaded("dftT"))

    @block.sync
    def _(sp):
        for n in range(NBLOCKS):
            if n == FIRST_BLOCK["hy_in"] + 1:
                sp.wait_ge(*after("psum", "gram", len(JOBS) - 1, 1, 1, 1))
            if n >= RING:
                sp.wait_ge(*after(*("psum",) + block_done[n - RING]))
            sp.dma_start(ring[:, n % RING, :], io["weights"][n]).then_inc(*slot_loaded[n % RING].loaded("block", n))
        for t in range(DT):
            sp.wait_ge(*after("out", t))
            sp.dma_start(io["out"][:, t, :], x2T[:, t, :]).then_inc(*out_stored.loaded("stored", t))
        sp.wait_ge(*after("stored", DT - 1))



def _constants():
    eye = np.eye(P, dtype=np.float32)
    i, j = np.arange(P)[:, None], np.arange(P)[None, :]
    head = (i // RH == j // RH).astype(np.float32)

    def cumulative(d, unit):
        at = np.arange(P + 1)[None, :]
        if d == 0:
            upto, first = (i < at).astype(np.float64), (i < P // 2).astype(np.float64)
        else:
            upto, first = (i >= at).astype(np.float64), (i >= P // 2).astype(np.float64)
        one = np.ones_like(first)
        return np.concatenate([upto - first, first, one, one - first], 1) * unit

    def level(d, m):
        a, b = (i, j) if d == 0 else (j, i)
        return ((a // (2 * m) == b // (2 * m)) & (a // m > b // m)) | (i == j)

    later = [(j >= i), (j <= i)]
    strict = [(j > i), (j < i)]
    parts = [eye, np.ones((P, P)), head]
    parts += [cumulative(d, 1.0 / 16.0) for d in range(2)]
    parts += [cumulative(d, DECAY) for d in range(2)]
    parts += later
    parts += [x for d in range(2) for x in (strict[d], later[d])]
    parts += [level(d, m) for d in range(2) for m in [1] + LEVELS]
    table = np.concatenate([np.asarray(x, np.float64) for x in parts], 1).astype(np.float32)
    assert table.shape == (P, NCONST)

    t, f = np.arange(L)[:, None], np.arange(L)[None, :]
    angle = 2.0 * np.pi * ((t * (2 * f + 1)) % (4 * L)) / (4.0 * L)
    cos, sin = np.cos(angle), np.sin(angle)

    def rows(a):
        return a.reshape(TT, P, L).transpose(1, 0, 2).reshape(P, TT * L)

    dft = np.stack([np.concatenate([rows(a) for a in m], 1) for m in ((cos, sin), (cos.T, sin.T))]).astype(np.float32)
    time = np.linspace(0.0, 1.0, L, dtype=np.float32)[:, None]
    w = (2.0 * math.pi * np.arange(L, dtype=np.float32) / L).astype(np.float32)
    bands = np.linspace(1e-4, 15, 16, dtype=np.float32)
    ang = (w[:, None] * bands[None, :]).astype(np.float32)
    feats = np.concatenate([time, np.cos(ang), -np.sin(ang)], 1).astype(np.float32)
    deltas = np.abs(np.linspace(math.log(1e-2) / 1.5, math.log(1e-2) / 0.3, HW, dtype=np.float32))
    window = np.exp(-time * deltas[None, :]).astype(np.float32)
    return table, dft, np.ascontiguousarray(feats.T), window.reshape(TT, P, HW).transpose(1, 0, 2)


def _blocks(w, width=BLK):
    k, n = w.shape
    kt = 2048 // width
    rows, colsn = -(-k // (kt * P)) * kt * P, -(-n // width) * width
    if (rows, colsn) != (k, n):
        padded = np.zeros((rows, colsn), w.dtype)
        padded[:k, :n] = w
        w = padded
    w = w.reshape(rows // (kt * P), kt, P, colsn // width, width)
    return w.transpose(3, 0, 2, 1, 4).reshape(-1, P, kt * width)


def kernel(**inputs):
    import concourse.bacc as bacc
    from concourse.bass_utils import run_bass_kernel_spmd

    a = {k: np.asarray(v) for k, v in inputs.items()}
    m = {k: (v[0] if v.shape[:1] == (1,) else v) for k, v in a.items()}

    offs = np.cumsum([0, 1024, 1024, 512, 1024, 1024, 1024, 512, 1024, 32])
    u, vs, q, r, ga, gb, k, v, lr = (m["w_in"][:, offs[i]:offs[i + 1]] for i in range(9))
    up, up2g, up2u = (_blocks(w) for w in (m["ffn_w_up"], m["ffn_w_gate_2"], m["ffn_w_up_2"]))
    half = FT // 2
    w_in2 = m["w_in_2"]
    streams = {
        "ada1": _blocks(m["w_ada"][:, :2048]), "ada2": _blocks(m["w_ada"][:, 2048:]),
        "k": _blocks(k), "v": _blocks(v), "lr": _blocks(lr), "q": _blocks(q), "r": _blocks(r), "gb": _blocks(gb),
        "br_b": _blocks(m["w_br_b"]), "ga": _blocks(ga), "vs": _blocks(vs), "u": _blocks(u),
        "br_a": _blocks(m["w_br_a"]), "w_o": _blocks(m["w_o"]),
        "up": np.stack([up[:half], up[half:]], 1).reshape(-1, P, 2048), "down": _blocks(m["ffn_w_down"]),
        "rw_in": _blocks(w_in2[:, 1536:3456])[list(RW_ORDER)], "hy_in": _blocks(w_in2[:, :1536]), "gates": _blocks(w_in2[:, 3456:]),
        "rw_out": _blocks(m["w_rw_out_2"], 2 * BLK), "hy_out": _blocks(m["w_hy_out_2"], 2 * BLK),
        "w_o2": _blocks(m["w_o_2"]), "up2": np.stack([up2g, up2u], 1).reshape(-1, P, 2048),
        "down2": _blocks(m["ffn_w_down_2"]),
    }
    assert all(len(streams[name]) == n for name, n in STREAM)
    weights = np.concatenate([streams[name] for name, _ in STREAM])

    def tile_columns(x, width=P):
        x = x.reshape(-1, width)
        return np.concatenate([x, np.zeros((len(x), P - width), x.dtype)], 1) if width < P else x

    source = {
        "c": m["c"], "c_ctx": a["c_ctx"], "b_ada": m["b_ada"], "norm1_g": m["norm1_g"], "norm2_g": m["norm2_g"],
        "gla_norm_g": m["gla_norm_g"], "final_norm_g": a["final_norm_g"], "conv_w": m["ffn_conv_w"],
        "conv_b": m["ffn_conv_b"], "hy_conv_w": m["hy_conv_w_2"], "hy_conv_b": m["hy_conv_b_2"],
        "rw_mu": m["rw_mu_2"], "a0": m["rw_a0_2"], "k_k": m["rw_k_k_2"], "k_a": m["rw_k_a_2"],
        "r_k": m["rw_r_k_2"], "gn_w": m["rw_gn_w_2"], "gn_b": m["rw_gn_b_2"], "ln1_w": m["ln1_w_2"],
        "ln1_b": m["ln1_b_2"], "ln2_w": m["ln2_w_2"], "ln2_b": m["ln2_b_2"],
        "filt_b": np.stack([m["hy_filt_b1_2"], m["hy_filt_b2_2"], m["hy_filt_b3_2"]]),
        "filt_sf": m["hy_sin_freq_2"],
    }
    table = np.concatenate([tile_columns(source[name], 64 if name.startswith("filt") else P) for name, _ in COLUMNS])
    consts, dft, featsT, window = _constants()

    def feature_major(x):
        return x.T.reshape(DT, P, -1).transpose(1, 0, 2)

    gla_w2 = np.zeros((33, 2, HW), np.float32)
    for d in range(2):
        gla_w2[d * RANK:(d + 1) * RANK, d] = m["gla_w2"][d]
        gla_w2[32, d] = m["gla_b2"][d]
    rw_w2 = np.zeros((P, 2, HW), np.float32)
    for d in range(2):
        rw_w2[d * 64:(d + 1) * 64, d] = m["rw_w2_2"][d]
    arrays = {
        "weights": weights, "cols": table.T, "consts": consts,
        "xT": feature_major(m["x"]), "ctxT": feature_major(m["ctx"]), "gla_w2": gla_w2,
        "ln_g": m["sgu_ln_g"], "ln_b": m["sgu_ln_b"], "w_s": m["sgu_w"].transpose(2, 0, 1),
        "b_s": m["sgu_b"].reshape(1, D),
        "rw_small": np.stack([m["rw_a2_2"].reshape(P, HW), m["rw_g2_2"]], 1), "rw_w2": rw_w2,
        "w0": m["rw_w0_2"].reshape(1, D), "featsT": featsT, "fw1": m["hy_filt_w1_2"], "fw2": m["hy_filt_w2_2"],
        "fw3": m["hy_filt_w3_2"], "fw4": m["hy_filt_w4_2"].reshape(64, 2, 2, HW), "skip": m["hy_skip_2"].reshape(1, D),
        "window": window, "dft": dft,
    }
    arrays = {f"{k}_dram": np.ascontiguousarray(x) for k, x in arrays.items()}

    def declare():
        nc = bacc.Bacc("TRN2", target_bir_lowering=False, num_devices=1)
        io = {k[:-5]: nc.dram_tensor(k, x.shape, F32, kind="ExternalInput").ap() for k, x in arrays.items()}
        io["out"] = nc.dram_tensor("out_dram", (P, DT, L), F32, kind="ExternalOutput").ap()
        return nc, io

    announced = build(*declare(), None)
    nc, io = declare()
    build(nc, io, announced)
    result = run_bass_kernel_spmd(nc, [arrays], core_ids=[0]).results[0]["out_dram"]
    return np.ascontiguousarray(result.transpose(1, 0, 2).reshape(D, L).T).reshape(1, L, D)
```

```python
import math
from contextlib import ExitStack

import numpy as np

import concourse.bass as bass
from concourse import mybir

F32 = mybir.dt.float32
ACT = mybir.ActivationFunctionType
ALU = mybir.AluOpType

P = 128
D = 1024
L = 512
LC = 256
DT = D // P
TT = L // P
TC = LC // P
HEADS = 4
DK, DV = 128, 256
RANK = 16
SGU_G = 8
FF = 2816
FT = FF // P
GRID = 64
ROWS = L // GRID
HW = 512
HT = HW // P
RH = 64
BLK = 256
RING = 3
BANKS = 8
EPS, LN_EPS, GN_EPS = 1e-6, 1e-5, 64e-5
ALPHA = 2.0 ** 0.25
DECAY = -math.exp(-0.5)
LEVELS = [2, 4, 8, 16, 32]
BIG = 1e30
U = 4096
CUM = P + 4

COLUMNS = [
    ("c", 8), ("c_ctx", 8), ("b_ada", 48), ("norm1_g", 8), ("norm2_g", 8), ("gla_norm_g", 8),
    ("final_norm_g", 8), ("conv_w", 9 * FT), ("conv_b", FT), ("hy_conv_w", 36), ("hy_conv_b", 12),
    ("rw_mu", 15), ("a0", 8), ("k_k", 4), ("k_a", 4), ("r_k", 4), ("gn_w", 4), ("gn_b", 4),
    ("ln1_w", 8), ("ln1_b", 8), ("ln2_w", 8), ("ln2_b", 8), ("filt_b", 3), ("filt_sf", 3),
]
COL = {}
for _name, _n in COLUMNS:
    COL[_name] = sum(n for _, n in COLUMNS[:len(COL)])
NCOL = sum(n for _, n in COLUMNS)

ADA_FIRST, ADA_REST = 8, 16
STREAM = [
    ("ada1", ADA_FIRST), ("lr", 1), ("k", 2), ("q", 2), ("v", 4), ("ada2", ADA_REST), ("r", 4), ("gb", 4),
    ("br_b", 4), ("ga", 4), ("vs", 4), ("u", 4), ("br_a", 4), ("w_o", 4), ("up", 22), ("down", 12),
    ("rw_in", 8), ("hy_in", 6), ("gates", 8), ("rw_out", 2), ("hy_out", 2), ("w_o2", 4), ("up2", 22), ("down2", 12),
]
BLOCK_ORDER, _rest = [], [("ada2", _i) for _i in range(ADA_REST)]
for _name, _n in STREAM:
    for _i in range(0 if _name == "ada2" else _n):
        BLOCK_ORDER.append((_name, _i))
        if _name != "ada1" and _rest:
            BLOCK_ORDER.append(_rest.pop(0))
POSITION = {_block: _n for _n, _block in enumerate(BLOCK_ORDER)}
NBLOCKS = sum(n for _, n in STREAM)

RW_ORDER = (6, 2, 3, 0, 1, 4, 5, 7)
RW_TILES = [t for _b in RW_ORDER for t in (2 * _b, 2 * _b + 1) if t < 15]

CONSTS = [
    ("ident", P), ("ones", P), ("headones", P), ("gla_cum", 2 * CUM), ("rw_cum", 2 * CUM), ("incl", 2 * P),
    ("pair_mask", 4 * P), ("level_mask", 2 * 6 * P),
]
CONST = {}
for _name, _n in CONSTS:
    CONST[_name] = sum(n for _, n in CONSTS[:len(CONST)])
NCONST = sum(n for _, n in CONSTS)


class Progress:

    def __init__(self, known):
        self.known = known
        self.found = {}
        self.signals = {}

    def stage(self, nc, ctx, name):
        self.signals[name] = Signal(self, name, ctx.enter_context(nc.semaphore(name)))
        return self.signals[name]

    def after(self, *what):
        name, count = self.known[what] if self.known is not None else (next(iter(self.signals)), 1)
        return self.signals[name].sem, count


class Signal:

    def __init__(self, progress, name, sem):
        self.progress, self.name, self.sem, self.count = progress, name, sem, 0

    def did(self, *what):
        self.count += 1
        if what:
            self.note(what)
        return self.sem, 1

    def both(self, *whats):
        self.count += 1
        for what in whats:
            self.note(what)
        return self.sem, 1

    def note(self, what):
        found = self.progress.found
        assert what not in found or what[0] in ("y", "rexp"), what
        found[what] = (self.name, self.count)

    def loaded(self, *what):
        self.count += 16
        self.progress.found[what] = (self.name, self.count)
        return self.sem, 16


def build(nc, io, known):
    progress = Progress(known)
    ctx = ExitStack()
    with ctx:
        _build(nc, io, progress, ctx)
    return progress.found


def _build(nc, io, progress, ctx):
    after = progress.after

    def sb(name, shape):
        return ctx.enter_context(nc.sbuf_tensor(name, shape, F32))

    cols = sb("cols", [P, NCOL])
    consts = sb("consts", [P, NCONST])
    ring = sb("ring", [P, RING, 8 * BLK])
    arena = sb("arena", [P, 10 * U])
    small = sb("small", [P, 1280])
    scratch = sb("scratch", [P, 8 * CUM])
    banks = ctx.enter_context(nc.psum_tensor("banks", [P, BANKS, 512], F32))

    def at(unit, size, offset=0):
        start = unit * U + offset
        return arena[:, start:start + size]

    def tiles(unit, n, width=L, offset=0):
        return at(unit, n * width, offset).rearrange("p (n t) -> p n t", n=n)

    def col(name, i=0, rows=slice(0, P)):
        return cols[rows, COL[name] + i:COL[name] + i + 1]

    def const(name, n, i=0):
        return consts[:, CONST[name] + i * n:CONST[name] + (i + 1) * n]

    ident, ones, headones = const("ident", P), const("ones", P), const("headones", P)
    gla_cum = [const("gla_cum", CUM, d) for d in range(2)]
    rw_cum = [const("rw_cum", CUM, d) for d in range(2)]
    incl = [const("incl", P, d) for d in range(2)]
    pair_mask = [const("pair_mask", 2 * P, d) for d in range(2)]
    level_mask = [[const("level_mask", P, 6 * d + i) for i in range(6)] for d in range(2)]

    csil = small[:, 0:16].rearrange("p (k n) -> p k n", n=2)
    mod = small[:, 16:80]
    modc = small[:, 80:96]
    gs1, gs1c, gs2 = small[:, 96:104], small[:, 104:112], small[:, 112:120]
    eps_cols = small[:, 120:124]
    bn = small[:, 124:124 + 48].rearrange("p (t h s) -> p t h s", t=4, h=2)
    mv = small[:, 172:180].rearrange("p (t s) -> p t s", t=4)
    ln_r = small[:, 180:184]
    stats_x = small[:, 184:184 + 96].rearrange("p (d h c s) -> p d h c s", d=2, h=4, c=4)
    stats_c = small[:, 280:280 + 48].rearrange("p (d h c s) -> p d h c s", d=2, h=4, c=2)
    mix_half, mix_one = small[:, 328:343], small[:, 343:358]
    half_ka, rest_ka, half_a0 = small[:, 358:362], small[:, 362:366], small[:, 366:374]
    filt_sb = small[:, 374:377]
    ones_row = small[0:1, 384:512]
    state = small[:, 512:640].rearrange("p (b v) -> p b v", b=2)
    state_t = small[:, 640:704]
    state_m = small[:, 1048:1176]
    ub = small[:, 768:896].rearrange("p (h v) -> p h v", h=2)
    sab = small[:, 896:1024].rearrange("p (h v) -> p h v", h=2)
    ada_sums = [small[:, 512 + BLK * i:512 + BLK * (i + 1)] for i in range(2)]
    job_stats = small[:, 1024:1048].rearrange("p (b c s) -> p b c s", b=2, c=4)

    psum_full = progress.stage(nc, ctx, "psum_full")
    slot_loaded = [progress.stage(nc, ctx, f"slot_loaded{i}") for i in range(RING)]
    names = ["start", "ada", "gla", "mix", "ffn", "rwkv", "hyena", "ffn2"]
    dve_in = {n: progress.stage(nc, ctx, f"dve_{n}") for n in names}
    act_in = {n: progress.stage(nc, ctx, f"act_{n}") for n in names}
    pool_in = {n: progress.stage(nc, ctx, f"pool_{n}") for n in names}
    loads = {n: progress.stage(nc, ctx, f"load_{n}") for n in
             ("cols", "consts", "masks", "x", "ctx", "gla_w2", "ln_g", "ln_b", "w_s", "b_s", "rw_small", "w0",
              "filters", "filters_out", "dft_first", "dft", "dftT", "window", "skip", "H0", "H1")}
    spectra_stored = [progress.stage(nc, ctx, f"spectra_stored{i}") for i in range(2)]
    out_stored = progress.stage(nc, ctx, "out_stored")

    xT = tiles(0, DT)
    hT = tiles(1, DT)
    ctxT = tiles(2, DT, LC, 0)
    hcT = tiles(2, DT, LC, 2048)
    sq, sqc = hT, hcT
    rstd = tiles(4, 2)
    kT, kcT = tiles(4, HEADS), tiles(4, HEADS, LC, 2048)
    lrT, lrcT = at(4, L, 3072)[0:33], at(4, LC, 3584)[0:33]
    v_tok = tiles(5, TT, D)
    vc_tok = tiles(6, TC, D)
    qT = tiles(6, HEADS, L, 2048)
    la = [tiles(7, TT, L, 2048 * d) for d in range(2)]
    lac = [tiles(3, TC, L, 1024 * d) for d in range(2)]
    gla_w2 = at(8, 1024)[0:33].rearrange("p (d n) -> p d n", d=2)
    soft = [at(9, L, 512 * i) for i in range(8)]
    q_dec = [tiles(8, HEADS, L, 2048 * d) for d in range(2)]
    k_inv = [tiles(9, HEADS, L, 2048 * d) for d in range(2)]
    kc_inv = [tiles(3, HEADS, LC, 2048 + 1024 * d) for d in range(2)]
    k_tok = [tiles(2, TT, L, 2048 * d) for d in range(2)]
    kc_tok = [tiles(3, TC, L, 1024 * d) for d in range(2)]
    s_gla = [at(6, DV, 2048 + 256 * i) for i in range(8)]
    sm = [[[at(7 if d == 0 else 4, DV, 256 * (4 * h + c)) for c in range(TT)] for h in range(HEADS)]
          for d in range(2)]
    sc = tiles(3, TT, L, 2048)
    oT = tiles(2, DT)
    osq = tiles(3, 4)
    silu_r = tiles(5, DT)
    sga, sgb = tiles(6, DT), tiles(7, DT)
    vs_tok = tiles(8, TT, D)
    guT = tiles(4, DT)
    ln_g, ln_b = at(9, D), at(9, D, 1024)
    w_sT = tiles(9, SGU_G, P, 2048)
    b_s = at(9, D, 3072)[0:1]
    gT = tiles(2, FT)
    pads = at(8, 4 * (ROWS + 2) * (GRID + 2)).rearrange("p (b y x) -> p b y x", b=4, y=ROWS + 2)
    acc = tiles(9, 4)
    sq5 = tiles(5, DT)
    exps = scratch[:, :].rearrange("p (k c j) -> p k c j", k=4, c=2)
    ada1_sums = [[scratch[:, BLK * (2 * n + i):BLK * (2 * n + i + 1)] for i in range(2)] for n in range(2)]
    work = [scratch[:, L * i:L * (i + 1)] for i in range(2)]
    rstd2 = tiles(9, 2, L, 2048)

    x2T = tiles(1, DT)
    raw = at(0, 3 * (L + 2), 2048).rearrange("p (b t) -> p b t", b=3)
    pair_sum = tiles(5, 2)
    rT, rkT = tiles(8, HT), tiles(8, HT, L, 2048)
    rvT = tiles(9, HT)
    wdT, adT, gdT = (at(9, L, 2048 + L * i) for i in range(3))
    mixed = [rT[:, i, :] for i in range(4)] + [rkT[:, i, :] for i in range(4)] + [rvT[:, i, :] for i in range(4)] + [wdT, adT, gdT]
    lw = [tiles(6, TT, L, 2048), tiles(0, TT)]
    rv_tok = tiles(7, TT)
    nkkT = tiles(7, HT, L, 2048)
    kk_sq, kk_n = (tiles(5, 2, L, 1024 * i) for i in (1, 2))
    w0_row = at(5, 2 * L, 3072)[0:1]
    yT = tiles(2, HT)
    rw_a2, rw_g2 = (at(2, L, 2048 + L * i) for i in range(2))
    rw_w2 = tiles(3, 2)
    job_t, kd_sum = at(2, L, 3584), at(9, L, 3584)
    sets = []
    for s in range(2):
        base = 7168 * s
        sets.append(dict(
            nqb=at(3, 2048, base).rearrange("p (s a t) -> p s a t", s=8, a=2),
            mqk=at(3, 2048, base + 2048).rearrange("p (s a t) -> p s a t", s=8, a=2),
            g=at(3, 1024, base + 4096).rearrange("p (s t) -> p s t", s=8),
            ar=at(3, 1024, base + 5120).rearrange("p (c a t) -> p c a t", c=4, a=2),
            b_tok=at(3, 512, base + 6144).rearrange("p (c f) -> p c f", c=4),
            k_tok=at(3, 512, base + 6656).rearrange("p (c f) -> p c f", c=4)))
    X, Y = (at(0, 1024, 2048 + 1024 * i).rearrange("p (s t) -> p s t", s=8) for i in range(2))
    job_slot = ring[:, POSITION["hy_in", 1] % RING, :].rearrange("p (n t) -> p n t", n=4)
    aT, kdT, bkT = job_slot[:, 0, :], job_slot[:, 1, :], job_slot[:, 2:4, :]
    y_sq, gn_s = tiles(3, HT), tiles(5, 2)
    zT = tiles(4, HT)
    hyT = tiles(3, 12)
    xv_tok, x1_tok = tiles(5, TT), tiles(5, TT, L, 2048)
    featsT = at(6, L)[0:33]
    fw1 = at(6, 64, 512)[0:33]
    fw23 = [at(6, 64, 576 + 64 * i)[0:64] for i in range(2)]
    fw4 = at(6, 2048, 704)[0:64].rearrange("p (o d n) -> p o d n", o=2, d=2)
    fsd = at(7, 2048)[0:64].rearrange("p (o d n) -> p o d n", o=2, d=2)
    filt_h, filt_k, filt_a = (at(7, L, 2048 + L * i)[0:64] for i in range(3))
    skip_row = at(6, 1024, 2816)[0:1]
    window = tiles(4, TT, L, 2048)
    ht = [[tiles((3, 8)[o], TT, L, 2048 * s) for s in range(2)] for o in range(2)]
    spectra = tiles(9, 8)
    dft_first = [tiles(5, TT), tiles(5, TT, L, 2048)]
    raw_h = at(8, 3 * (L + 2)).rearrange("p (b t) -> p b t", b=3)
    dft = [tiles(0, TT), tiles(0, TT, L, 2048)]
    dftT = [tiles(6, TT), tiles(6, TT, L, 2048)]
    Hcs = [[tiles((7, 3)[o], TT, L, 2048 * s) for s in range(2)] for o in range(2)]
    Ycs = [tiles(8, TT), tiles(8, TT, L, 2048)]
    prod = tiles(9, 8)
    gate_h, gate_r = tiles(0, DT), tiles(7, DT)
    lnc, lnsq = tiles(3, DT), tiles(4, DT)
    gT2 = tiles(3, FT)
    silu_g = tiles(6, 4)
    norm_s = tiles(9, 2)

    block = ctx.enter_context(nc.Block())
    bank_of, block_done = {}, {}
    bank_user = {}
    order = [(0, 1, 2, 3), (3, 2, 1, 0)]
    JOBS = [(hp, d) for hp in range(HT) for d in range(2)]
    LO, HI = slice(0, 64), slice(64, 128)

    def bank(*name):
        return banks[:, bank_of[name], :]

    @block.tensor
    def _(pe):
        taken = [0]

        def take(*name):
            b = taken[0] % BANKS
            taken[0] += 1
            if b in bank_user:
                pe.wait_ge(*after(*("free",) + bank_user[b]))
            bank_user[b] = name
            bank_of[name] = b
            return banks[:, b, :]

        def weights(name, i):
            n = POSITION[name, i]
            pe.wait_ge(*after("block", n))
            return ring[:, n % RING, :].rearrange("p (k c) -> p k c", c=BLK)

        def weights_done(name, i, *group):
            block_done[POSITION[name, i]] = ("psum",) + group

        def linear(name, b, rhs, rhs_ready, group, tiles_of=(0, 1), kt=DT):
            w = weights(name, b)
            for j in tiles_of:
                t = 2 * b + j
                ps = take(group, t)
                for k in range(kt):
                    pe.wait_ge(*after(rhs_ready, k))
                    mm = pe.matmul(ps, w[:, k, j * P:(j + 1) * P], rhs[:, k, :], start=k == 0, stop=k == kt - 1)
                mm.then_inc(*psum_full.did("psum", group, t))
            weights_done(name, b, group, t)

        def feature_sum(group, src, ready, weight, n=L, kt=DT):
            pe.wait_ge(*after("consts"))
            ps = take(group)
            for k in range(kt):
                pe.wait_ge(*after(ready, k))
                mm = pe.matmul(ps[:, 0:n], weight, src[:, k, :], start=k == 0, stop=k == kt - 1)
            mm.then_inc(*psum_full.did("psum", group))

        def filter_layer(n):
            fw, src = ((fw1, featsT), (fw23[0], filt_h), (fw23[1], filt_h))[n]
            ps = take("filt", n)
            pe.wait_ge(*after("filters"))
            if n:
                pe.wait_ge(*after("filt_h", n - 1))
            pe.matmul(ps[0:64, :], fw, src, start=True, stop=True).then_inc(*psum_full.did("psum", "filt", n))

        def filters(o):
            for sd in range(2):
                for tt in range(TT):
                    pe.wait_ge(*after("fsd", o, sd))
                    pe.wait_ge(*after("filt_h", 2))
                    ps = take("hf", o, sd, tt)
                    pe.matmul(ps, filt_h[:, tt * P:(tt + 1) * P], fsd[:, o, sd, :], start=True, stop=True).then_inc(
                        *psum_full.did("psum", "hf", o, sd, tt))

        def filter_spectrum(o, sd):
            pe.wait_ge(*after("dft_first"))
            for ft in range(TT):
                ps = take("H", o, sd, ft)
                for k in range(TT):
                    pe.wait_ge(*after("ht", o, sd, k))
                    mm = pe.matmul(ps, dft_first[sd][:, k, ft * P:(ft + 1) * P], ht[o][sd][:, k, :],
                                   start=k == 0, stop=k == TT - 1)
                mm.then_inc(*psum_full.did("psum", "H", o, sd, ft))
                if (ft == 1 and (o, sd) > (0, 0)) or ft == 3:
                    modulation("ada1", (4 * (2 * o + sd) + ft - 3) // 2, ada1_sums)

        def modulation(name, b, vectors):
            ps = take(name, b)
            for n, sums in enumerate(vectors):
                pe.wait_ge(*after(name + "_sums", b, n))
                for j in range(2):
                    mm = pe.matmul(ps[:, 2 * n + j:2 * n + j + 1], sums[b % 2][:, j * P:(j + 1) * P], ones[:, 0:1],
                                   start=True, stop=True)
            mm.then_inc(*psum_full.did("psum", name, b))

        filter_layer(0)
        feature_sum("ss_c", sqc, "sqc", ones, LC)
        filter_layer(1)
        feature_sum("ss_x", sq, "sq", ones)
        filter_layer(2)
        filters(0)
        filter_spectrum(0, 0)
        filters(1)
        filter_spectrum(0, 1)
        filter_spectrum(1, 0)
        filter_spectrum(1, 1)
        modulation("ada1", ADA_FIRST - 1, ada1_sums)

        pe.wait_ge(*after("masks"))
        ada2_next = [0]

        def later_modulation():
            b = ada2_next[0]
            ada2_next[0] += 1
            if 0 <= b - 1 < ADA_REST:
                modulation("ada2", b - 1, [ada_sums])

        def token_major(group, w, b, src, half):
            ps = take(group, b, half)
            for i in range(2):
                tt = 2 * half + i
                for k in range(DT):
                    mm = pe.matmul(ps[:, i * BLK:(i + 1) * BLK], src[:, k, tt * P:(tt + 1) * P], w[:, k, :],
                                   start=k == 0, stop=k == DT - 1)
            mm.then_inc(*psum_full.did("psum", group, b, half))

        def keys(b):
            w = weights("k", b)
            for j in range(2):
                t = 2 * b + j
                for group, src, n in (("kc", hcT, LC), ("k", hT, L)):
                    ps = take(group, t)
                    for k in range(DT):
                        mm = pe.matmul(ps[:, 0:n], w[:, k, j * P:(j + 1) * P], src[:, k, :],
                                       start=k == 0, stop=k == DT - 1)
                    mm.then_inc(*psum_full.did("psum", group, t))
            weights_done("k", b, "k", t)
            later_modulation()

        def values(b):
            w = weights("v", b)
            token_major("vc", w, b, hcT, 0)
            token_major("v", w, b, hT, 0)
            token_major("v", w, b, hT, 1)
            weights_done("v", b, "v", b, 1)
            later_modulation()

        def gates(group, d, low_rank, chunks):
            for tt in range(chunks):
                ps = take(group, d, tt)
                pe.matmul(ps, low_rank[:, tt * P:(tt + 1) * P], gla_w2[:, d, :], start=True, stop=True).then_inc(
                    *psum_full.did("psum", group, d, tt))

        def cumulate(group, log_decay, ready, d, cps):
            for h in range(HEADS):
                for cp in range(cps):
                    ps = take(group, d, h, cp)
                    for i in range(2):
                        c = 2 * cp + i
                        pe.wait_ge(*after(ready, d, c))
                        mm = pe.matmul(ps[:, i * CUM:(i + 1) * CUM], log_decay[d][:, c, h * P:(h + 1) * P],
                                       gla_cum[d], start=True, stop=True)
                    mm.then_inc(*psum_full.did("psum", group, d, h, cp))

        def key_tokens(group, src, ready, chunks):
            for d in range(2):
                for c in range(chunks):
                    ps = take(group, d, c)
                    for h in range(HEADS):
                        pe.wait_ge(*after(ready, d, h, c // 2))
                        mm = pe.transpose(ps[:, h * P:(h + 1) * P], src[d][:, h, c * P:(c + 1) * P], ident)
                    mm.then_inc(*psum_full.did("psum", group, d, c))

        def scores(c):
            for d in range(2):
                ps = take("sc", d, c)
                for h in range(HEADS):
                    pe.wait_ge(*after("k_inv", d, h, c // 2))
                    mm = pe.matmul(ps[:, h * P:(h + 1) * P], k_inv[d][:, h, c * P:(c + 1) * P],
                                   q_dec[d][:, h, c * P:(c + 1) * P], start=True, stop=True)
                mm.then_inc(*psum_full.did("psum", "sc", d, c))

        def added(step, hp):
            for d in range(2):
                if step < 2:
                    c = (step, 1 - step)[d]
                    keys, vals = kc_tok[d], vc_tok
                    pe.wait_ge(*after("kc_tok", d, c))
                    pe.wait_ge(*after("vc_tok", 2 * hp + 1))
                else:
                    c = order[d][step - 2]
                    keys, vals = k_tok[d], v_tok
                    pe.wait_ge(*after("k_tok", d, c))
                    pe.wait_ge(*after("v_tok", 2 * hp + 1))
                ps = take("su", step, d, hp)
                for i in range(2):
                    h = 2 * hp + i
                    mm = pe.matmul(ps[:, i * DV:(i + 1) * DV], keys[:, c, h * P:(h + 1) * P],
                                   vals[:, c, h * DV:(h + 1) * DV], start=True, stop=True)
                mm.then_inc(*psum_full.did("psum", "su", step, d, hp))

        w = weights("lr", 0)
        for group, src, ready, n in (("lrc", hcT, "hcT", LC), ("lr", hT, "hT", L)):
            ps = take(group)
            for k in range(DT):
                pe.wait_ge(*after(ready, k))
                mm = pe.matmul(ps[0:32, 0:n], w[:, k, 0:32], src[:, k, :], start=k == 0, stop=k == DT - 1)
            mm.then_inc(*psum_full.did("psum", group))
        weights_done("lr", 0, "lr")
        later_modulation()
        keys(0)
        pe.wait_ge(*after("gla_w2"))
        pe.wait_ge(*after("lrcT"))
        pe.wait_ge(*after("lrT"))
        pe.wait_ge(*after("lr_ones"))
        gates("zc", 0, lrcT, TC)
        gates("zc", 1, lrcT, TC)
        keys(1)
        gates("z", 0, lrT, TT)
        linear("q", 0, hT, "hT", "q")
        later_modulation()
        gates("z", 1, lrT, TT)
        linear("q", 1, hT, "hT", "q")
        later_modulation()
        for d in range(2):
            cumulate("cumc", lac, "lac", d, 1)
        values(0)
        cumulate("cum", la, "la", 0, 2)
        values(1)
        cumulate("cum", la, "la", 1, 2)
        values(2)
        key_tokens("ktc", kc_inv, "kc_inv", TC)
        scores(0)
        w = weights("v", 3)
        token_major("vc", w, 3, hcT, 0)
        key_tokens("kt", k_inv, "k_inv", TT)
        scores(1)
        for step in range(2):
            added(step, 0)
            added(step, 1)
        token_major("v", w, 3, hT, 0)
        added(2, 0)
        added(3, 0)
        scores(2)
        token_major("v", w, 3, hT, 1)
        weights_done("v", 3, "v", 3, 1)
        later_modulation()
        added(4, 0)
        added(2, 1)
        scores(3)
        added(3, 1)
        added(4, 1)

        def out_sum(h):
            ps = take("oss", h)
            for vt in range(2):
                pe.wait_ge(*after("osq", 2 * h + vt))
                mm = pe.matmul(ps, ones, osq[:, (2 * h + vt) % 4, :], start=vt == 0, stop=vt == 1)
            mm.then_inc(*psum_full.did("psum", "oss", h))

        for h in range(HEADS):
            for vt in range(2):
                ps = take("o", 2 * h + vt)
                vcols = slice(h * DV + vt * P, h * DV + (vt + 1) * P)
                for c in range(TT):
                    pe.wait_ge(*after("sc", c))
                    pe.wait_ge(*after("sm", 0, h, c))
                    pe.wait_ge(*after("sm", 1, h, c))
                    out = ps[:, c * P:(c + 1) * P]
                    pe.matmul(out, v_tok[:, c, vcols], sc[:, c, h * P:(h + 1) * P], start=True, stop=False)
                    for d in range(2):
                        mm = pe.matmul(out, sm[d][h][c][:, vt * P:(vt + 1) * P], q_dec[d][:, h, c * P:(c + 1) * P],
                                       start=False, stop=d == 1)
                mm.then_inc(*psum_full.did("psum", "o", 2 * h + vt))
            if h >= 1:
                out_sum(h - 1)
        for b in range(4):
            linear("r", b, hT, "hT", "r")
            later_modulation()
            if b == 0:
                out_sum(HEADS - 1)
        for b in range(4):
            linear("gb", b, hT, "hT", "gb")
            later_modulation()
        for b in range(4):
            linear("br_b", b, oT, "ob", "br_b")
        for b in range(4):
            linear("ga", b, hT, "hT", "ga")

        for b in range(4):
            w = weights("vs", b)
            token_major("vs", w, b, hT, 0)
            token_major("vs", w, b, hT, 1)
            weights_done("vs", b, "vs", b, 1)
        for b in range(4):
            linear("u", b, hT, "hT", "u")
        pe.wait_ge(*after("w_s"))
        pe.wait_ge(*after("b_s"))
        pe.wait_ge(*after("ones_row"))
        for g in range(SGU_G):
            ps = take("s", g)
            pe.matmul(ps, ones_row, b_s[:, g * P:(g + 1) * P].unsqueeze(1).to_broadcast([1, TT, P]), start=True,
                      stop=False)
            for n in range(TT):
                pe.wait_ge(*after("vn", n))
                mm = pe.matmul(ps[:, n * P:(n + 1) * P], vs_tok[:, n, g * P:(g + 1) * P], w_sT[:, g, :],
                               start=False, stop=n == TT - 1)
            mm.then_inc(*psum_full.did("psum", "s", g))
        for b in range(4):
            linear("br_a", b, guT, "aT", "br_a")
        for b in range(4):
            linear("w_o", b, sga, "merged", "w_o")

        feature_sum("ss2", sq5, "sq2", ones)
        for b in range(FT // 2):
            for group, base in (("fa", 0), ("fv", 1)):
                w = weights("up", 2 * b + base)
                for j in range(2):
                    ps = take(group, 2 * b + j)
                    for k in range(DT):
                        pe.wait_ge(*after("h2T", k))
                        mm = pe.matmul(ps, w[:, k, j * P:(j + 1) * P], hT[:, k, :], start=k == 0, stop=k == DT - 1)
                    mm.then_inc(*psum_full.did("psum", group, 2 * b + j))
                weights_done("up", 2 * b + base, group, 2 * b + 1)

        def down(name, group, src, ready):
            for b in range(4):
                ps = [take(group, 2 * b + j) for j in range(2)]
                for part in range(3):
                    w = weights(name, 3 * b + part)
                    kt = min(8, FT - 8 * part)
                    for j in range(2):
                        for k in range(kt):
                            pe.wait_ge(*after(ready, 8 * part + k))
                            mm = pe.matmul(ps[j], w[:, k, j * P:(j + 1) * P], src[:, 8 * part + k, :],
                                           start=part == 0 and k == 0, stop=part == 2 and k == kt - 1)
                        if part == 2:
                            mm.then_inc(*psum_full.did("psum", group, 2 * b + j))
                    if part < 2:
                        mm.then_inc(*psum_full.did("psum", group, "part", b, part))
                        weights_done(name, 3 * b + part, group, "part", b, part)
                weights_done(name, 3 * b + 2, group, 2 * b + 1)

        down("down", "down", gT, "gT")
        feature_sum("ss3", sq5, "sq3", ones)

        def key_norms(hps):
            for hp in hps:
                ps = take("kk", hp)
                pe.wait_ge(*after("kk_sq", hp))
                pe.matmul(ps, headones, kk_sq[:, hp % 2, :], start=True, stop=True).then_inc(
                    *psum_full.did("psum", "kk", hp))

        def rwkv_projection(i):
            b = RW_ORDER[i]
            w = weights("rw_in", i)
            for t in (2 * b, 2 * b + 1):
                if t < 15:
                    ps = take("rw", t)
                    for k in range(DT):
                        pe.wait_ge(*after("x2T", k))
                        mm = pe.matmul(ps, w[:, k, (t % 2) * P:(t % 2 + 1) * P], x2T[:, k, :],
                                       start=k == 0, stop=k == DT - 1)
                    mm.then_inc(*psum_full.did("psum", "rw", t))
                    last = t
                if t in (0, 1):
                    key_norms((2 * t, 2 * t + 1))
            weights_done("rw_in", i, "rw", last)
            if i in (2, 3):
                d = i - 2
                pe.wait_ge(*after("wd_tanh"))
                pe.wait_ge(*after("rw_w2"))
                pe.wait_ge(*after("w0"))
                for tt in range(TT):
                    ps = take("w", d, tt)
                    pe.matmul(ps, wdT[:, tt * P:(tt + 1) * P], rw_w2[:, d, :], start=True, stop=False)
                    pe.matmul(ps, ones_row, w0_row[:, d * L:(d + 1) * L], start=False, stop=True).then_inc(
                        *psum_full.did("psum", "w", d, tt))

        for i in range(7):
            rwkv_projection(i)

        def inputs(j):
            hp, d = JOBS[j]
            ps = take("a", j)
            rows = (LO, HI)[d]
            pe.wait_ge(*after("mixed", 13))
            pe.matmul(ps, rw_a2[rows, hp * P:(hp + 1) * P], adT[rows, :], start=True, stop=True).then_inc(
                *psum_full.did("psum", "a", j))
            for cp in range(2):
                ps = take("rcum", j, cp)
                for i in range(2):
                    c = 2 * cp + i
                    pe.wait_ge(*after("lw", d, c))
                    mm = pe.matmul(ps[:, i * CUM:(i + 1) * CUM], lw[d][:, c, hp * P:(hp + 1) * P], rw_cum[d],
                                   start=True, stop=True)
                mm.then_inc(*psum_full.did("psum", "rcum", j, cp))

        def tokens(j):
            for what, i in (("job_b", 0), ("job_k", 1)):
                ps = take("tok", j, i)
                pe.wait_ge(*after(what, j))
                for c in range(TT):
                    mm = pe.transpose(ps[:, c * P:(c + 1) * P], bkT[:, i, c * P:(c + 1) * P], ident)
                mm.then_inc(*psum_full.did("psum", "tok", j, i))

        def gram(j, i, cp):
            s = sets[j % 2]
            pe.wait_ge(*after("job_a", j))
            pe.wait_ge(*after("job_r", j))
            for h in range(2):
                ps = take("gram", j, i, cp, h)
                rows = (LO, HI)[h]
                for n in range(2):
                    c = 2 * cp + n
                    mm = pe.matmul(ps[:, n * 2 * P:(n + 1) * 2 * P], bkT[rows, i, c * P:(c + 1) * P],
                                   s["ar"][rows, c, :, :], start=True, stop=True)
                mm.then_inc(*psum_full.did("psum", "gram", j, i, cp, h))

        def bonus(j):
            hp, d = JOBS[j]
            if d == 1:
                ps = take("bonus", hp)
                pe.wait_ge(*after("bonus_in", hp))
                pe.matmul(ps, headones, kd_sum, start=True, stop=True).then_inc(*psum_full.did("psum", "bonus", hp))

        def inverse_start(j, half):
            ps = take("x0", j, half)
            pe.wait_ge(*after("g0", j))
            for i in range(4):
                mm = pe.transpose(ps[:, i * P:(i + 1) * P], sets[j % 2]["g"][:, 4 * half + i, :], ident)
            mm.then_inc(*psum_full.did("psum", "x0", j, half))

        def invert_y(j, lv, half):
            s = sets[j % 2]
            ps = take("iy", j, lv, half)
            pe.wait_ge(*after("x", j, lv, half))
            pe.wait_ge(*after("lt", j))
            for i in range(4):
                n = 4 * half + i
                mm = pe.matmul(ps[:, i * P:(i + 1) * P], s["nqb"][:, n, 0, :], X[:, n, :], start=True, stop=True)
            mm.then_inc(*psum_full.did("psum", "iy", j, lv, half))

        def invert_xg(j, lv, half):
            s = sets[j % 2]
            pe.wait_ge(*after("yi", j, lv, half))
            pe.wait_ge(*after(*(("g", j, lv, half) if lv else ("g0", j))))
            for what in ("ix", "ig"):
                ps = take(what, j, lv, half)
                for i in range(4):
                    n = 4 * half + i
                    out = ps[:, i * P:(i + 1) * P]
                    if what == "ix":
                        mm = pe.matmul(out, s["g"][:, n, :], Y[:, n, :], start=True, stop=True)
                    else:
                        mm = pe.matmul(out, Y[:, n, :], s["g"][:, n, :], start=True, stop=True)
                mm.then_inc(*psum_full.did("psum", what, j, lv, half))

        def invert_last(j, stage):
            s = sets[j % 2]
            d = JOBS[j][1]
            first, second = (LO, HI) if d == 0 else (HI, LO)
            ps = take("il", j, stage)
            if stage == 0:
                pe.wait_ge(*after("x", j, 5, 0))
                pe.wait_ge(*after("x", j, 5, 1))
                for n in range(8):
                    mm = pe.matmul(ps[second, n * 64:(n + 1) * 64], s["nqb"][first, n, 0, second],
                                   X[first, n, first], start=True, stop=True)
            else:
                pe.wait_ge(*after("y_last", j))
                pe.wait_ge(*after("g", j, 5, 0))
                pe.wait_ge(*after("g", j, 5, 1))
                for n in range(8):
                    mm = pe.matmul(ps[first, n * 64:(n + 1) * 64], Y[second, n, first], s["g"][second, n, second],
                                   start=True, stop=True)
            mm.then_inc(*psum_full.did("psum", "il", j, stage))

        def chain_u(j, step):
            hp, d = JOBS[j]
            s = sets[j % 2]
            c = order[d][step]
            pe.wait_ge(*after("rv_tok", c))
            ps = take("cu", j, step)
            for h in range(2):
                out = ps[:, h * 64:(h + 1) * 64]
                mm = pe.matmul(out, s["mqk"][:, 2 * c + h, 0, :], rv_tok[:, c, hp * P + h * 64:hp * P + (h + 1) * 64],
                               start=step == 0 or h == 0, stop=step == 0)
            if step:
                pe.wait_ge(*after("state_m", j, step))
                mm = pe.matmul(ps[:, 0:P], s["ar"][:, c, 0, :], state_m, start=False, stop=True)
            mm.then_inc(*psum_full.did("psum", "cu", j, step))

        def chain_sa(j, step):
            s = sets[j % 2]
            c = order[JOBS[j][1]][step]
            pe.wait_ge(*after("u", j, step))
            pe.wait_ge(*after("g_done", j))
            ps = take("cs", j, step)
            for h in range(2):
                mm = pe.matmul(ps[:, h * 64:(h + 1) * 64], s["g"][:, 2 * c + h, :], ub[:, h, :], start=True, stop=True)
            mm.then_inc(*psum_full.did("psum", "cs", j, step))

        def chain_out(j, step):
            hp, d = JOBS[j]
            s = sets[j % 2]
            c = order[d][step]
            pe.wait_ge(*after("sa", j, step))
            if step < 3:
                ps = take("ch", j, step)
                for h in range(2):
                    rows = (LO, HI)[h]
                    pe.matmul(ps[rows, 0:64], s["b_tok"][:, c, rows], sab[:, h, :], start=True, stop=False)
                    mm = pe.matmul(ps[rows, 0:64], s["k_tok"][:, c, rows],
                                   rv_tok[:, c, hp * P + h * 64:hp * P + (h + 1) * 64], start=False, stop=True)
                mm.then_inc(*psum_full.did("psum", "ch", j, step))
            ps = take("cy", j, step)
            for h in range(2):
                rows = (LO, HI)[h]
                out = ps[rows, 0:P]
                pe.matmul(out, sab[:, h, :], s["nqb"][:, 2 * c + h, 1, :], start=True, stop=False)
                mm = pe.matmul(out, rv_tok[:, c, hp * P + h * 64:hp * P + (h + 1) * 64],
                               s["mqk"][:, 2 * c + h, 1, :], start=False, stop=step == 0)
            if step:
                mm = pe.matmul(ps[:, 0:P], state_m, s["ar"][:, c, 1, :], start=False, stop=True)
            mm.then_inc(*psum_full.did("psum", "cy", j, step))

        inputs(0)
        rwkv_projection(7)
        for c in range(TT):
            ps = take("vt", c)
            for hp in range(HT):
                pe.wait_ge(*after("mixed", 8 + hp))
                mm = pe.transpose(ps[:, hp * P:(hp + 1) * P], rvT[:, hp, c * P:(c + 1) * P], ident)
            mm.then_inc(*psum_full.did("psum", "vt", c))
        tokens(0)
        gram(0, 0, 0)
        gram(0, 0, 1)
        for j in range(len(JOBS) + 1):
            new, old, ahead = j < len(JOBS), j > 0, j + 1 < len(JOBS)
            if old:
                chain_u(j - 1, 0)
            if new:
                gram(j, 1, 0)
            if old:
                chain_sa(j - 1, 0)
            if new:
                gram(j, 1, 1)
                inverse_start(j, 0)
                bonus(j)
                inverse_start(j, 1)
            if old:
                chain_out(j - 1, 0)
            if ahead:
                inputs(j + 1)
            for lv in range(5):
                chained = old and lv < 3
                if new:
                    for half in range(2):
                        invert_y(j, lv, half)
                if chained:
                    chain_u(j - 1, lv + 1)
                if new:
                    invert_xg(j, lv, 0)
                if chained:
                    chain_sa(j - 1, lv + 1)
                if new:
                    invert_xg(j, lv, 1)
                if chained:
                    chain_out(j - 1, lv + 1)
            if new:
                invert_last(j, 0)
            if ahead:
                tokens(j + 1)
                gram(j + 1, 0, 0)
            if new:
                invert_last(j, 1)
            if ahead:
                gram(j + 1, 0, 1)

        for hp in range(HT):
            ps = take("ym", hp)
            pe.wait_ge(*after("y", 2 * hp + 1))
            pe.matmul(ps, headones, yT[:, hp, :], start=True, stop=True).then_inc(*psum_full.did("psum", "ym", hp))
        for hp in range(HT):
            ps = take("yv", hp)
            pe.wait_ge(*after("y_sq", hp))
            pe.matmul(ps, headones, y_sq[:, hp, :], start=True, stop=True).then_inc(*psum_full.did("psum", "yv", hp))
        pe.wait_ge(*after("gd_sig"))
        for hp in range(HT):
            ps = take("g", hp)
            pe.matmul(ps, rw_g2[:, hp * P:(hp + 1) * P], gdT, start=True, stop=True).then_inc(
                *psum_full.did("psum", "g", hp))

        for b in range(6):
            linear("hy_in", b, x2T, "x2T", "hy")
        for what, dst in (("hvt", 0), ("hxt", 4)):
            for c in range(TT):
                ps = take(what, c)
                for i in range(HT):
                    pe.wait_ge(*after("hyT", dst + i))
                    mm = pe.transpose(ps[:, i * P:(i + 1) * P], hyT[:, dst + i, c * P:(c + 1) * P], ident)
                mm.then_inc(*psum_full.did("psum", what, c))
        pe.wait_ge(*after("dft"))
        for o in range(2):
            z, ready = xv_tok, (lambda k: ("xv_tok", k)) if o == 0 else (lambda k: ("z2", k))
            for ft in range(TT):
                for cs in range(2):
                    ps = take("Z", o, cs, ft)
                    for k in range(TT):
                        pe.wait_ge(*after(*ready(k)))
                        mm = pe.matmul(ps, dft[cs][:, k, ft * P:(ft + 1) * P], z[:, k, :], start=k == 0, stop=k == TT - 1)
                    mm.then_inc(*psum_full.did("psum", "Z", o, cs, ft))
            pe.wait_ge(*after("dftT"))
            for tt in range(TT):
                ps = take("conv", o, tt)
                for cs in range(2):
                    for k in range(TT):
                        pe.wait_ge(*after("Y", o, cs, k))
                        if o == 0:
                            a, b = dftT[cs][:, k, tt * P:(tt + 1) * P], Ycs[cs][:, k, :]
                        else:
                            a, b = Ycs[cs][:, k, tt * P:(tt + 1) * P], dftT[cs][:, k, :]
                        mm = pe.matmul(ps, a, b, start=cs == 0 and k == 0, stop=cs == 1 and k == TT - 1)
                mm.then_inc(*psum_full.did("psum", "conv", o, tt))

        for b in range(8):
            linear("gates", b, x2T, "x2T", "gate")

        def half_width(name, group, src, ready):
            for b in range(2):
                n = POSITION[name, b]
                pe.wait_ge(*after("block", n))
                w = ring[:, n % RING, :].rearrange("p (k c) -> p k c", c=2 * BLK)
                for j in range(4):
                    ps = take(group, 4 * b + j)
                    for k in range(HT):
                        pe.wait_ge(*after(ready, k))
                        mm = pe.matmul(ps, w[:, k, j * P:(j + 1) * P], src[:, k, :], start=k == 0, stop=k == HT - 1)
                    mm.then_inc(*psum_full.did("psum", group, 4 * b + j))
                weights_done(name, b, group, 4 * b + j)

        half_width("rw_out", "rwo", yT, "yT")
        half_width("hy_out", "hyo", zT, "zT")
        for b in range(4):
            linear("w_o2", b, gate_h, "merged2", "w_o2")
        feature_sum("lm0", x2T, "res0", ones)
        feature_sum("lv0", lnsq, "lnsq0", ones)
        for b in range(FT // 2):
            for group, base in (("fg", 0), ("fu", 1)):
                w = weights("up2", 2 * b + base)
                for j in range(2):
                    ps = take(group, 2 * b + j)
                    for k in range(DT):
                        pe.wait_ge(*after("x3T", k))
                        mm = pe.matmul(ps, w[:, k, j * P:(j + 1) * P], x2T[:, k, :], start=k == 0, stop=k == DT - 1)
                    mm.then_inc(*psum_full.did("psum", group, 2 * b + j))
                weights_done("up2", 2 * b + base, group, 2 * b + 1)
        down("down2", "down2", gT2, "gT2")
        feature_sum("lm1", x2T, "res1", ones)
        feature_sum("lv1", lnsq, "lnsq1", ones)

    @block.vector
    def _(dve):
        V = nc.vector

        def mul(out, a, b):
            return V.tensor_tensor(out, a, b, ALU.mult)

        def stt(out, a, scalar, b, op0, op1):
            return V.scalar_tensor_tensor(out, a, scalar, b, op0, op1)

        def gate_values(t):
            dve.wait_ge(*after("gelu", t))
            dve.wait_ge(*after("psum", "fv", t))
            mul(gT[:, t, :], bank("fv", t), acc[:, t % 4, :]).then_inc(*now.both(("gT", t), ("free", "fv", t)))

        now = dve_in["start"]
        V.memset(eps_cols[:, 0:1], EPS).then_inc(*now.did())
        V.memset(eps_cols[:, 1:2], LN_EPS).then_inc(*now.did())
        V.memset(eps_cols[:, 2:3], GN_EPS).then_inc(*now.did())
        V.memset(eps_cols[:, 3:4], 1.0).then_inc(*now.did())
        V.memset(ones_row, 1.0).then_inc(*now.both(("eps",), ("ones_row",)))
        dve.wait_ge(*after("cols"))
        dve.wait_ge(*after("cols"))
        mul(filt_sb[0:64, :], cols[0:64, COL["filt_b"]:COL["filt_b"] + 3],
            cols[0:64, COL["filt_sf"]:COL["filt_sf"] + 3]).then_inc(*now.did("filt_sb"))
        turn = 2.0 * math.pi
        parts = [6.28125, 0.0019340515136718750, turn - 6.28125 - 0.0019340515136718750]
        magic = 1.5 * 2.0 ** 23

        def sine_argument(n):
            dve.wait_ge(now.sem, now.count)
            dve.wait_ge(*after("filt_a", n))
            V.tensor_scalar(filt_k, filt_a, 1.0 / turn, magic, ALU.mult, ALU.add).then_inc(*now.did("fk", n))
            dve.wait_ge(*after("fk", n))
            V.tensor_scalar(filt_k, filt_k, -magic, None, ALU.add).then_inc(*now.did("fr", n, -1))
            dve.wait_ge(*after("fr", n, -1))
            for i, part in enumerate(parts):
                stt(filt_a, filt_k, -part, filt_a, ALU.mult, ALU.add).then_inc(*now.did("fr", n, i))
                dve.wait_ge(*after("fr", n, i))
            V.tensor_scalar(filt_a, filt_a, 3.1415925, -3.1415925, ALU.min, ALU.max).then_inc(*now.did("filt_r", n))

        def filters(o):
            for sd in range(2):
                for tt in range(TT):
                    dve.wait_ge(*after("psum", "hf", o, sd, tt))
                    dve.wait_ge(*after("window"))
                    mul(ht[o][sd][:, tt, :], bank("hf", o, sd, tt), window[:, tt, :]).then_inc(
                        *now.both(("ht0" if (sd, tt) == (0, 0) else "ht", o, sd, tt), ("free", "hf", o, sd, tt)))
                    if (sd, tt) == (0, 0):
                        dve.wait_ge(*after("ht0", o, 0, 0))
                        dve.wait_ge(*after("skip"))
                        first = ht[o][0][0:1, 0, :]
                        V.tensor_tensor(first, first, skip_row[:, o * HW:(o + 1) * HW], ALU.add).then_inc(
                            *now.both(("ht", o, 0, 0), ("skip_added", o)))

        def inverse_rms(which, i, n):
            dve.wait_ge(*after("rms", which))
            V.reciprocal(rstd[:, i, 0:n], rstd[:, i, 0:n]).then_inc(*now.did("rstd", which))

        def modulation_sums(name, b, vectors):
            n = POSITION[name, b]
            w = ring[:, n % RING, :].rearrange("p (k c) -> p k c", c=BLK)
            dve.wait_ge(*after("block", n))
            dve.wait_ge(*after("csil"))
            for k in range(DT):
                for i, sums in enumerate(vectors):
                    out = sums[b % 2]
                    if k:
                        dve.wait_ge(*after(name + "_part", b, i, k - 1))
                        stt(out, w[:, k, :], csil[:, k, i:i + 1], out, ALU.mult, ALU.add).then_inc(
                            *now.did(*(name + "_sums", b, i) if k == DT - 1 else (name + "_part", b, i, k)))
                    else:
                        V.tensor_scalar(out, w[:, k, :], csil[:, k, i:i + 1], None, ALU.mult).then_inc(
                            *now.did(name + "_part", b, i, k))
            block_done[n] = (name + "_sums", b, len(vectors) - 1)

        def modulation_columns(name, b, outs, first):
            dve.wait_ge(*after("psum", name, b))
            t = 2 * b
            for i, (out, what) in enumerate(outs):
                V.tensor_tensor(out[:, first + t:first + t + 2], bank(name, b)[:, 2 * i:2 * i + 2],
                                cols[:, COL["b_ada"] + first + t:COL["b_ada"] + first + t + 2], ALU.add).then_inc(
                    *now.both((what, b), *([("free", name, b)] if i == len(outs) - 1 else [])))

        sine_argument(0)
        dve.wait_ge(*after("filters_out"))
        for o in range(2):
            V.tensor_tensor(fsd[:, o, 0, :], fw4[:, o, 0, :], fw4[:, o, 1, :], ALU.add).then_inc(
                *now.did("fsd", o, 0))
            V.tensor_tensor(fsd[:, o, 1, :], fw4[:, o, 0, :], fw4[:, o, 1, :], ALU.subtract).then_inc(
                *now.did("fsd", o, 1))
        sine_argument(1)
        sine_argument(2)
        filters(0)
        modulation_sums("ada1", 0, ada1_sums)
        modulation_sums("ada1", 1, ada1_sums)
        modulation_columns("ada1", 0, ((mod, "mod"), (modc, "modc")), 0)
        filters(1)
        dve.wait_ge(now.sem, now.count)
        V.memset(lrcT[32:33, :], 1.0).then_inc(*now.did())
        V.memset(lrT[32:33, :], 1.0).then_inc(*now.did("lr_ones"))
        for b in range(2, ADA_FIRST):
            if b > 2:
                modulation_columns("ada1", b - 2, ((mod, "mod"), (modc, "modc")), 0)
            modulation_sums("ada1", b, ada1_sums)
            if b == 4:
                inverse_rms("c", 1, LC)
                inverse_rms("x", 0, L)
        for b in (ADA_FIRST - 2, ADA_FIRST - 1):
            modulation_columns("ada1", b, ((mod, "mod"), (modc, "modc")), 0)
        g1 = cols[:, COL["norm1_g"]:COL["norm1_g"] + 8]
        dve.wait_ge(*after("modc", ADA_FIRST - 1))
        stt(gs1c, modc[:, 8:16], 1.0, g1, ALU.add, ALU.mult).then_inc(*now.did("gs1c"))
        stt(gs1, mod[:, 8:16], 1.0, g1, ALU.add, ALU.mult).then_inc(*now.did("gs1"))
        dve.wait_ge(*after("gs1c"))
        dve.wait_ge(*after("rstd", "c"))
        dve.wait_ge(*after("ctx"))
        for k in range(DT):
            stt(hcT[:, k, :], ctxT[:, k, :], gs1c[:, k:k + 1], rstd[:, 1, 0:LC], ALU.mult, ALU.mult).then_inc(
                *now.did("hcT_scaled", k))
        dve.wait_ge(*after("gs1"))
        dve.wait_ge(*after("rstd", "x"))
        dve.wait_ge(*after("x"))
        for k in range(DT):
            stt(hT[:, k, :], xT[:, k, :], gs1[:, k:k + 1], rstd[:, 0, :], ALU.mult, ALU.mult).then_inc(
                *now.did("hT_scaled", k))

        def later_modulation(b):
            modulation_sums("ada2", b, [ada_sums])
            if b:
                modulation_columns("ada2", b - 1, ((mod, "mod2"),), 16)

        now = dve_in["gla"]
        def log_sigmoid(group, out, d, chunks, first):
            for tt in range(chunks):
                dve.wait_ge(*after("soft", group, d, tt))
                stt(out[d][:, tt, :], bank(group, d, tt), 0.0, soft[(first + tt) % 8], ALU.min, ALU.subtract).then_inc(
                    *now.both(("la" if group == "z" else "lac", d, tt), ("free", group, d, tt)))

        exp_count = [0]

        def decayed(group, d, cps):
            inc = slice(1, P + 1) if d == 0 else slice(0, P)
            for h in range(HEADS):
                for cp in range(cps):
                    e = exp_count[0]
                    exp_count[0] += 1
                    plus, minus = exps[:, e % 2], exps[:, 2 + e % 2]
                    dve.wait_ge(*after("exp", group, d, h, cp))
                    st = stats_c if group == "cumc" else stats_x
                    V.tensor_copy(st[:, d, h, 2 * cp:2 * cp + 2, :], plus[:, :, P + 1:CUM]).then_inc(
                        *now.did("stats", group, d, h, cp))
                    span = slice(2 * cp * P, 2 * (cp + 1) * P)
                    src, dst = (kcT, kc_inv) if group == "cumc" else (kT, k_inv)
                    dve.wait_ge(*after("kcT" if group == "cumc" else "kT", h))
                    if group == "cum":
                        dve.wait_ge(*after("qT", h))
                        mul(q_dec[d][:, h, span].rearrange("p (c t) -> p c t", c=2),
                            qT[:, h, span].rearrange("p (c t) -> p c t", c=2), plus[:, :, inc]).then_inc(
                            *now.did("q_dec", d, h, cp))
                    mul(dst[d][:, h, span].rearrange("p (c t) -> p c t", c=2),
                        src[:, h, span].rearrange("p (c t) -> p c t", c=2), minus[:, :, 0:P]).then_inc(
                        *now.both(("kc_inv" if group == "cumc" else "k_inv", d, h, cp), ("exp_used", e)))

        def states(step, hp):
            for d in range(2):
                if step < 2:
                    c, st, group = (step, 1 - step)[d], stats_c, "cumc"
                else:
                    c, st, group = order[d][step - 2], stats_x, "cum"
                dve.wait_ge(*after("psum", "su", step, d, hp))
                ps = bank("su", step, d, hp)
                for i in range(2):
                    h = 2 * hp + i
                    s = s_gla[4 * d + h]
                    add = ps[:, i * DV:(i + 1) * DV]
                    freed = [("free", "su", step, d, hp)] if i else []
                    dve.wait_ge(*after("stats", group, d, h, c // 2))
                    if step == 0:
                        V.tensor_scalar(s, add, st[:, d, h, c, 2:3], None, ALU.mult).then_inc(
                            *now.both(("s", step, d, h), *freed))
                    else:
                        if step >= 2:
                            dve.wait_ge(*after("sm", d, h, order[d][step - 2]))
                        t = work[0][:, i * DV:(i + 1) * DV]
                        dve.wait_ge(now.sem, now.count)
                        V.tensor_scalar(t, add, st[:, d, h, c, 2:3], None, ALU.mult).then_inc(
                            *now.both(("s_add", step, d, h), *freed))
                        dve.wait_ge(*after("s_add", step, d, h))
                        stt(s, s, st[:, d, h, c, 1:2], t, ALU.mult, ALU.add).then_inc(*now.did("s", step, d, h))

        def scores(c):
            for d in range(2):
                dve.wait_ge(now.sem, now.count)
                dve.wait_ge(*after("psum", "sc", d, c))
                V.tensor_scalar(work[0], bank("sc", d, c), BIG, -BIG, ALU.min, ALU.max).then_inc(
                    *now.both(("clamped", d, c), ("free", "sc", d, c)))
                dve.wait_ge(*after("clamped", d, c))
                out = sc[:, c, :] if d == 0 else work[1]
                mul(out.rearrange("p (h t) -> p h t", h=4), work[0].rearrange("p (h t) -> p h t", h=4),
                    incl[d].unsqueeze(1).to_broadcast([P, 4, P])).then_inc(*now.did("masked", d, c))
                dve.wait_ge(*after("masked", d, c))
            V.tensor_tensor(sc[:, c, :], sc[:, c, :], work[1], ALU.add).then_inc(*now.did("sc", c))
            dve.wait_ge(*after("sc", c))

        later_modulation(0)
        later_modulation(1)
        log_sigmoid("zc", lac, 0, TC, 0)
        log_sigmoid("zc", lac, 1, TC, 2)
        later_modulation(2)
        log_sigmoid("z", la, 0, TT, 4)
        later_modulation(3)
        log_sigmoid("z", la, 1, TT, 8)
        later_modulation(4)
        for d in range(2):
            decayed("cumc", d, 1)
        later_modulation(5)
        decayed("cum", 0, 2)
        later_modulation(6)
        decayed("cum", 1, 2)
        later_modulation(7)
        scores(0)
        scores(1)
        for step in range(2):
            states(step, 0)
            states(step, 1)
        states(2, 0)
        states(3, 0)
        scores(2)
        states(4, 0)
        states(2, 1)
        scores(3)
        modulation_columns("ada2", 7, ((mod, "mod2"),), 16)
        states(3, 1)
        states(4, 1)
        modulation_sums("ada2", 8, [ada_sums])
        for h in range(HEADS):
            dve.wait_ge(*after("o_rms", h))
            r = work[h % 2]
            V.reciprocal(r, r).then_inc(*now.did("o_rstd", h))
            dve.wait_ge(*after("o_rstd", h))
            for vt in range(2):
                t = 2 * h + vt
                dve.wait_ge(*after("oT", t))
                stt(oT[:, t, :], oT[:, t, :], col("gla_norm_g", t), r, ALU.mult, ALU.mult).then_inc(
                    *now.did("o_normed", t))

        now = dve_in["mix"]
        for t in range(DT):
            dve.wait_ge(*after("silu_r", t))
            dve.wait_ge(*after("o_normed", t))
            mul(oT[:, t, :], oT[:, t, :], silu_r[:, t, :]).then_inc(*now.did("ob", t))
            if t % 2 and t >= 1:
                later_modulation(9 + t // 2)
        for b in range(13, ADA_REST):
            later_modulation(b)
        modulation_columns("ada2", ADA_REST - 1, ((mod, "mod2"),), 16)
        dve.wait_ge(*after("mod2", ADA_REST - 1))
        stt(gs2, mod[:, 32:40], 1.0, cols[:, COL["norm2_g"]:COL["norm2_g"] + 8], ALU.add, ALU.mult).then_inc(
            *now.did("gs2"))
        for t in range(DT):
            dve.wait_ge(*after("psum", "br_b", t))
            dve.wait_ge(*after("sgb", t))
            mul(sgb[:, t, :], bank("br_b", t), sgb[:, t, :]).then_inc(*now.both(("mb", t), ("free", "br_b", t)))
        for n in range(TT):
            for b in range(4):
                dve.wait_ge(*after("vs", b, n // 2))
            for half in range(2):
                V.bn_stats(bn[:, n, half, :], vs_tok[:, n, half * 512:(half + 1) * 512]).then_inc(
                    *now.did("bn", n, half))
            dve.wait_ge(*after("bn", n, 1))
            V.bn_aggr(mv[:, n, :], bn[:, n, :, :].rearrange("p h s -> p (h s)")).then_inc(*now.did("mv", n))
        dve.wait_ge(*after("ln_std"))
        V.reciprocal(ln_r, ln_r).then_inc(*now.did("ln_r"))
        dve.wait_ge(*after("ln_r"))
        dve.wait_ge(*after("ln_g"))
        dve.wait_ge(*after("ln_b"))
        for n in range(TT):
            V.tensor_scalar(vs_tok[:, n, :], vs_tok[:, n, :], mv[:, n, 0:1], ln_r[:, n:n + 1], ALU.subtract,
                            ALU.mult).then_inc(*now.did("vn0", n))
            dve.wait_ge(*after("vn0", n))
            mul(vs_tok[:, n, :], vs_tok[:, n, :], ln_g).then_inc(*now.did("vn1", n))
            dve.wait_ge(*after("vn1", n))
            V.tensor_tensor(vs_tok[:, n, :], vs_tok[:, n, :], ln_b, ALU.add).then_inc(*now.did("vn", n))
        for g in range(SGU_G):
            dve.wait_ge(*after("psum", "s", g))
            dve.wait_ge(*after("guT", g))
            mul(guT[:, g, :], bank("s", g), guT[:, g, :]).then_inc(*now.both(("aT", g), ("free", "s", g)))
        for t in range(DT):
            dve.wait_ge(*after("psum", "br_a", t))
            dve.wait_ge(*after("sga", t))
            mul(sga[:, t, :], bank("br_a", t), sga[:, t, :]).then_inc(*now.both(("ma", t), ("free", "br_a", t)))
            dve.wait_ge(*after("ma", t))
            dve.wait_ge(*after("mb", t))
            V.tensor_tensor(sga[:, t, :], sga[:, t, :], sgb[:, t, :], ALU.add).then_inc(*now.did("merged", t))
        for t in range(DT):
            dve.wait_ge(*after("psum", "w_o", t))
            dve.wait_ge(*after("mod2", ADA_REST - 1))
            stt(xT[:, t, :], bank("w_o", t), mod[:, 16 + t:17 + t], xT[:, t, :], ALU.mult, ALU.add).then_inc(
                *now.both(("x1", t), ("free", "w_o", t)))

        now = dve_in["ffn"]
        V.memset(pads, 0.0).then_inc(*now.did("pads"))
        dve.wait_ge(*after("rms", "2"))
        V.reciprocal(rstd2[:, 0, :], rstd2[:, 0, :]).then_inc(*now.did("rstd2"))
        dve.wait_ge(*after("rstd2"))
        dve.wait_ge(*after("gs2"))
        for k in range(DT):
            stt(hT[:, k, :], xT[:, k, :], gs2[:, k:k + 1], rstd2[:, 0, :], ALU.mult, ALU.mult).then_inc(
                *now.did("h2T_scaled", k))
        for t in range(FT):
            a = acc[:, t % 4, :].rearrange("p (y x) -> p y x", x=GRID)
            dve.wait_ge(*after("conv", t, 0))
            for tap in range(1, 9):
                ky, kx = tap // 3, tap % 3
                stt(a, pads[:, t % 4, ky:ky + ROWS, kx:kx + GRID], col("conv_w", tap * FT + t), a, ALU.mult,
                    ALU.add).then_inc(*now.did("conv", t, tap))
                dve.wait_ge(*after("conv", t, tap))
            if t:
                gate_values(t - 1)
        gate_values(FT - 1)
        for t in range(DT):
            dve.wait_ge(*after("psum", "down", t))
            stt(xT[:, t, :], bank("down", t), mod[:, 40 + t:41 + t], xT[:, t, :], ALU.mult, ALU.add).then_inc(
                *now.both(("x2", t), ("free", "down", t)))
        dve.wait_ge(*after("rms", "3"))
        V.reciprocal(rstd2[:, 1, :], rstd2[:, 1, :]).then_inc(*now.did("rstd3"))
        dve.wait_ge(*after("rstd3"))
        for k in range(DT):
            stt(x2T[:, k, :], xT[:, k, :], col("final_norm_g", k), rstd2[:, 1, :], ALU.mult, ALU.mult).then_inc(
                *now.did("x2T", k))

        now = dve_in["rwkv"]
        dve.wait_ge(dve_in["ffn"].sem, dve_in["ffn"].count)
        mu = cols[:, COL["rw_mu"]:COL["rw_mu"] + 15]
        ka = cols[:, COL["k_a"]:COL["k_a"] + 4]
        V.tensor_scalar(mix_half, mu, 0.5, None, ALU.mult).then_inc(*now.did("mix_half"))
        V.tensor_scalar(mix_one, mu, -1.0, 1.0, ALU.mult, ALU.add).then_inc(*now.did("mix_one"))
        V.tensor_scalar(half_ka, ka, 0.5, None, ALU.mult).then_inc(*now.did())
        V.tensor_scalar(rest_ka, ka, -0.5, 1.0, ALU.mult, ALU.add).then_inc(*now.did())
        V.tensor_scalar(half_a0, cols[:, COL["a0"]:COL["a0"] + 8], 0.5, None, ALU.mult).then_inc(*now.did("half"))
        V.memset(state_m, 0.0).then_inc(*now.did())
        V.memset(raw[:, :, 0:1], 0.0).then_inc(*now.did())
        V.memset(raw[:, :, L + 1:L + 2], 0.0).then_inc(*now.did("raw_zero"))
        dve.wait_ge(*after("mix_half"))
        def key_squares(hp):
            if hp >= 2:
                dve.wait_ge(*after("psum", "kk", hp - 2))
            V.tensor_scalar(nkkT[:, hp, :], rkT[:, hp, :], col("k_k", hp), None, ALU.mult).then_inc(
                *now.did("kk_raw", hp))
            dve.wait_ge(*after("kk_raw", hp))
            mul(kk_sq[:, hp % 2, :], nkkT[:, hp, :], nkkT[:, hp, :]).then_inc(*now.did("kk_sq", hp))

        def keys_normalised(hp):
            n = kk_n[:, hp % 2, :]
            dve.wait_ge(*after("kk_norm", hp))
            V.tensor_scalar(n, n, 1e-12, None, ALU.max).then_inc(*now.did("kk_max", hp))
            dve.wait_ge(*after("kk_max", hp))
            V.reciprocal(n, n).then_inc(*now.did("kk_inv", hp))
            dve.wait_ge(*after("kk_inv", hp))
            stt(nkkT[:, hp, :], nkkT[:, hp, :], -1.0, n, ALU.mult, ALU.mult).then_inc(*now.did("nkk", hp))

        def mix(i):
            t = RW_TILES[i]
            dve.wait_ge(*after("raw", t))
            V.tensor_tensor(pair_sum[:, i % 2, :], raw[:, i % 3, 0:L], raw[:, i % 3, 2:L + 2], ALU.add).then_inc(
                *now.did("pair_sum", t))
            dve.wait_ge(*after("pair_sum", t))
            dve.wait_ge(*after("mixed0", t))
            stt(mixed[t], pair_sum[:, i % 2, :], mix_half[:, t:t + 1], mixed[t], ALU.mult, ALU.add).then_inc(
                *now.did("mixed", t))
            dve.wait_ge(*after("mixed", t))
            if t == 7:
                key_squares(0)
                key_squares(1)
            if t == 0:
                key_squares(2)
                key_squares(3)
            if t in (1, 2, 3, 8):
                keys_normalised((1, 2, 3, 8).index(t))

        for i in range(14):
            mix(i)

        def as_chunks(ap):
            return ap.rearrange("p (c t) -> p c t", c=TT)

        def prepare(j, part):
            hp, d = JOBS[j]
            s = sets[j % 2]
            inc, exc = (slice(1, P + 1), slice(0, P)) if d == 0 else (slice(0, P), slice(1, P + 1))
            plus = exps[:, 0:2].rearrange("p a c j -> p (a c) j")
            minus = exps[:, 2:4].rearrange("p a c j -> p (a c) j")
            dve.wait_ge(now.sem, now.count)
            if part == 0:
                dve.wait_ge(*after("a", j))
                V.tensor_scalar(job_t, aT, half_ka[:, hp:hp + 1], rest_ka[:, hp:hp + 1], ALU.mult, ALU.add).then_inc(
                    *now.did("job_t", j))
                dve.wait_ge(*after("job_t", j))
                mul(kdT, job_t, rkT[:, hp, :]).then_inc(*now.did("kd", j))
            if part == 1:
                V.tensor_scalar(job_t, aT, -0.5, -0.5, ALU.mult, ALU.add).then_inc(*now.did("job_t2", j))
                dve.wait_ge(*after("job_t2", j))
                mul(job_t, job_t, nkkT[:, hp, :]).then_inc(*now.did("kka", j))
                if d == 0:
                    V.tensor_copy(kd_sum, kdT).then_inc(*now.did("kd_sum", hp))
                else:
                    V.tensor_tensor(kd_sum, kd_sum, kdT, ALU.add).then_inc(*now.did("kd_sum2", hp))
            if part == 2:
                dve.wait_ge(*after("rexp", j))
                mul(as_chunks(bkT[:, 0, :]), as_chunks(job_t), minus[:, :, 0:P]).then_inc(*now.did("job_b", j))
                mul(as_chunks(bkT[:, 1, :]), as_chunks(kdT), minus[:, :, 0:P]).then_inc(*now.did("job_k", j))
                if d == 1:
                    stt(kd_sum, kd_sum, col("r_k", hp), rT[:, hp, :], ALU.mult, ALU.mult).then_inc(
                        *now.did("bonus_in", hp))
            if part == 3:
                mul(s["ar"][:, :, 0, :], as_chunks(nkkT[:, hp, :]), plus[:, :, exc]).then_inc(*now.did("job_a", j))
                mul(s["ar"][:, :, 1, :], as_chunks(rT[:, hp, :]), plus[:, :, inc]).then_inc(*now.did("job_r", j))
                V.tensor_copy(job_stats[:, j % 2, :, :], plus[:, :, P + 1:CUM]).then_inc(*now.did("job_stats", j))

        def gram(j, i, cp):
            d = JOBS[j][1]
            dst = sets[j % 2][("nqb", "mqk")[i]]
            for h in range(2):
                dve.wait_ge(*after("psum", "gram", j, i, cp, h))
                mul(dst[:, 4 * cp + h:4 * cp + h + 3:2, :, :].rearrange("p n a t -> p n (a t)"),
                    bank("gram", j, i, cp, h).rearrange("p (n t) -> p n t", n=2),
                    pair_mask[d].unsqueeze(1).to_broadcast([P, 2, 2 * P])).then_inc(
                    *now.both(("gram", j, i, cp, h), ("free", "gram", j, i, cp, h)))

        def inverse_start(j):
            s = sets[j % 2]
            dve.wait_ge(*after("gram", j, 0, 1, 1))
            lt = s["nqb"][:, :, 0, :]
            V.tensor_tensor(lt, lt, ident.unsqueeze(1).to_broadcast([P, 8, P]), ALU.add).then_inc(*now.did("lt", j))
            dve.wait_ge(*after("lt", j))
            mul(s["g"], lt, level_mask[1 - JOBS[j][1]][0].unsqueeze(1).to_broadcast([P, 8, P])).then_inc(
                *now.did("g0", j))

        def bonus(j):
            hp, d = JOBS[j]
            if d == 1:
                dve.wait_ge(*after("psum", "bonus", hp))
                mul(rvT[:, hp, :], bank("bonus", hp), rvT[:, hp, :]).then_inc(
                    *now.both(("bonus", hp), ("free", "bonus", hp)))

        def invert_y(j, lv, half):
            dve.wait_ge(*after("psum", "iy", j, lv, half))
            dve.wait_ge(now.sem, now.count)
            mul(Y[:, 4 * half:4 * half + 4, :], bank("iy", j, lv, half).rearrange("p (s t) -> p s t", s=4),
                level_mask[JOBS[j][1]][lv + 1].unsqueeze(1).to_broadcast([P, 4, P])).then_inc(
                *now.both(("yi", j, lv, half), ("free", "iy", j, lv, half)))

        def chain_start(j, step):
            if step:
                c = order[JOBS[j][1]][step]
                dve.wait_ge(*after("state", j, step))
                for h, rows in enumerate((LO, HI)):
                    V.tensor_scalar(state_m[rows, h * RH:(h + 1) * RH], state[rows, j % 2, :],
                                    job_stats[rows, j % 2, c, 0:1], None, ALU.mult).then_inc(
                        *(now.did("state_m", j, step) if h else now.did()))

        def chain_sa(j, step):
            dve.wait_ge(now.sem, now.count)
            dve.wait_ge(*after("psum", "cs", j, step))
            V.tensor_copy(sab, bank("cs", j, step)[:, 0:P].rearrange("p (h v) -> p h v", h=2)).then_inc(
                *now.both(("sa", j, step), ("free", "cs", j, step)))

        def chain_end(j, step):
            hp, d = JOBS[j]
            c = order[d][step]
            dve.wait_ge(now.sem, now.count)
            if step < 3:
                dve.wait_ge(*after("psum", "ch", j, step))
                st = job_stats[:, j % 2, c, :]
                s = state[:, j % 2, :]
                if step == 0:
                    V.tensor_scalar(s, bank("ch", j, step)[:, 0:64], st[:, 2:3], None, ALU.mult).then_inc(
                        *now.both(("state", j, 1), ("free", "ch", j, step)))
                else:
                    V.tensor_scalar(state_t, bank("ch", j, step)[:, 0:64], st[:, 2:3], None, ALU.mult).then_inc(
                        *now.both(("state_t", j, step), ("free", "ch", j, step)))
                    dve.wait_ge(*after("state_t", j, step))
                    stt(s, s, st[:, 1:2], state_t, ALU.mult, ALU.add).then_inc(*now.did("state", j, step + 1))
            dve.wait_ge(*after("psum", "cy", j, step))
            y = yT[:, hp, c * P:(c + 1) * P]
            if d == 0:
                ins = V.tensor_copy(y, bank("cy", j, step)[:, 0:P])
            else:
                dve.wait_ge(*after("y_chunk", j - 1, c))
                ins = V.tensor_tensor(y, bank("cy", j, step)[:, 0:P], y, ALU.add)
            ins.then_inc(*now.both(("y_chunk", j, c), ("y", j), ("free", "cy", j, step)))

        for part in range(4):
            prepare(0, part)
        mix(14)
        gram(0, 0, 0)
        gram(0, 0, 1)
        inverse_start(0)
        for j in range(len(JOBS) + 1):
            new, old, ahead = j < len(JOBS), j > 0, j + 1 < len(JOBS)
            if new:
                gram(j, 1, 0)
            if old:
                chain_sa(j - 1, 0)
            if new:
                gram(j, 1, 1)
                bonus(j)
            if old:
                chain_end(j - 1, 0)
            for lv in range(5):
                chained = old and lv < 3
                if chained:
                    chain_start(j - 1, lv + 1)
                if new:
                    invert_y(j, lv, 0)
                    invert_y(j, lv, 1)
                if chained:
                    chain_sa(j - 1, lv + 1)
                    chain_end(j - 1, lv + 1)
                if ahead and lv < 4:
                    prepare(j + 1, lv)
            if new:
                first, second = (LO, HI) if JOBS[j][1] == 0 else (HI, LO)
                dve.wait_ge(*after("psum", "il", j, 0))
                V.tensor_copy(Y[second, :, first], bank("il", j, 0)[second, :].rearrange("p (s t) -> p s t", s=8)
                              ).then_inc(*now.both(("y_last", j), ("free", "il", j, 0)))
            if ahead:
                gram(j + 1, 0, 0)
            if new:
                dve.wait_ge(*after("psum", "il", j, 1))
                V.tensor_copy(sets[j % 2]["g"][first, :, second],
                              bank("il", j, 1)[first, :].rearrange("p (s t) -> p s t", s=8)).then_inc(
                    *now.both(("g_done", j), ("free", "il", j, 1)))
            if ahead:
                gram(j + 1, 0, 1)
                inverse_start(j + 1)

        dve.wait_ge(now.sem, now.count)
        for hp in range(HT):
            dve.wait_ge(*after("psum", "ym", hp))
            dve.wait_ge(*after("y", 2 * hp + 1))
            stt(yT[:, hp, :], bank("ym", hp), -1.0 / RH, yT[:, hp, :], ALU.mult, ALU.add).then_inc(
                *now.both(("yc", hp), ("free", "ym", hp)))
            dve.wait_ge(*after("yc", hp))
            mul(y_sq[:, hp, :], yT[:, hp, :], yT[:, hp, :]).then_inc(*now.did("y_sq", hp))
        for hp in range(HT):
            r = gn_s[:, hp % 2, :]
            dve.wait_ge(*after("gn_std", hp))
            V.reciprocal(r, r).then_inc(*now.did("gn_r", hp))
            dve.wait_ge(*after("gn_r", hp))
            stt(yT[:, hp, :], yT[:, hp, :], col("gn_w", hp), r, ALU.mult, ALU.mult).then_inc(*now.did("yn", hp))
            dve.wait_ge(*after("yn", hp))
            dve.wait_ge(*after("bonus", hp))
            stt(yT[:, hp, :], yT[:, hp, :], col("gn_b", hp), rvT[:, hp, :], ALU.add, ALU.add).then_inc(
                *now.did("yb", hp))
            dve.wait_ge(*after("yb", hp))
            dve.wait_ge(*after("psum", "g", hp))
            mul(yT[:, hp, :], bank("g", hp), yT[:, hp, :]).then_inc(*now.both(("yT", hp), ("free", "g", hp)))

        now = dve_in["hyena"]
        dve.wait_ge(dve_in["rwkv"].sem, dve_in["rwkv"].count)
        V.memset(raw_h[:, :, 0:1], 0.0).then_inc(*now.did())
        V.memset(raw_h[:, :, L + 1:L + 2], 0.0).then_inc(*now.did("raw_zero2"))
        for t in range(12):
            dve.wait_ge(*after("hy0", t))
            stt(hyT[:, t, :], raw_h[:, t % 3, 0:L], col("hy_conv_w", t), hyT[:, t, :], ALU.mult, ALU.add).then_inc(
                *now.did("hy1", t))
            dve.wait_ge(*after("hy1", t))
            stt(hyT[:, t, :], raw_h[:, t % 3, 2:L + 2], col("hy_conv_w", 24 + t), hyT[:, t, :], ALU.mult,
                ALU.add).then_inc(*now.did("hyT", t))
        for o in range(2):
            Hc, Hs = Hcs[o]
            for ft in range(TT):
                p = [prod[:, 4 * (ft % 2) + i, :] for i in range(4)]
                dve.wait_ge(now.sem, now.count)
                dve.wait_ge(*after("psum", "Z", o, 0, ft))
                dve.wait_ge(*after("H", o))
                zc = bank("Z", o, 0, ft)
                mul(p[0], zc, Hc[:, ft, :]).then_inc(*now.did("p", o, ft, 0))
                mul(p[2], zc, Hs[:, ft, :]).then_inc(*now.both(("p", o, ft, 2), ("free", "Z", o, 0, ft)))
                dve.wait_ge(*after("psum", "Z", o, 1, ft))
                zs = bank("Z", o, 1, ft)
                mul(p[1], zs, Hs[:, ft, :]).then_inc(*now.did("p", o, ft, 1))
                mul(p[3], zs, Hc[:, ft, :]).then_inc(*now.both(("p", o, ft, 3), ("free", "Z", o, 1, ft)))
                dve.wait_ge(*after("p", o, ft, 1))
                V.tensor_tensor(Ycs[0][:, ft, :], p[0], p[1], ALU.subtract).then_inc(*now.did("Y", o, 0, ft))
                dve.wait_ge(*after("p", o, ft, 3))
                V.tensor_tensor(Ycs[1][:, ft, :], p[2], p[3], ALU.add).then_inc(*now.did("Y", o, 1, ft))
            for tt in range(TT):
                dve.wait_ge(*after("psum", "conv", o, tt))
                if o == 0:
                    dve.wait_ge(*after("x1_tok", tt))
                    out, gate, name = xv_tok[:, tt, :], x1_tok[:, tt, :], ("z2", tt)
                else:
                    out, gate, name = zT[:, tt, :], hyT[:, 8 + tt, :], ("zT", tt)
                stt(out, bank("conv", o, tt), 1.0 / L, gate, ALU.mult, ALU.mult).then_inc(
                    *now.both(name, ("free", "conv", o, tt)))

        now = dve_in["ffn2"]
        dve.wait_ge(dve_in["hyena"].sem, dve_in["hyena"].count)
        for t in range(DT):
            dve.wait_ge(*after("psum", "rwo", t))
            dve.wait_ge(*after("gate", 8 + t))
            mul(gate_r[:, t, :], bank("rwo", t), gate_r[:, t, :]).then_inc(*now.both(("mr", t), ("free", "rwo", t)))
        for t in range(DT):
            dve.wait_ge(*after("psum", "hyo", t))
            dve.wait_ge(*after("gate", t))
            mul(gate_h[:, t, :], bank("hyo", t), gate_h[:, t, :]).then_inc(*now.both(("mh", t), ("free", "hyo", t)))
            dve.wait_ge(*after("mh", t))
            dve.wait_ge(*after("mr", t))
            V.tensor_tensor(gate_h[:, t, :], gate_h[:, t, :], gate_r[:, t, :], ALU.add).then_inc(
                *now.did("merged2", t))
        for n, group in enumerate(("w_o2", "down2")):
            for t in range(DT):
                dve.wait_ge(*after("psum", group, t))
                stt(x2T[:, t, :], x2T[:, t, :], ALPHA, bank(group, t), ALU.mult, ALU.add).then_inc(
                    *now.both(("res%d" % n, t), ("free", group, t)))
            dve.wait_ge(now.sem, now.count)
            dve.wait_ge(*after("psum", "lm%d" % n))
            mean = norm_s[:, 1, :]
            V.tensor_scalar(mean, bank("lm%d" % n), 1.0 / D, None, ALU.mult).then_inc(
                *now.both(("mean", n), ("free", "lm%d" % n)))
            dve.wait_ge(*after("mean", n))
            for t in range(DT):
                V.tensor_tensor(lnc[:, t, :], x2T[:, t, :], mean, ALU.subtract).then_inc(*now.did("lnc", n, t))
            dve.wait_ge(*after("ln_std2", n))
            r = norm_s[:, 0, :]
            V.reciprocal(r, r).then_inc(*now.did("ln_rstd", n))
            dve.wait_ge(*after("ln_rstd", n))
            for t in range(DT):
                stt(lnc[:, t, :], lnc[:, t, :], col("ln%d_w" % (n + 1), t), r, ALU.mult, ALU.mult).then_inc(
                    *now.did("lnn", n, t))
            if n == 0:
                for t in range(FT):
                    dve.wait_ge(*after("psum", "fu", t))
                    dve.wait_ge(*after("silu_g", t))
                    mul(gT2[:, t, :], bank("fu", t), silu_g[:, t % 4, :]).then_inc(
                        *now.both(("gT2", t), ("free", "fu", t)))

    @block.scalar
    def _(act):

        def run(out, src, func, **kw):
            return nc.scalar.activation(out, src, func, **kw)

        def eps(i, rows=slice(0, P)):
            return eps_cols[rows, i:i + 1]

        now = act_in["start"]
        first = CONST["gla_cum"]
        act.dma_start(cols[:, :], io["cols"]).then_inc(*loads["cols"].loaded("cols"))
        act.dma_start(consts[:, 0:first], io["consts"][:, 0:first]).then_inc(*loads["consts"].loaded("consts"))
        act.dma_start(ctxT, io["ctxT"]).then_inc(*loads["ctx"].loaded("ctx"))
        act.dma_start(xT, io["xT"]).then_inc(*loads["x"].loaded("x"))
        act.dma_start(window, io["window"]).then_inc(*loads["window"].loaded("window"))
        act.dma_start(at(5, U), io["dft"][0]).then_inc(*loads["dft_first"].loaded("dft_first"))
        act.dma_start(consts[:, first:], io["consts"][:, first:]).then_inc(*loads["masks"].loaded("masks"))
        act.wait_ge(*after("cols"))
        run(csil[:, :, 0], cols[:, COL["c"]:COL["c"] + 8], ACT.Silu).then_inc(*now.did())
        run(csil[:, :, 1], cols[:, COL["c_ctx"]:COL["c_ctx"] + 8], ACT.Silu).then_inc(*now.did("csil"))
        def filter_layer(n, meanwhile=()):
            act.wait_ge(*after("filt_sb"))
            act.wait_ge(*after("psum", "filt", n))
            run(filt_a, bank("filt", n)[0:64, :], ACT.Identity, scale=col("filt_sf", n, slice(0, 64)),
                bias=filt_sb[0:64, n:n + 1]).then_inc(*now.both(("filt_a", n), ("free", "filt", n)))
            for src, dst, name, source in meanwhile:
                act.wait_ge(*after(source))
                for k in range(DT):
                    run(dst[:, k, :], src[:, k, :], ACT.Square).then_inc(*now.did(name, k))
            act.wait_ge(*after("filt_r", n))
            run(filt_h, filt_a, ACT.Sin).then_inc(*now.did("filt_h", n))

        filter_layer(0, [(ctxT, sqc, "sqc", "ctx")])
        filter_layer(1, [(xT, sq, "sq", "x")])
        filter_layer(2)

        def mean_square(which, n):
            act.wait_ge(*after("psum", "ss_" + which))
            act.wait_ge(*after("eps"))
            run(rstd[:, n, 0:(L, LC)[n]], bank("ss_" + which)[:, 0:(L, LC)[n]], ACT.Sqrt, scale=1.0 / D,
                bias=eps(0)).then_inc(*now.both(("rms", which), ("free", "ss_" + which)))

        mean_square("c", 1)
        mean_square("x", 0)
        for g in range(4):
            half = spectra[:, 4 * (g % 2):4 * (g % 2) + 4, :]
            if g >= 2:
                act.wait_ge(*after("spectrum_stored", g - 2))
            for ft in range(TT):
                act.wait_ge(*after("psum", "H", g // 2, g % 2, ft))
                run(half[:, ft, :], bank("H", g // 2, g % 2, ft), ACT.Copy).then_inc(
                    *now.both(("spectrum", g, ft), ("free", "H", g // 2, g % 2, ft)))
            act.wait_ge(*after("spectrum", g, TT - 1))
            act.dma_start(io["spectra"][:, g], half).then_inc(*spectra_stored[g % 2].loaded("spectrum_stored", g))
        for k in range(DT):
            act.wait_ge(*after("hcT_scaled", k))
            run(hcT[:, k, :], hcT[:, k, :], ACT.Identity, bias=modc[:, k:k + 1]).then_inc(*now.did("hcT", k))
        for k in range(DT):
            act.wait_ge(*after("hT_scaled", k))
            run(hT[:, k, :], hT[:, k, :], ACT.Identity, bias=mod[:, k:k + 1]).then_inc(*now.did("hT", k))

        now = act_in["gla"]
        def keys(b):
            for t in (2 * b, 2 * b + 1):
                act.wait_ge(*after("psum", "kc", t))
                run(kcT[:, t, :], bank("kc", t)[:, 0:LC], ACT.Copy).then_inc(*now.both(("kcT", t), ("free", "kc", t)))
                act.wait_ge(*after("psum", "k", t))
                run(kT[:, t, :], bank("k", t), ACT.Copy).then_inc(*now.both(("kT", t), ("free", "k", t)))

        def queries(b):
            for t in (2 * b, 2 * b + 1):
                act.wait_ge(*after("psum", "q", t))
                run(qT[:, t, :], bank("q", t), ACT.Copy, scale=DK ** -0.5).then_inc(
                    *now.both(("qT", t), ("free", "q", t)))

        def evacuate_tokens(group, b, half, dst, func, name):
            act.wait_ge(*after("psum", group, b, half))
            run(dst[:, 2 * half:2 * half + 2, b * BLK:(b + 1) * BLK],
                bank(group, b, half).rearrange("p (i c) -> p i c", i=2), func).then_inc(
                *now.both(name, ("free", group, b, half)))

        def values(b):
            evacuate_tokens("vc", b, 0, vc_tok, ACT.Copy, ("vc_tok", b))
            evacuate_tokens("v", b, 0, v_tok, ACT.Copy, ("v_tok0", b))
            evacuate_tokens("v", b, 1, v_tok, ACT.Copy, ("v_tok", b))

        zs = [("zc", d, tt) for d in range(2) for tt in range(TC)] + [("z", d, tt) for d in range(2) for tt in range(TT)]

        def log_sigmoid(first):
            batch = list(enumerate(zs))[first:first + 4]
            for i, (group, d, tt) in batch:
                act.wait_ge(*after("psum", group, d, tt))
                if i >= 8:
                    act.wait_ge(*after(*("free",) + zs[i - 8]))
                run(soft[i % 8], bank(group, d, tt), ACT.Abs).then_inc(*now.did("abs", i))
            for i, z in batch:
                act.wait_ge(*after("abs", i))
                run(soft[i % 8], soft[i % 8], ACT.Exp, scale=-1.0).then_inc(*now.did("exp_z", i))
            for i, z in batch:
                act.wait_ge(*after("exp_z", i))
                run(soft[i % 8], soft[i % 8], ACT.Ln, bias=eps(3)).then_inc(*now.did("soft", *z))

        exp_count = [0]

        def exponentials(group, d, cps):
            inc = slice(1, P + 1) if d == 0 else slice(0, P)
            for h in range(HEADS):
                for cp in range(cps):
                    e = exp_count[0]
                    exp_count[0] += 1
                    act.wait_ge(*after("psum", group, d, h, cp))
                    if e >= 2:
                        act.wait_ge(*after("exp_used", e - 2))
                    ps = bank(group, d, h, cp)[:, 0:2 * CUM].rearrange("p (c j) -> p c j", c=2)
                    run(exps[:, e % 2], ps, ACT.Exp).then_inc(*now.did())
                    run(exps[:, 2 + e % 2, :, 0:P], ps[:, :, inc], ACT.Exp, scale=-1.0).then_inc(
                        *now.both(("exp", group, d, h, cp), ("free", group, d, h, cp)))

        def key_tokens(group, dst, chunks, name):
            for d in range(2):
                for c in range(chunks):
                    act.wait_ge(*after("psum", group, d, c))
                    run(dst[d][:, c, :], bank(group, d, c), ACT.Copy).then_inc(
                        *now.both((name, d, c), ("free", group, d, c)))

        act.wait_ge(*after("psum", "lrc"))
        act.wait_ge(*after("lr_ones"))
        run(lrcT[0:32, :], bank("lrc")[0:32, 0:LC], ACT.Copy).then_inc(*now.both(("lrcT",), ("free", "lrc")))
        act.wait_ge(*after("psum", "lr"))
        run(lrT[0:32, :], bank("lr")[0:32, :], ACT.Copy).then_inc(*now.both(("lrT",), ("free", "lr")))
        keys(0)
        act.wait_ge(*after("spectrum_stored", 2))
        act.wait_ge(*after("spectrum_stored", 3))
        log_sigmoid(0)
        keys(1)
        log_sigmoid(4)
        queries(0)
        log_sigmoid(8)
        queries(1)
        for d in range(2):
            exponentials("cumc", d, 1)
        values(0)
        exponentials("cum", 0, 2)
        values(1)
        exponentials("cum", 1, 2)
        values(2)
        key_tokens("ktc", kc_tok, TC, "kc_tok")
        evacuate_tokens("vc", 3, 0, vc_tok, ACT.Copy, ("vc_tok", 3))
        key_tokens("kt", k_tok, TT, "k_tok")

        def decayed_states(i, hp):
            for d in range(2):
                c = order[d][i]
                for h in (2 * hp, 2 * hp + 1):
                    act.wait_ge(*after("s", 1 + i, d, h))
                    run(sm[d][h][c], s_gla[4 * d + h], ACT.Copy, scale=stats_x[:, d, h, c, 0:1]).then_inc(
                        *now.did("sm", d, h, c))

        decayed_states(0, 0)
        decayed_states(0, 1)
        evacuate_tokens("v", 3, 0, v_tok, ACT.Copy, ("v_tok0", 3))
        decayed_states(1, 0)
        decayed_states(2, 0)
        evacuate_tokens("v", 3, 1, v_tok, ACT.Copy, ("v_tok", 3))
        decayed_states(3, 0)
        for i in range(1, TT):
            decayed_states(i, 1)

        def output_rms(h):
            act.wait_ge(*after("psum", "oss", h))
            if h >= 2:
                act.wait_ge(*after("o_normed", 2 * (h - 2) + 1))
            run(work[h % 2], bank("oss", h), ACT.Sqrt, scale=1.0 / DV, bias=eps(0)).then_inc(
                *now.both(("o_rms", h), ("free", "oss", h)))

        for h in range(HEADS):
            for t in (2 * h, 2 * h + 1):
                act.wait_ge(*after("psum", "o", t))
                run(oT[:, t, :], bank("o", t), ACT.Copy).then_inc(*now.did("oT", t))
                if h >= 2:
                    act.wait_ge(*after("psum", "oss", h - 2))
                run(osq[:, t % 4, :], bank("o", t), ACT.Square).then_inc(*now.both(("osq", t), ("free", "o", t)))
            if h >= 1:
                output_rms(h - 1)

        now = act_in["mix"]

        def evacuate(group, t, dst, func, name, **kw):
            act.wait_ge(*after("psum", group, t))
            run(dst, bank(group, t), func, **kw).then_inc(*now.both((name, t), ("free", group, t)))

        for t in range(DT):
            evacuate("r", t, silu_r[:, t, :], ACT.Silu, "silu_r")
            if t == 1:
                output_rms(HEADS - 1)
        for t in range(DT):
            evacuate("gb", t, sgb[:, t, :], ACT.Sigmoid, "sgb")
        for t in range(DT):
            evacuate("ga", t, sga[:, t, :], ACT.Sigmoid, "sga")
        for b in range(4):
            for half in range(2):
                evacuate_tokens("vs", b, half, vs_tok, ACT.Gelu, ("vs", b, half))
        for t in range(DT):
            evacuate("u", t, guT[:, t, :], ACT.Gelu, "guT")
            if t == 3:
                act.wait_ge(*after("mv", 3))
                run(ln_r, mv[:, :, 1], ACT.Sqrt, bias=eps(0)).then_inc(*now.did("ln_std"))
        for k in range(DT):
            act.wait_ge(*after("x1", k))
            run(sq5[:, k, :], xT[:, k, :], ACT.Square).then_inc(*now.did("sq2", k))
        act.wait_ge(*after("psum", "ss2"))
        run(rstd2[:, 0, :], bank("ss2"), ACT.Sqrt, scale=1.0 / D, bias=eps(0)).then_inc(
            *now.both(("rms", "2"), ("free", "ss2")))

        now = act_in["ffn"]
        for k in range(DT):
            act.wait_ge(*after("h2T_scaled", k))
            run(hT[:, k, :], hT[:, k, :], ACT.Identity, bias=mod[:, 24 + k:25 + k]).then_inc(*now.did("h2T", k))
        act.wait_ge(*after("pads"))

        def gelu(t):
            act.wait_ge(*after("conv", t, 8))
            run(acc[:, t % 4, :], acc[:, t % 4, :], ACT.Gelu).then_inc(*now.did("gelu", t))

        for t in range(FT):
            act.wait_ge(*after("psum", "fa", t))
            if t >= 4:
                act.wait_ge(*after("conv", t - 4, 8))
            run(pads[:, t % 4, 1:1 + ROWS, 1:1 + GRID], bank("fa", t).rearrange("p (y x) -> p y x", x=GRID),
                ACT.Copy).then_inc(*now.both(("pad", t), ("free", "fa", t)))
            act.wait_ge(*after("pad", t))
            if t >= 4:
                act.wait_ge(*after("gT", t - 4))
            run(acc[:, t % 4, :].rearrange("p (y x) -> p y x", x=GRID), pads[:, t % 4, 0:ROWS, 0:GRID], ACT.Identity,
                scale=col("conv_w", t), bias=col("conv_b", t)).then_inc(*now.did("conv", t, 0))
            if t:
                gelu(t - 1)
        gelu(FT - 1)
        for k in range(DT):
            act.wait_ge(*after("x2", k))
            run(sq5[:, k, :], xT[:, k, :], ACT.Square).then_inc(*now.did("sq3", k))
        act.wait_ge(*after("psum", "ss3"))
        run(rstd2[:, 1, :], bank("ss3"), ACT.Sqrt, scale=1.0 / D, bias=eps(0)).then_inc(
            *now.both(("rms", "3"), ("free", "ss3")))

        now = act_in["rwkv"]
        act.wait_ge(*after("raw_zero"))
        act.wait_ge(*after("mix_one"))
        def key_norm(hp):
            if hp >= 2:
                act.wait_ge(*after("nkk", hp - 2))
            evacuate("kk", hp, kk_n[:, hp % 2, :], ACT.Sqrt, "kk_norm")

        def project(i):
            t = RW_TILES[i]
            if i >= 3:
                act.wait_ge(*after("mixed", RW_TILES[i - 3]))
            evacuate("rw", t, raw[:, i % 3, 1:L + 1], ACT.Copy, "raw")
            act.wait_ge(*after("raw", t))
            run(mixed[t], raw[:, i % 3, 1:L + 1], ACT.Copy, scale=mix_one[:, t:t + 1]).then_inc(
                *now.did("mixed0", t))
            if t == 4:
                act.wait_ge(*after("mixed", 12))
                run(wdT, wdT, ACT.Tanh).then_inc(*now.did("wd_tanh"))
            if t == 1:
                key_norm(0)
                key_norm(1)
            if t in (7, 2):
                d = (7, 2).index(t)
                for tt in range(TT):
                    act.wait_ge(*after("psum", "w", d, tt))
                    run(lw[d][:, tt, :], bank("w", d, tt), ACT.Sigmoid).then_inc(
                        *now.both(("lw", d, tt), ("free", "w", d, tt)))
            if t in (2, 3):
                key_norm(t)

        for i in range(14):
            project(i)
        act.wait_ge(*after("half"))

        def inputs(j):
            hp, d = JOBS[j]
            inc = slice(1, P + 1) if d == 0 else slice(0, P)
            if j:
                act.wait_ge(*after("job_stats", j - 1))
            evacuate("a", j, aT, ACT.Tanh, "a", scale=0.5, bias=half_a0[:, 4 * d + hp:4 * d + hp + 1])
            for cp in range(2):
                act.wait_ge(*after("psum", "rcum", j, cp))
                ps = bank("rcum", j, cp)[:, 0:2 * CUM].rearrange("p (c j) -> p c j", c=2)
                run(exps[:, cp], ps, ACT.Exp).then_inc(*now.did())
                run(exps[:, 2 + cp, :, 0:P], ps[:, :, inc], ACT.Exp, scale=-1.0).then_inc(
                    *now.both(("rexp", j), ("free", "rcum", j, cp)))

        def tokens(j):
            for i, dst in ((0, "b_tok"), (1, "k_tok")):
                act.wait_ge(*after("psum", "tok", j, i))
                run(sets[j % 2][dst], bank("tok", j, i).rearrange("p (c f) -> p c f", c=4), ACT.Copy).then_inc(
                    *now.both(("tok", j, i), ("free", "tok", j, i)))

        def inverse_start(j, half):
            act.wait_ge(*after("psum", "x0", j, half))
            run(X[:, 4 * half:4 * half + 4, :], bank("x0", j, half).rearrange("p (s t) -> p s t", s=4),
                ACT.Copy).then_inc(*now.both(("x", j, 0, half), ("free", "x0", j, half)))

        def invert_xg(j, lv, half):
            for what, dst, name in (("ix", X, "x"), ("ig", sets[j % 2]["g"], "g")):
                act.wait_ge(*after("psum", what, j, lv, half))
                run(dst[:, 4 * half:4 * half + 4, :], bank(what, j, lv, half).rearrange("p (s t) -> p s t", s=4),
                    ACT.Copy).then_inc(*now.both((name, j, lv + 1, half), ("free", what, j, lv, half)))

        def chain_u(j, step):
            act.wait_ge(*after("psum", "cu", j, step))
            run(ub, bank("cu", j, step)[:, 0:P].rearrange("p (h v) -> p h v", h=2), ACT.Copy).then_inc(
                *now.both(("u", j, step), ("free", "cu", j, step)))

        inputs(0)
        project(14)
        for c in range(TT):
            evacuate("vt", c, rv_tok[:, c, :], ACT.Copy, "rv_tok")
        tokens(0)
        act.wait_ge(*after("mixed", 14))
        run(gdT, gdT, ACT.Sigmoid).then_inc(*now.did("gd_sig"))
        for j in range(len(JOBS) + 1):
            new, old, ahead = j < len(JOBS), j > 0, j + 1 < len(JOBS)
            if old:
                chain_u(j - 1, 0)
            if new:
                inverse_start(j, 0)
                inverse_start(j, 1)
            if ahead:
                inputs(j + 1)
            for lv in range(5):
                if old and lv < 3:
                    chain_u(j - 1, lv + 1)
                if new:
                    invert_xg(j, lv, 0)
                    invert_xg(j, lv, 1)
            if ahead:
                tokens(j + 1)
        for hp in range(HT):
            act.wait_ge(*after("psum", "yv", hp))
            if hp >= 2:
                act.wait_ge(*after("yn", hp - 2))
            run(gn_s[:, hp % 2, :], bank("yv", hp), ACT.Sqrt, scale=1.0 / RH, bias=eps(2)).then_inc(
                *now.both(("gn_std", hp), ("free", "yv", hp)))

        now = act_in["hyena"]
        act.wait_ge(*after("raw_zero2"))
        for t in range(12):
            if t >= 3:
                act.wait_ge(*after("hyT", t - 3))
            evacuate("hy", t, raw_h[:, t % 3, 1:L + 1], ACT.Copy, "hraw")
            act.wait_ge(*after("hraw", t))
            run(hyT[:, t, :], raw_h[:, t % 3, 1:L + 1], ACT.Identity, scale=col("hy_conv_w", 12 + t),
                bias=col("hy_conv_b", t)).then_inc(*now.did("hy0", t))
        for c in range(TT):
            evacuate("hvt", c, xv_tok[:, c, :], ACT.Copy, "xv_tok")
        for c in range(TT):
            evacuate("hxt", c, x1_tok[:, c, :], ACT.Copy, "x1_tok")

        now = act_in["ffn2"]
        for t in range(2 * DT):
            evacuate("gate", t, (gate_h if t < DT else gate_r)[:, t % DT, :], ACT.Sigmoid, "gate")
        for n in range(2):
            for t in range(DT):
                act.wait_ge(*after("lnc", n, t))
                run(lnsq[:, t, :], lnc[:, t, :], ACT.Square).then_inc(*now.did("lnsq%d" % n, t))
            act.wait_ge(*after("psum", "lv%d" % n))
            run(norm_s[:, 0, :], bank("lv%d" % n), ACT.Sqrt, scale=1.0 / D, bias=eps(1)).then_inc(
                *now.both(("ln_std2", n), ("free", "lv%d" % n)))
            for t in range(DT):
                act.wait_ge(*after("lnn", n, t))
                run(x2T[:, t, :], lnc[:, t, :], ACT.Identity, bias=col("ln%d_b" % (n + 1), t)).then_inc(
                    *now.did("x3T" if n == 0 else "out", t))
            if n == 0:
                for t in range(FT):
                    if t >= 4:
                        act.wait_ge(*after("gT2", t - 4))
                    evacuate("fg", t, silu_g[:, t % 4, :], ACT.Silu, "silu_g")

    @block.gpsimd
    def _(pool):

        def load(name, dst, src=None):
            pool.dma_start(dst, io[name] if src is None else src).then_inc(*loads[name].loaded(name))

        load("skip", skip_row)
        pool.wait_ge(*after("psum", "H", 1, 1, 3))
        load("gla_w2", gla_w2)
        pool.wait_ge(*after("psum", "sc", 1, 3))
        pool.wait_ge(*after("psum", "kt", 1, 3))
        pool.wait_ge(*after("la", 1, 3))
        load("ln_g", ln_g, io["ln_g"].partition_broadcast(P))
        load("ln_b", ln_b, io["ln_b"].partition_broadcast(P))
        load("w_s", w_sT)
        load("b_s", b_s)
        pool.wait_ge(*after("psum", "ss3"))
        load("rw_small", at(2, 2 * L, 2048).rearrange("p (n c) -> p n c", n=2))
        pool.dma_start(rw_w2, io["rw_w2"]).then_inc(*loads["rw_small"].loaded("rw_w2"))
        load("w0", w0_row)
        last = len(JOBS) - 1
        pool.wait_ge(*after("y", last))
        pool.wait_ge(*after("spectrum_stored", 2))
        pool.wait_ge(*after("spectrum_stored", 3))
        pool.dma_start(at(0, U), io["dft"][0]).then_inc(*loads["dft"].loaded("dft"))
        pool.dma_start(at(7, U).rearrange("p (s f n) -> p s f n", s=2, f=TT), io["spectra"][:, 0:2]).then_inc(
            *loads["H0"].loaded("H", 0))
        pool.dma_start(at(6, U), io["dft"][1]).then_inc(*loads["dftT"].loaded("dftT"))
        for c in range(TT):
            pool.wait_ge(*after("psum", "hvt", c))
            pool.wait_ge(*after("psum", "hxt", c))
        pool.dma_start(at(3, U).rearrange("p (s f n) -> p s f n", s=2, f=TT), io["spectra"][:, 2:4]).then_inc(
            *loads["H1"].loaded("H", 1))

    @block.sync
    def _(sp):
        for name, dst in (("featsT", featsT), ("fw1", fw1), ("fw2", fw23[0]), ("fw3", fw23[1])):
            sp.dma_start(dst, io[name]).then_inc(*loads["filters"].loaded("filters"))
        sp.dma_start(fw4, io["fw4"]).then_inc(*loads["filters_out"].loaded("filters_out"))
        for n in range(NBLOCKS):
            if n == POSITION["hy_in", 1]:
                sp.wait_ge(*after("psum", "gram", len(JOBS) - 1, 1, 1, 1))
            if n >= RING:
                sp.wait_ge(*after(*block_done[n - RING]))
            sp.dma_start(ring[:, n % RING, :], io["weights"][n]).then_inc(*slot_loaded[n % RING].loaded("block", n))
        for t in range(DT):
            sp.wait_ge(*after("out", t))
            sp.dma_start(io["out"][:, t, :], x2T[:, t, :]).then_inc(*out_stored.loaded("stored", t))
        sp.wait_ge(*after("stored", DT - 1))



def _constants():
    eye = np.eye(P, dtype=np.float32)
    i, j = np.arange(P)[:, None], np.arange(P)[None, :]
    head = (i // RH == j // RH).astype(np.float32)

    def cumulative(d, unit):
        at = np.arange(P + 1)[None, :]
        if d == 0:
            upto, first = (i < at).astype(np.float64), (i < P // 2).astype(np.float64)
        else:
            upto, first = (i >= at).astype(np.float64), (i >= P // 2).astype(np.float64)
        one = np.ones_like(first)
        return np.concatenate([upto - first, first, one, one - first], 1) * unit

    def level(d, m):
        a, b = (i, j) if d == 0 else (j, i)
        return ((a // (2 * m) == b // (2 * m)) & (a // m > b // m)) | (i == j)

    later = [(j >= i), (j <= i)]
    strict = [(j > i), (j < i)]
    parts = [eye, np.ones((P, P)), head]
    parts += [cumulative(d, 1.0 / 16.0) for d in range(2)]
    parts += [cumulative(d, DECAY) for d in range(2)]
    parts += later
    parts += [x for d in range(2) for x in (strict[d], later[d])]
    parts += [level(d, m) for d in range(2) for m in [1] + LEVELS]
    table = np.concatenate([np.asarray(x, np.float64) for x in parts], 1).astype(np.float32)
    assert table.shape == (P, NCONST)

    t, f = np.arange(L)[:, None], np.arange(L)[None, :]
    angle = 2.0 * np.pi * ((t * (2 * f + 1)) % (4 * L)) / (4.0 * L)
    cos, sin = np.cos(angle), np.sin(angle)

    def rows(a):
        return a.reshape(TT, P, L).transpose(1, 0, 2).reshape(P, TT * L)

    dft = np.stack([np.concatenate([rows(a) for a in m], 1) for m in ((cos, sin), (cos.T, sin.T))]).astype(np.float32)
    time = np.linspace(0.0, 1.0, L, dtype=np.float32)[:, None]
    w = (2.0 * math.pi * np.arange(L, dtype=np.float32) / L).astype(np.float32)
    bands = np.linspace(1e-4, 15, 16, dtype=np.float32)
    ang = (w[:, None] * bands[None, :]).astype(np.float32)
    feats = np.concatenate([time, np.cos(ang), -np.sin(ang)], 1).astype(np.float32)
    deltas = np.abs(np.linspace(math.log(1e-2) / 1.5, math.log(1e-2) / 0.3, HW, dtype=np.float32))
    window = np.exp(-time * deltas[None, :]).astype(np.float32)
    return table, dft, np.ascontiguousarray(feats.T), window.reshape(TT, P, HW).transpose(1, 0, 2)


def _blocks(w, width=BLK):
    k, n = w.shape
    kt = 2048 // width
    rows, colsn = -(-k // (kt * P)) * kt * P, -(-n // width) * width
    if (rows, colsn) != (k, n):
        padded = np.zeros((rows, colsn), w.dtype)
        padded[:k, :n] = w
        w = padded
    w = w.reshape(rows // (kt * P), kt, P, colsn // width, width)
    return w.transpose(3, 0, 2, 1, 4).reshape(-1, P, kt * width)


def kernel(**inputs):
    import concourse.bacc as bacc
    from concourse.bass_utils import run_bass_kernel_spmd

    a = {k: np.asarray(v) for k, v in inputs.items()}
    m = {k: (v[0] if v.shape[:1] == (1,) else v) for k, v in a.items()}

    offs = np.cumsum([0, 1024, 1024, 512, 1024, 1024, 1024, 512, 1024, 32])
    u, vs, q, r, ga, gb, k, v, lr = (m["w_in"][:, offs[i]:offs[i + 1]] for i in range(9))
    up, up2g, up2u = (_blocks(w) for w in (m["ffn_w_up"], m["ffn_w_gate_2"], m["ffn_w_up_2"]))
    half = FT // 2
    w_in2 = m["w_in_2"]
    streams = {
        "ada1": _blocks(m["w_ada"][:, :2048]), "ada2": _blocks(m["w_ada"][:, 2048:]),
        "k": _blocks(k), "v": _blocks(v), "lr": _blocks(lr), "q": _blocks(q), "r": _blocks(r), "gb": _blocks(gb),
        "br_b": _blocks(m["w_br_b"]), "ga": _blocks(ga), "vs": _blocks(vs), "u": _blocks(u),
        "br_a": _blocks(m["w_br_a"]), "w_o": _blocks(m["w_o"]),
        "up": np.stack([up[:half], up[half:]], 1).reshape(-1, P, 2048), "down": _blocks(m["ffn_w_down"]),
        "rw_in": _blocks(w_in2[:, 1536:3456])[list(RW_ORDER)], "hy_in": _blocks(w_in2[:, :1536]), "gates": _blocks(w_in2[:, 3456:]),
        "rw_out": _blocks(m["w_rw_out_2"], 2 * BLK), "hy_out": _blocks(m["w_hy_out_2"], 2 * BLK),
        "w_o2": _blocks(m["w_o_2"]), "up2": np.stack([up2g, up2u], 1).reshape(-1, P, 2048),
        "down2": _blocks(m["ffn_w_down_2"]),
    }
    assert all(len(streams[name]) == n for name, n in STREAM)
    weights = np.stack([streams[name][i] for name, i in BLOCK_ORDER])

    def tile_columns(x, width=P):
        x = x.reshape(-1, width)
        return np.concatenate([x, np.zeros((len(x), P - width), x.dtype)], 1) if width < P else x

    source = {
        "c": m["c"], "c_ctx": a["c_ctx"], "b_ada": m["b_ada"], "norm1_g": m["norm1_g"], "norm2_g": m["norm2_g"],
        "gla_norm_g": m["gla_norm_g"], "final_norm_g": a["final_norm_g"], "conv_w": m["ffn_conv_w"],
        "conv_b": m["ffn_conv_b"], "hy_conv_w": m["hy_conv_w_2"], "hy_conv_b": m["hy_conv_b_2"],
        "rw_mu": m["rw_mu_2"], "a0": m["rw_a0_2"], "k_k": m["rw_k_k_2"], "k_a": m["rw_k_a_2"],
        "r_k": m["rw_r_k_2"], "gn_w": m["rw_gn_w_2"], "gn_b": m["rw_gn_b_2"], "ln1_w": m["ln1_w_2"],
        "ln1_b": m["ln1_b_2"], "ln2_w": m["ln2_w_2"], "ln2_b": m["ln2_b_2"],
        "filt_b": np.stack([m["hy_filt_b1_2"], m["hy_filt_b2_2"], m["hy_filt_b3_2"]]),
        "filt_sf": m["hy_sin_freq_2"],
    }
    table = np.concatenate([tile_columns(source[name], 64 if name.startswith("filt") else P) for name, _ in COLUMNS])
    consts, dft, featsT, window = _constants()

    def feature_major(x):
        return x.T.reshape(DT, P, -1).transpose(1, 0, 2)

    gla_w2 = np.zeros((33, 2, HW), np.float32)
    for d in range(2):
        gla_w2[d * RANK:(d + 1) * RANK, d] = m["gla_w2"][d]
        gla_w2[32, d] = m["gla_b2"][d]
    rw_w2 = np.zeros((P, 2, HW), np.float32)
    for d in range(2):
        rw_w2[d * 64:(d + 1) * 64, d] = m["rw_w2_2"][d]
    arrays = {
        "weights": weights, "cols": table.T, "consts": consts,
        "xT": feature_major(m["x"]), "ctxT": feature_major(m["ctx"]), "gla_w2": gla_w2,
        "ln_g": m["sgu_ln_g"], "ln_b": m["sgu_ln_b"], "w_s": m["sgu_w"].transpose(2, 0, 1),
        "b_s": m["sgu_b"].reshape(1, D),
        "rw_small": np.stack([m["rw_a2_2"].reshape(P, HW), m["rw_g2_2"]], 1), "rw_w2": rw_w2,
        "w0": m["rw_w0_2"].reshape(1, D), "featsT": featsT, "fw1": m["hy_filt_w1_2"], "fw2": m["hy_filt_w2_2"],
        "fw3": m["hy_filt_w3_2"], "fw4": m["hy_filt_w4_2"].reshape(64, 2, 2, HW), "skip": m["hy_skip_2"].reshape(1, D),
        "window": window, "dft": dft,
    }
    arrays = {f"{k}_dram": np.ascontiguousarray(x) for k, x in arrays.items()}

    def declare():
        nc = bacc.Bacc("TRN2", target_bir_lowering=False, num_devices=1)
        io = {k[:-5]: nc.dram_tensor(k, x.shape, F32, kind="ExternalInput").ap() for k, x in arrays.items()}
        io["spectra"] = nc.dram_tensor("spectra_dram", (P, 4, TT, HW), F32, kind="Internal").ap()
        io["out"] = nc.dram_tensor("out_dram", (P, DT, L), F32, kind="ExternalOutput").ap()
        return nc, io

    announced = build(*declare(), None)
    nc, io = declare()
    build(nc, io, announced)
    result = run_bass_kernel_spmd(nc, [arrays], core_ids=[0]).results[0]["out_dram"]
    return np.ascontiguousarray(result.transpose(1, 0, 2).reshape(D, L).T).reshape(1, L, D)
```

```python
import math
from contextlib import ExitStack

import numpy as np

import concourse.bass as bass
from concourse import mybir

F32 = mybir.dt.float32
F32R = mybir.dt.float32r
ACT = mybir.ActivationFunctionType
ALU = mybir.AluOpType

P = 128
D = 1024
L = 512
LC = 256
DT = D // P
TT = L // P
TC = LC // P
HEADS = 4
DK, DV = 128, 256
RANK = 16
SGU_G = 8
FF = 2816
FT = FF // P
GRID = 64
ROWS = L // GRID
HW = 512
HT = HW // P
RH = 64
BLK = 256
RING = 3
BANKS = 8
EPS, LN_EPS, GN_EPS = 1e-6, 1e-5, 64e-5
ALPHA = 2.0 ** 0.25
DECAY = -math.exp(-0.5)
LEVELS = [2, 4, 8, 16, 32]
BIG = 1e30
U = 4096
CUM = P + 4

COLUMNS = [
    ("c", 8), ("c_ctx", 8), ("b_ada", 48), ("norm1_g", 8), ("norm2_g", 8), ("gla_norm_g", 8),
    ("final_norm_g", 8), ("conv_w", 9 * FT), ("conv_b", FT), ("hy_conv_w", 36), ("hy_conv_b", 12),
    ("rw_mu", 15), ("a0", 8), ("k_k", 4), ("k_a", 4), ("r_k", 4), ("gn_w", 4), ("gn_b", 4),
    ("ln1_w", 8), ("ln1_b", 8), ("ln2_w", 8), ("ln2_b", 8), ("filt_b", 3), ("filt_sf", 3),
]
COL = {}
for _name, _n in COLUMNS:
    COL[_name] = sum(n for _, n in COLUMNS[:len(COL)])
NCOL = sum(n for _, n in COLUMNS)

ADA_FIRST, ADA_REST = 8, 16
STREAM = [
    ("ada1", ADA_FIRST), ("lr", 1), ("k", 2), ("q", 2), ("v", 4), ("ada2", ADA_REST), ("r", 4), ("gb", 4),
    ("br_b", 4), ("ga", 4), ("vs", 4), ("u", 4), ("br_a", 4), ("w_o", 4), ("up", 22), ("down", 12),
    ("rw_in", 8), ("hy_in", 6), ("gates", 8), ("rw_out", 2), ("hy_out", 2), ("w_o2", 4), ("up2", 22), ("down2", 12),
]
BLOCK_ORDER, _rest = [], [("ada2", _i) for _i in range(ADA_REST)]
for _name, _n in STREAM:
    for _i in range(0 if _name == "ada2" else _n):
        BLOCK_ORDER.append((_name, _i))
        if _name != "ada1" and _rest:
            BLOCK_ORDER.append(_rest.pop(0))
POSITION = {_block: _n for _n, _block in enumerate(BLOCK_ORDER)}
NBLOCKS = sum(n for _, n in STREAM)

RW_ORDER = (6, 2, 3, 0, 1, 4, 5, 7)
RW_TILES = [t for _b in RW_ORDER for t in (2 * _b, 2 * _b + 1) if t < 15]

CONSTS = [
    ("ident", P), ("ones", P), ("headones", P), ("gla_cum", 2 * CUM), ("rw_cum", 2 * CUM), ("incl", 2 * P),
    ("pair_mask", 4 * P), ("level_mask", 2 * 6 * P),
]
CONST = {}
for _name, _n in CONSTS:
    CONST[_name] = sum(n for _, n in CONSTS[:len(CONST)])
NCONST = sum(n for _, n in CONSTS)


class Progress:

    def __init__(self, known):
        self.known = known
        self.found = {}
        self.signals = {}

    def stage(self, nc, ctx, name):
        self.signals[name] = Signal(self, name, ctx.enter_context(nc.semaphore(name)))
        return self.signals[name]

    def after(self, *what):
        name, count = self.known[what] if self.known is not None else (next(iter(self.signals)), 1)
        return self.signals[name].sem, count


class Signal:

    def __init__(self, progress, name, sem):
        self.progress, self.name, self.sem, self.count = progress, name, sem, 0

    def did(self, *what):
        self.count += 1
        if what:
            self.note(what)
        return self.sem, 1

    def both(self, *whats):
        self.count += 1
        for what in whats:
            self.note(what)
        return self.sem, 1

    def note(self, what):
        found = self.progress.found
        assert what not in found or what[0] in ("y", "rexp"), what
        found[what] = (self.name, self.count)

    def loaded(self, *what):
        self.count += 16
        self.progress.found[what] = (self.name, self.count)
        return self.sem, 16


def build(nc, io, known):
    progress = Progress(known)
    ctx = ExitStack()
    with ctx:
        _build(nc, io, progress, ctx)
    return progress.found


def _build(nc, io, progress, ctx):
    after = progress.after

    def sb(name, shape):
        return ctx.enter_context(nc.sbuf_tensor(name, shape, F32))

    cols = sb("cols", [P, NCOL])
    consts = sb("consts", [P, NCONST])
    ring_at = nc.sbuf_base
    ring = sb("ring", [P, RING, 8 * BLK])
    ring_split = nc.alloc_sbuf_tensor_at("ring_split", [P, RING, 8 * BLK], F32R, offset=ring_at)
    arena_at = nc.sbuf_base
    arena = sb("arena", [P, 10 * U])
    small = sb("small", [P, 1280])
    scratch = sb("scratch", [P, 8 * CUM])
    banks = ctx.enter_context(nc.psum_tensor("banks", [P, BANKS, 512], F32))

    def at(unit, size, offset=0):
        start = unit * U + offset
        return arena[:, start:start + size]

    def tiles(unit, n, width=L, offset=0):
        return at(unit, n * width, offset).rearrange("p (n t) -> p n t", n=n)

    def split_at(name, unit, size, offset=0):
        place = arena_at + 4 * (unit * U + offset)
        return nc.alloc_sbuf_tensor_at(name, [P, size], F32R, offset=place)[:, :]

    def split_tiles(name, unit, n):
        return split_at(name, unit, n * L).rearrange("p (n t) -> p n t", n=n)

    def col(name, i=0, rows=slice(0, P)):
        return cols[rows, COL[name] + i:COL[name] + i + 1]

    def const(name, n, i=0):
        return consts[:, CONST[name] + i * n:CONST[name] + (i + 1) * n]

    ident, ones, headones = const("ident", P), const("ones", P), const("headones", P)
    gla_cum = [const("gla_cum", CUM, d) for d in range(2)]
    rw_cum = [const("rw_cum", CUM, d) for d in range(2)]
    incl = [const("incl", P, d) for d in range(2)]
    pair_mask = [const("pair_mask", 2 * P, d) for d in range(2)]
    level_mask = [[const("level_mask", P, 6 * d + i) for i in range(6)] for d in range(2)]

    csil = small[:, 0:16].rearrange("p (k n) -> p k n", n=2)
    mod = small[:, 16:80]
    modc = small[:, 80:96]
    gs1, gs1c, gs2 = small[:, 96:104], small[:, 104:112], small[:, 112:120]
    eps_cols = small[:, 120:124]
    bn = small[:, 124:124 + 48].rearrange("p (t h s) -> p t h s", t=4, h=2)
    mv = small[:, 172:180].rearrange("p (t s) -> p t s", t=4)
    ln_r = small[:, 180:184]
    stats_x = small[:, 184:184 + 96].rearrange("p (d h c s) -> p d h c s", d=2, h=4, c=4)
    stats_c = small[:, 280:280 + 48].rearrange("p (d h c s) -> p d h c s", d=2, h=4, c=2)
    mix_half, mix_one = small[:, 328:343], small[:, 343:358]
    half_ka, rest_ka, half_a0 = small[:, 358:362], small[:, 362:366], small[:, 366:374]
    filt_sb = small[:, 374:377]
    ones_row = small[0:1, 384:512]
    state = small[:, 512:640].rearrange("p (b v) -> p b v", b=2)
    state_t = small[:, 640:704]
    state_m = small[:, 1048:1176]
    ub = small[:, 768:896].rearrange("p (h v) -> p h v", h=2)
    sab = small[:, 896:1024].rearrange("p (h v) -> p h v", h=2)
    ada_sums = [small[:, 512 + BLK * i:512 + BLK * (i + 1)] for i in range(2)]
    job_stats = small[:, 1024:1048].rearrange("p (b c s) -> p b c s", b=2, c=4)

    psum_full = progress.stage(nc, ctx, "psum_full")
    slot_loaded = [progress.stage(nc, ctx, f"slot_loaded{i}") for i in range(RING)]
    names = ["start", "ada", "gla", "mix", "ffn", "rwkv", "hyena", "ffn2"]
    dve_in = {n: progress.stage(nc, ctx, f"dve_{n}") for n in names}
    act_in = {n: progress.stage(nc, ctx, f"act_{n}") for n in names}
    pool_in = {n: progress.stage(nc, ctx, f"pool_{n}") for n in names}
    loads = {n: progress.stage(nc, ctx, f"load_{n}") for n in
             ("cols", "consts", "masks", "x", "ctx", "gla_w2", "ln_g", "ln_b", "w_s", "b_s", "rw_small", "w0",
              "filters", "filters_out", "dft_first", "dft", "window", "skip", "H0", "H1")}
    spectra_stored = [progress.stage(nc, ctx, f"spectra_stored{i}") for i in range(2)]
    out_stored = progress.stage(nc, ctx, "out_stored")

    xT = tiles(0, DT)
    hT = tiles(1, DT)
    ctxT = tiles(2, DT, LC, 0)
    hcT = tiles(2, DT, LC, 2048)
    sq, sqc = hT, hcT
    rstd = tiles(4, 2)
    kT, kcT = tiles(4, HEADS), tiles(4, HEADS, LC, 2048)
    lrT, lrcT = at(4, L, 3072)[0:33], at(4, LC, 3584)[0:33]
    v_tok = tiles(5, TT, D)
    vc_tok = tiles(6, TC, D)
    qT = tiles(6, HEADS, L, 2048)
    la = [tiles(7, TT, L, 2048 * d) for d in range(2)]
    lac = [tiles(3, TC, L, 1024 * d) for d in range(2)]
    gla_w2 = at(8, 1024)[0:33].rearrange("p (d n) -> p d n", d=2)
    soft = [at(9, L, 512 * i) for i in range(8)]
    q_dec = [tiles(8, HEADS, L, 2048 * d) for d in range(2)]
    k_inv = [tiles(9, HEADS, L, 2048 * d) for d in range(2)]
    kc_inv = [tiles(3, HEADS, LC, 2048 + 1024 * d) for d in range(2)]
    k_tok = [tiles(2, TT, L, 2048 * d) for d in range(2)]
    kc_tok = [tiles(3, TC, L, 1024 * d) for d in range(2)]
    s_gla = [at(6, DV, 2048 + 256 * i) for i in range(8)]
    sm = [[[at(7 if d == 0 else 4, DV, 256 * (4 * h + c)) for c in range(TT)] for h in range(HEADS)]
          for d in range(2)]
    sc = tiles(3, TT, L, 2048)
    oT = tiles(2, DT)
    osq = tiles(3, 4)
    silu_r = tiles(5, DT)
    sga, sgb = tiles(6, DT), tiles(7, DT)
    vs_tok = tiles(8, TT, D)
    guT = tiles(4, DT)
    ln_g, ln_b = at(3, D), at(3, D, 1024)
    w_sT = tiles(3, SGU_G, P, 2048)
    b_s = at(3, D, 3072)[0:1]
    gT = tiles(2, FT)
    pads = at(8, 4 * (ROWS + 2) * (GRID + 2)).rearrange("p (b y x) -> p b y x", b=4, y=ROWS + 2)
    acc = tiles(9, 4)
    sq5 = tiles(5, DT)
    exps = scratch[:, :].rearrange("p (k c j) -> p k c j", k=4, c=2)
    ada1_sums = [[scratch[:, BLK * (2 * n + i):BLK * (2 * n + i + 1)] for i in range(2)] for n in range(2)]
    work = [scratch[:, L * i:L * (i + 1)] for i in range(2)]
    rstd2 = tiles(9, 2, L, 2048)
    h_lo = split_tiles("h_lo", 1, DT)
    hm_hi, h_hi = split_tiles("hm_hi", 9, DT), split_tiles("h_hi", 5, DT)
    ob_hi, ob_lo = split_tiles("ob_hi", 8, DT), split_tiles("ob_lo", 2, DT)
    a_hi, a_lo = split_tiles("a_hi", 9, DT), split_tiles("a_lo", 4, DT)
    m_hi, m_lo = split_tiles("m_hi", 8, DT), split_tiles("m_lo", 6, DT)
    br_b_hi, ga_hi, u_hi, br_a_hi = (
        [split_at("mix_hi%d_%d" % (u, o), u, 8 * BLK, o) for o in (0, 2048)] for u in (6, 4, 5, 2))
    g_lo = split_tiles("g_lo", 2, FT)
    g_hi = [split_at("g_hi%d" % k, (5, 7, 8)[k // 8], L, L * (k % 8)) for k in range(FT)]
    sq1 = tiles(1, DT)
    up_hi = [split_at("up_hi%d_%d" % (u, o), u, 8 * BLK, o) for u in (7, 6) for o in (0, 2048)]

    x2T = tiles(1, DT)
    raw = at(0, 3 * (L + 2), 2048).rearrange("p (b t) -> p b t", b=3)
    pair_sum = tiles(5, 2)
    rT, rkT = tiles(8, HT), tiles(8, HT, L, 2048)
    rvT = tiles(9, HT)
    wdT, adT, gdT = (at(9, L, 2048 + L * i) for i in range(3))
    mixed = [tile[:, i, :] for tile in (rT, rkT, rvT) for i in range(4)] + [wdT, adT, gdT]
    lw = [tiles(6, TT, L, 2048), tiles(0, TT)]
    rv_tok = tiles(7, TT)
    nkkT = tiles(7, HT, L, 2048)
    kk_sq, kk_n = (tiles(5, 2, L, 1024 * i) for i in (1, 2))
    w0_row = at(5, 2 * L, 3072)[0:1]
    yT = tiles(2, HT)
    rw_a2, rw_g2 = (at(2, L, 2048 + L * i) for i in range(2))
    rw_w2 = tiles(3, 2)
    job_t, kd_sum = at(2, L, 3584), at(9, L, 3584)
    sets = []
    for s in range(2):
        base = 7168 * s
        sets.append(dict(
            nqb=at(3, 2048, base).rearrange("p (s a t) -> p s a t", s=8, a=2),
            mqk=at(3, 2048, base + 2048).rearrange("p (s a t) -> p s a t", s=8, a=2),
            g=at(3, 1024, base + 4096).rearrange("p (s t) -> p s t", s=8),
            ar=at(3, 1024, base + 5120).rearrange("p (c a t) -> p c a t", c=4, a=2),
            b_tok=at(3, 512, base + 6144).rearrange("p (c f) -> p c f", c=4),
            k_tok=at(3, 512, base + 6656).rearrange("p (c f) -> p c f", c=4)))
    X, Y = (at(0, 1024, 2048 + 1024 * i).rearrange("p (s t) -> p s t", s=8) for i in range(2))
    job_slot = ring[:, POSITION["hy_in", 1] % RING, :].rearrange("p (n t) -> p n t", n=4)
    aT, kdT, bkT = job_slot[:, 0, :], job_slot[:, 1, :], job_slot[:, 2:4, :]
    y_sq, gn_s = tiles(3, HT), tiles(5, 2)
    zT = tiles(4, HT)
    z_even = tiles(0, 2, L, 2048)
    hyT = tiles(3, 12)
    xv_tok, x1_tok = tiles(5, TT), tiles(5, TT, L, 2048)
    featsT = at(6, L)[0:33]
    fw1 = at(6, 64, 512)[0:33]
    fw23 = [at(6, 64, 576 + 64 * i)[0:64] for i in range(2)]
    fw4 = at(6, 2048, 704)[0:64].rearrange("p (o d n) -> p o d n", o=2, d=2)
    fsd = at(7, 2048)[0:64].rearrange("p (o d n) -> p o d n", o=2, d=2)
    filt_h, filt_k, filt_a = (at(7, L, 2048 + L * i)[0:64] for i in range(3))
    skip_row = at(6, 1024, 2816)[0:1]
    window = tiles(4, TT, L, 2048)
    ht = [[tiles((3, 8)[o], TT, L, 2048 * s) for s in range(2)] for o in range(2)]
    spectra = tiles(9, 8)
    dft_first = at(5, 2048).rearrange("p (s e k f) -> p s e k f", s=2, e=2, k=2)
    halves = tiles(5, 4, L, 2048)
    raw_h = at(8, 3 * (L + 2)).rearrange("p (b t) -> p b t", b=3)
    dft, dftT = (at(6, 2048, 2048 * i).rearrange("p (s e k f) -> p s e k f", s=2, e=2, k=2) for i in range(2))
    Hcs = [[tiles((7, 3)[o], TT, L, 2048 * s) for s in range(2)] for o in range(2)]
    Ycs = [tiles(8, TT), tiles(8, TT, L, 2048)]
    prod = tiles(9, 8)
    gate_h, gate_r = tiles(0, DT), tiles(7, DT)
    lnc, lnsq = tiles(3, DT), tiles(4, DT)
    gT2 = tiles(3, FT)
    silu_g = tiles(6, 4)
    m2_hi, m2_lo = split_tiles("m2_hi", 5, DT), split_tiles("m2_lo", 0, DT)
    out_hi = [split_at("out_hi%d" % o, 8, 8 * BLK, o) for o in (0, 2048)]
    x2_hi, x2_lo = split_tiles("x2_hi", 6, DT), split_tiles("x2_lo", 3, DT)
    x_hi, x_lo = split_tiles("x_hi", 0, DT), split_tiles("x_lo", 2, DT)
    g2_lo = split_tiles("g2_lo", 3, FT)
    g2_hi = [split_at("g2_hi%d" % k, (0, 2, 7)[k // 8], L, L * (k % 8)) for k in range(FT)]
    up2_hi = [split_at("up2_hi%d_%d" % (u, o), u, 8 * BLK, o) for u in (7, 8) for o in (0, 2048)]
    norm_s, res_sum = tiles(9, 2), at(9, L, 1024)

    block = ctx.enter_context(nc.Block())
    bank_of, block_done = {}, {}
    bank_user = {}
    order = [(0, 1, 2, 3), (3, 2, 1, 0)]
    JOBS = [(hp, d) for hp in range(HT) for d in range(2)]
    LO, HI = slice(0, 64), slice(64, 128)

    def sums_of(name, b):
        return (b - (b > 2) - (b > 5)) % 2 if name == "ada1" else b % 2

    def bank(*name):
        return banks[:, bank_of[name], :]

    @block.tensor
    def _(pe):
        taken = [0]

        def take(*name):
            b = taken[0] % BANKS
            taken[0] += 1
            if b in bank_user:
                pe.wait_ge(*after(*("free",) + bank_user[b]))
            bank_user[b] = name
            bank_of[name] = b
            return banks[:, b, :]

        def weights(name, i, memory=ring):
            n = POSITION[name, i]
            pe.wait_ge(*after("block", n))
            return memory[:, n % RING, :].rearrange("p (k c) -> p k c", c=BLK)

        def weights_done(name, i, *group):
            block_done[POSITION[name, i]] = ("psum",) + group

        def linear(name, b, rhs, rhs_ready, group, tiles_of=(0, 1), kt=DT):
            w = weights(name, b)
            for j in tiles_of:
                t = 2 * b + j
                ps = take(group, t)
                for k in range(kt):
                    pe.wait_ge(*after(rhs_ready, k))
                    mm = pe.matmul(ps, w[:, k, j * P:(j + 1) * P], rhs[:, k, :], start=k == 0, stop=k == kt - 1)
                mm.then_inc(*psum_full.did("psum", group, t))
            weights_done(name, b, group, t)

        def feature_sum(group, src, ready, weight, n=L, kt=DT):
            pe.wait_ge(*after("consts"))
            ps = take(group)
            for k in range(kt):
                pe.wait_ge(*after(ready, k))
                mm = pe.matmul(ps[:, 0:n], weight, src[:, k, :], start=k == 0, stop=k == kt - 1)
            mm.then_inc(*psum_full.did("psum", group))

        def tile_sum(group, tile, ready):
            ps = take(group)
            pe.wait_ge(*after(ready))
            pe.matmul(ps, ones, tile, start=True, stop=True).then_inc(*psum_full.did("psum", group))

        def split_linear(name, n, parts, hi, lo, ready, group, first):
            w_lo = weights(name, n, ring_split)
            w_hi = parts[n % len(parts)].rearrange("p (k c) -> p k c", c=BLK)
            pe.wait_ge(*after("w_hi", name, n))
            pe.wait_ge(*after("w_lo", name, n))
            for j in range(2):
                ps = take(group, first + j)
                cut = slice(j * P, (j + 1) * P)
                for k in range(DT):
                    pe.wait_ge(*after(ready + "_hi", k))
                    pe.wait_ge(*after(ready + "_lo", k))
                    x_high, x_low = hi[:, k, :], lo[:, k, :]
                    pe.matmul(ps, w_hi[:, k, cut], x_high, start=k == 0, stop=False)
                    pe.matmul(ps, w_hi[:, k, cut], x_low, start=False, stop=False)
                    mm = pe.matmul(ps, w_lo[:, k, cut], x_high, start=False, stop=k == DT - 1)
                mm.then_inc(*psum_full.did("psum", group, first + j))
            weights_done(name, n, group, first + 1)

        def split_token_major(name, n, parts, hi, lo, ready):
            w_lo = weights(name, n, ring_split)
            w_hi = parts[n % len(parts)].rearrange("p (k c) -> p k c", c=BLK)
            pe.wait_ge(*after("w_hi", name, n))
            pe.wait_ge(*after("w_lo", name, n))
            pe.wait_ge(*after(ready + "_hi", DT - 1))
            pe.wait_ge(*after(ready + "_lo", DT - 1))
            for half in range(2):
                ps = take(name, n, half)
                for i in range(2):
                    cut = slice((2 * half + i) * P, (2 * half + i + 1) * P)
                    out = ps[:, i * BLK:(i + 1) * BLK]
                    for k in range(DT):
                        pe.matmul(out, hi[:, k, cut], w_hi[:, k, :], start=k == 0, stop=False)
                        pe.matmul(out, hi[:, k, cut], w_lo[:, k, :], start=False, stop=False)
                        mm = pe.matmul(out, lo[:, k, cut], w_hi[:, k, :], start=False, stop=k == DT - 1)
                mm.then_inc(*psum_full.did("psum", name, n, half))
            weights_done(name, n, name, n, 1)

        def filter_layer(n):
            fw, src = ((fw1, featsT), (fw23[0], filt_h), (fw23[1], filt_h))[n]
            ps = take("filt", n)
            pe.wait_ge(*after("filters"))
            if n:
                pe.wait_ge(*after("filt_h", n - 1))
            pe.matmul(ps[0:64, :], fw, src, start=True, stop=True).then_inc(*psum_full.did("psum", "filt", n))

        def filters(o):
            for sd in range(2):
                for tt in range(TT):
                    pe.wait_ge(*after("fsd", o, sd))
                    pe.wait_ge(*after("filt_h", 2))
                    ps = take("hf", o, sd, tt)
                    pe.matmul(ps, filt_h[:, tt * P:(tt + 1) * P], fsd[:, o, sd, :], start=True, stop=True).then_inc(
                        *psum_full.did("psum", "hf", o, sd, tt))

        def filter_spectrum(o, sd):
            pe.wait_ge(*after("dft_first"))
            for q in range(2):
                for e in range(2):
                    ps = take("H", o, sd, q, e)
                    for k in range(2):
                        pe.wait_ge(*after("ht", o, sd, 2 * e + k))
                        mm = pe.matmul(ps, dft_first[:, sd, e, k, q * P:(q + 1) * P], ht[o][sd][:, 2 * e + k, :],
                                       start=k == 0, stop=k == 1)
                    mm.then_inc(*psum_full.did("psum", "H", o, sd, q, e))

        def modulation(name, b, vectors):
            ps = take(name, b)
            for n, sums in enumerate(vectors):
                pe.wait_ge(*after(name + "_sums", b, n))
                for j in range(2):
                    mm = pe.matmul(ps[:, 2 * n + j:2 * n + j + 1], sums[sums_of(name, b)][:, j * P:(j + 1) * P],
                                   ones[:, 0:1], start=True, stop=True)
            mm.then_inc(*psum_full.did("psum", name, b))

        def modulation_whole(name, b):
            w = weights(name, b)
            ps = take(name, b)
            pe.wait_ge(*after("csil"))
            for j in range(2):
                for k in range(DT):
                    mm = pe.matmul(ps[:, j:j + 3:2], w[:, k, j * P:(j + 1) * P], csil[:, k, :],
                                   start=k == 0, stop=k == DT - 1)
            mm.then_inc(*psum_full.did("psum", name, b))
            weights_done(name, b, name, b)

        filter_layer(0)
        feature_sum("ss_c", sqc, "sqc", ones, LC)
        filter_layer(1)
        feature_sum("ss_x", sq, "sq", ones)
        filter_layer(2)
        filters(0)
        filter_spectrum(0, 0)
        modulation("ada1", 0, ada1_sums)
        filters(1)
        modulation_whole("ada1", 2)
        filter_spectrum(0, 1)
        modulation("ada1", 1, ada1_sums)
        filter_spectrum(1, 0)
        modulation_whole("ada1", 5)
        modulation("ada1", 3, ada1_sums)
        filter_spectrum(1, 1)
        for b in (4, 6, 7):
            modulation("ada1", b, ada1_sums)

        pe.wait_ge(*after("masks"))
        ada2_next = [0]

        def later_modulation():
            b = ada2_next[0]
            ada2_next[0] += 1
            if 0 <= b - 1 < ADA_REST:
                modulation("ada2", b - 1, [ada_sums])

        def token_major(group, w, b, src, half):
            ps = take(group, b, half)
            for i in range(2):
                tt = 2 * half + i
                for k in range(DT):
                    mm = pe.matmul(ps[:, i * BLK:(i + 1) * BLK], src[:, k, tt * P:(tt + 1) * P], w[:, k, :],
                                   start=k == 0, stop=k == DT - 1)
            mm.then_inc(*psum_full.did("psum", group, b, half))

        def keys(b):
            w = weights("k", b)
            for j in range(2):
                t = 2 * b + j
                for group, src, n in (("kc", hcT, LC), ("k", hT, L)):
                    ps = take(group, t)
                    for k in range(DT):
                        mm = pe.matmul(ps[:, 0:n], w[:, k, j * P:(j + 1) * P], src[:, k, :],
                                       start=k == 0, stop=k == DT - 1)
                    mm.then_inc(*psum_full.did("psum", group, t))
            weights_done("k", b, "k", t)
            later_modulation()

        def values(b):
            w = weights("v", b)
            token_major("vc", w, b, hcT, 0)
            token_major("v", w, b, hT, 0)
            token_major("v", w, b, hT, 1)
            weights_done("v", b, "v", b, 1)
            later_modulation()

        def gates(group, d, low_rank, chunks):
            for tt in range(chunks):
                ps = take(group, d, tt)
                pe.matmul(ps, low_rank[:, tt * P:(tt + 1) * P], gla_w2[:, d, :], start=True, stop=True).then_inc(
                    *psum_full.did("psum", group, d, tt))

        def cumulate(group, log_decay, ready, d, cps):
            for h in range(HEADS):
                for cp in range(cps):
                    ps = take(group, d, h, cp)
                    for i in range(2):
                        c = 2 * cp + i
                        pe.wait_ge(*after(ready, d, c))
                        mm = pe.matmul(ps[:, i * CUM:(i + 1) * CUM], log_decay[d][:, c, h * P:(h + 1) * P],
                                       gla_cum[d], start=True, stop=True)
                    mm.then_inc(*psum_full.did("psum", group, d, h, cp))

        def key_tokens(group, src, ready, chunks):
            for d in range(2):
                for c in range(chunks):
                    ps = take(group, d, c)
                    for h in range(HEADS):
                        pe.wait_ge(*after(ready, d, h, c // 2))
                        mm = pe.transpose(ps[:, h * P:(h + 1) * P], src[d][:, h, c * P:(c + 1) * P], ident)
                    mm.then_inc(*psum_full.did("psum", group, d, c))

        def scores(c):
            for d in range(2):
                ps = take("sc", d, c)
                for h in range(HEADS):
                    pe.wait_ge(*after("k_inv", d, h, c // 2))
                    mm = pe.matmul(ps[:, h * P:(h + 1) * P], k_inv[d][:, h, c * P:(c + 1) * P],
                                   q_dec[d][:, h, c * P:(c + 1) * P], start=True, stop=True)
                mm.then_inc(*psum_full.did("psum", "sc", d, c))

        def added(step, hp):
            for d in range(2):
                if step < 2:
                    c = (step, 1 - step)[d]
                    keys, vals = kc_tok[d], vc_tok
                    pe.wait_ge(*after("kc_tok", d, c))
                    pe.wait_ge(*after("vc_tok", 2 * hp + 1))
                else:
                    c = order[d][step - 2]
                    keys, vals = k_tok[d], v_tok
                    pe.wait_ge(*after("k_tok", d, c))
                    pe.wait_ge(*after("v_tok", 2 * hp + 1))
                ps = take("su", step, d, hp)
                for i in range(2):
                    h = 2 * hp + i
                    mm = pe.matmul(ps[:, i * DV:(i + 1) * DV], keys[:, c, h * P:(h + 1) * P],
                                   vals[:, c, h * DV:(h + 1) * DV], start=True, stop=True)
                mm.then_inc(*psum_full.did("psum", "su", step, d, hp))

        w = weights("lr", 0)
        for group, src, ready, n in (("lrc", hcT, "hcT", LC), ("lr", hT, "hT", L)):
            ps = take(group)
            for k in range(DT):
                pe.wait_ge(*after(ready, k))
                mm = pe.matmul(ps[0:32, 0:n], w[:, k, 0:32], src[:, k, :], start=k == 0, stop=k == DT - 1)
            mm.then_inc(*psum_full.did("psum", group))
        weights_done("lr", 0, "lr")
        later_modulation()
        keys(0)
        pe.wait_ge(*after("gla_w2"))
        pe.wait_ge(*after("lrcT"))
        pe.wait_ge(*after("lrT"))
        pe.wait_ge(*after("lr_ones"))
        gates("zc", 0, lrcT, TC)
        gates("zc", 1, lrcT, TC)
        keys(1)
        gates("z", 0, lrT, TT)
        linear("q", 0, hT, "hT", "q")
        later_modulation()
        gates("z", 1, lrT, TT)
        linear("q", 1, hT, "hT", "q")
        later_modulation()
        for d in range(2):
            cumulate("cumc", lac, "lac", d, 1)
        values(0)
        cumulate("cum", la, "la", 0, 2)
        values(1)
        cumulate("cum", la, "la", 1, 2)
        values(2)
        key_tokens("ktc", kc_inv, "kc_inv", TC)
        scores(0)
        w = weights("v", 3)
        token_major("vc", w, 3, hcT, 0)
        key_tokens("kt", k_inv, "k_inv", TT)
        scores(1)
        for step in range(2):
            added(step, 0)
            added(step, 1)
        token_major("v", w, 3, hT, 0)
        added(2, 0)
        added(3, 0)
        scores(2)
        token_major("v", w, 3, hT, 1)
        weights_done("v", 3, "v", 3, 1)
        later_modulation()
        added(4, 0)
        added(2, 1)
        scores(3)
        added(3, 1)
        added(4, 1)

        def out_sum(h):
            ps = take("oss", h)
            for vt in range(2):
                pe.wait_ge(*after("osq", 2 * h + vt))
                mm = pe.matmul(ps, ones, osq[:, (2 * h + vt) % 4, :], start=vt == 0, stop=vt == 1)
            mm.then_inc(*psum_full.did("psum", "oss", h))

        for h in range(HEADS):
            for vt in range(2):
                ps = take("o", 2 * h + vt)
                vcols = slice(h * DV + vt * P, h * DV + (vt + 1) * P)
                for c in range(TT):
                    pe.wait_ge(*after("sc", c))
                    pe.wait_ge(*after("sm", 0, h, c))
                    pe.wait_ge(*after("sm", 1, h, c))
                    out = ps[:, c * P:(c + 1) * P]
                    pe.matmul(out, v_tok[:, c, vcols], sc[:, c, h * P:(h + 1) * P], start=True, stop=False)
                    for d in range(2):
                        mm = pe.matmul(out, sm[d][h][c][:, vt * P:(vt + 1) * P], q_dec[d][:, h, c * P:(c + 1) * P],
                                       start=False, stop=d == 1)
                mm.then_inc(*psum_full.did("psum", "o", 2 * h + vt))
            if h >= 1:
                out_sum(h - 1)
        for b in range(4):
            linear("r", b, hT, "hT", "r")
            later_modulation()
            if b == 0:
                out_sum(HEADS - 1)
        for b in range(4):
            linear("gb", b, hT, "hT", "gb")
            later_modulation()
        for b in range(4):
            split_linear("br_b", b, br_b_hi, ob_hi, ob_lo, "ob", "br_b", 2 * b)
        for b in range(4):
            split_linear("ga", b, ga_hi, hm_hi, h_lo, "hm", "ga", 2 * b)

        for b in range(4):
            split_token_major("vs", b, ga_hi, hm_hi, h_lo, "hm")
        for b in range(4):
            split_linear("u", b, u_hi, hm_hi, h_lo, "hm", "u", 2 * b)
        pe.wait_ge(*after("w_s"))
        pe.wait_ge(*after("b_s"))
        pe.wait_ge(*after("ones_row"))
        for g in range(SGU_G):
            ps = take("s", g)
            pe.matmul(ps, ones_row, b_s[:, g * P:(g + 1) * P].unsqueeze(1).to_broadcast([1, TT, P]), start=True,
                      stop=False)
            for n in range(TT):
                pe.wait_ge(*after("vn", n))
                mm = pe.matmul(ps[:, n * P:(n + 1) * P], vs_tok[:, n, g * P:(g + 1) * P], w_sT[:, g, :],
                               start=False, stop=n == TT - 1)
            mm.then_inc(*psum_full.did("psum", "s", g))
        for b in range(4):
            split_linear("br_a", b, br_a_hi, a_hi, a_lo, "aT", "br_a", 2 * b)
        for b in range(4):
            split_linear("w_o", b, br_a_hi, m_hi, m_lo, "merged", "w_o", 2 * b)

        tile_sum("ss2", sq5[:, 0, :], "sq2_sum")

        for b in range(FT // 2):
            split_linear("up", 2 * b, up_hi, h_hi, h_lo, "h2", "fa", 2 * b)
            split_linear("up", 2 * b + 1, up_hi, h_hi, h_lo, "h2", "fv", 2 * b)

        def down(name, parts, hi, lo, ready):
            for b in range(4):
                ps = [take(name, 2 * b + j) for j in range(2)]
                for part in range(3):
                    n = 3 * b + part
                    w_lo = weights(name, n, ring_split)
                    w_hi = parts[n % 2].rearrange("p (k c) -> p k c", c=BLK)
                    pe.wait_ge(*after("w_hi", name, n))
                    pe.wait_ge(*after("w_lo", name, n))
                    kt = min(8, FT - 8 * part)
                    for j in range(2):
                        cut = slice(j * P, (j + 1) * P)
                        for k in range(kt):
                            if n < 3:
                                pe.wait_ge(*after(ready + "_hi", 8 * part + k))
                                pe.wait_ge(*after(ready + "_lo", 8 * part + k))
                            high, low = hi[8 * part + k], lo[:, 8 * part + k, :]
                            pe.matmul(ps[j], w_hi[:, k, cut], high, start=part == 0 and k == 0, stop=False)
                            pe.matmul(ps[j], w_hi[:, k, cut], low, start=False, stop=False)
                            mm = pe.matmul(ps[j], w_lo[:, k, cut], high, start=False,
                                           stop=part == 2 and k == kt - 1)
                        if part == 2:
                            mm.then_inc(*psum_full.did("psum", name, 2 * b + j))
                    if part < 2:
                        mm.then_inc(*psum_full.did("psum", name, "part", b, part))
                        weights_done(name, n, name, "part", b, part)
                weights_done(name, 3 * b + 2, name, 2 * b + 1)

        down("down", up_hi[2:], g_hi, g_lo, "gT")
        tile_sum("ss3", sq1[:, 0, :], "sq3_sum")

        def key_norms(hps):
            for hp in hps:
                ps = take("kk", hp)
                pe.wait_ge(*after("kk_sq", hp))
                pe.matmul(ps, headones, kk_sq[:, hp % 2, :], start=True, stop=True).then_inc(
                    *psum_full.did("psum", "kk", hp))

        def rwkv_projection(i):
            b = RW_ORDER[i]
            w = weights("rw_in", i)
            for t in (2 * b, 2 * b + 1):
                if t < 15:
                    ps = take("rw", t)
                    for k in range(DT):
                        pe.wait_ge(*after("x2T", k))
                        mm = pe.matmul(ps, w[:, k, (t % 2) * P:(t % 2 + 1) * P], x2T[:, k, :],
                                       start=k == 0, stop=k == DT - 1)
                    mm.then_inc(*psum_full.did("psum", "rw", t))
                    last = t
                if t in (0, 1):
                    key_norms((2 * t, 2 * t + 1))
            weights_done("rw_in", i, "rw", last)
            if i in (2, 3):
                d = i - 2
                pe.wait_ge(*after("wd_tanh"))
                pe.wait_ge(*after("rw_w2"))
                pe.wait_ge(*after("w0"))
                for tt in range(TT):
                    ps = take("w", d, tt)
                    pe.matmul(ps, wdT[:, tt * P:(tt + 1) * P], rw_w2[:, d, :], start=True, stop=False)
                    pe.matmul(ps, ones_row, w0_row[:, d * L:(d + 1) * L], start=False, stop=True).then_inc(
                        *psum_full.did("psum", "w", d, tt))

        for i in range(7):
            rwkv_projection(i)

        def inputs(j):
            hp, d = JOBS[j]
            ps = take("a", j)
            rows = (LO, HI)[d]
            pe.wait_ge(*after("mixed", 13))
            pe.matmul(ps, rw_a2[rows, hp * P:(hp + 1) * P], adT[rows, :], start=True, stop=True).then_inc(
                *psum_full.did("psum", "a", j))
            for cp in range(2):
                ps = take("rcum", j, cp)
                for i in range(2):
                    c = 2 * cp + i
                    pe.wait_ge(*after("lw", d, c))
                    mm = pe.matmul(ps[:, i * CUM:(i + 1) * CUM], lw[d][:, c, hp * P:(hp + 1) * P], rw_cum[d],
                                   start=True, stop=True)
                mm.then_inc(*psum_full.did("psum", "rcum", j, cp))

        def tokens(j):
            for what, i in (("job_b", 0), ("job_k", 1)):
                ps = take("tok", j, i)
                pe.wait_ge(*after(what, j))
                for c in range(TT):
                    mm = pe.transpose(ps[:, c * P:(c + 1) * P], bkT[:, i, c * P:(c + 1) * P], ident)
                mm.then_inc(*psum_full.did("psum", "tok", j, i))

        def gram(j, i, cp):
            s = sets[j % 2]
            pe.wait_ge(*after("job_a", j))
            pe.wait_ge(*after("job_r", j))
            for h in range(2):
                ps = take("gram", j, i, cp, h)
                rows = (LO, HI)[h]
                for n in range(2):
                    c = 2 * cp + n
                    mm = pe.matmul(ps[:, n * 2 * P:(n + 1) * 2 * P], bkT[rows, i, c * P:(c + 1) * P],
                                   s["ar"][rows, c, :, :], start=True, stop=True)
                mm.then_inc(*psum_full.did("psum", "gram", j, i, cp, h))

        def bonus(j):
            hp, d = JOBS[j]
            if d == 1:
                ps = take("bonus", hp)
                pe.wait_ge(*after("bonus_in", hp))
                pe.matmul(ps, headones, kd_sum, start=True, stop=True).then_inc(*psum_full.did("psum", "bonus", hp))

        def inverse_start(j, half):
            ps = take("x0", j, half)
            pe.wait_ge(*after("g0", j))
            for i in range(4):
                mm = pe.transpose(ps[:, i * P:(i + 1) * P], sets[j % 2]["g"][:, 4 * half + i, :], ident)
            mm.then_inc(*psum_full.did("psum", "x0", j, half))

        def invert_y(j, lv, half):
            s = sets[j % 2]
            ps = take("iy", j, lv, half)
            pe.wait_ge(*after("x", j, lv, half))
            pe.wait_ge(*after("lt", j))
            for i in range(4):
                n = 4 * half + i
                mm = pe.matmul(ps[:, i * P:(i + 1) * P], s["nqb"][:, n, 0, :], X[:, n, :], start=True, stop=True)
            mm.then_inc(*psum_full.did("psum", "iy", j, lv, half))

        def invert_xg(j, lv, half):
            s = sets[j % 2]
            pe.wait_ge(*after("yi", j, lv, half))
            pe.wait_ge(*after(*(("g", j, lv, half) if lv else ("g0", j))))
            for what in ("ix", "ig"):
                ps = take(what, j, lv, half)
                for i in range(4):
                    n = 4 * half + i
                    out = ps[:, i * P:(i + 1) * P]
                    if what == "ix":
                        d = JOBS[j][1]
                        part = slice(0, P) if lv < 4 else (LO, HI)[d]
                        mm = pe.matmul(out[:, part], s["g"][:, n, :], Y[:, n, part], start=True, stop=True)
                    else:
                        mm = pe.matmul(out, Y[:, n, :], s["g"][:, n, :], start=True, stop=True)
                mm.then_inc(*psum_full.did("psum", what, j, lv, half))

        def invert_last(j, stage):
            s = sets[j % 2]
            d = JOBS[j][1]
            first, second = (LO, HI) if d == 0 else (HI, LO)
            ps = take("il", j, stage)
            if stage == 0:
                pe.wait_ge(*after("x", j, 5, 0))
                pe.wait_ge(*after("x", j, 5, 1))
                for n in range(8):
                    mm = pe.matmul(ps[second, n * 64:(n + 1) * 64], s["nqb"][first, n, 0, second],
                                   X[first, n, first], start=True, stop=True)
            else:
                pe.wait_ge(*after("y_last", j))
                pe.wait_ge(*after("g", j, 5, 0))
                pe.wait_ge(*after("g", j, 5, 1))
                for n in range(8):
                    mm = pe.matmul(ps[first, n * 64:(n + 1) * 64], Y[second, n, first], s["g"][second, n, second],
                                   start=True, stop=True)
            mm.then_inc(*psum_full.did("psum", "il", j, stage))

        def chain_u(j, step):
            hp, d = JOBS[j]
            s = sets[j % 2]
            c = order[d][step]
            pe.wait_ge(*after("rv_tok", c))
            ps = take("cu", j, step)
            for h in range(2):
                out = ps[:, h * 64:(h + 1) * 64]
                mm = pe.matmul(out, s["mqk"][:, 2 * c + h, 0, :], rv_tok[:, c, hp * P + h * 64:hp * P + (h + 1) * 64],
                               start=step == 0 or h == 0, stop=step == 0)
            if step:
                pe.wait_ge(*after("state_m", j, step))
                mm = pe.matmul(ps[:, 0:P], s["ar"][:, c, 0, :], state_m, start=False, stop=True)
            mm.then_inc(*psum_full.did("psum", "cu", j, step))

        def chain_sa(j, step):
            s = sets[j % 2]
            c = order[JOBS[j][1]][step]
            pe.wait_ge(*after("u", j, step))
            pe.wait_ge(*after("g_done", j))
            ps = take("cs", j, step)
            for h in range(2):
                mm = pe.matmul(ps[:, h * 64:(h + 1) * 64], s["g"][:, 2 * c + h, :], ub[:, h, :], start=True, stop=True)
            mm.then_inc(*psum_full.did("psum", "cs", j, step))

        def chain_out(j, step):
            hp, d = JOBS[j]
            s = sets[j % 2]
            c = order[d][step]
            pe.wait_ge(*after("sa", j, step))
            if step < 3:
                ps = take("ch", j, step)
                for h in range(2):
                    rows = (LO, HI)[h]
                    pe.matmul(ps[rows, 0:64], s["b_tok"][:, c, rows], sab[:, h, :], start=True, stop=False)
                    mm = pe.matmul(ps[rows, 0:64], s["k_tok"][:, c, rows],
                                   rv_tok[:, c, hp * P + h * 64:hp * P + (h + 1) * 64], start=False, stop=True)
                mm.then_inc(*psum_full.did("psum", "ch", j, step))
            ps = take("cy", j, step)
            for h in range(2):
                rows = (LO, HI)[h]
                out = ps[rows, 0:P]
                pe.matmul(out, sab[:, h, :], s["nqb"][:, 2 * c + h, 1, :], start=True, stop=False)
                mm = pe.matmul(out, rv_tok[:, c, hp * P + h * 64:hp * P + (h + 1) * 64],
                               s["mqk"][:, 2 * c + h, 1, :], start=False, stop=step == 0)
            if step:
                mm = pe.matmul(ps[:, 0:P], state_m, s["ar"][:, c, 1, :], start=False, stop=True)
            mm.then_inc(*psum_full.did("psum", "cy", j, step))

        inputs(0)
        rwkv_projection(7)
        for c in range(TT):
            ps = take("vt", c)
            for hp in range(HT):
                pe.wait_ge(*after("mixed", 8 + hp))
                mm = pe.transpose(ps[:, hp * P:(hp + 1) * P], rvT[:, hp, c * P:(c + 1) * P], ident)
            mm.then_inc(*psum_full.did("psum", "vt", c))
        tokens(0)
        gram(0, 0, 0)
        gram(0, 0, 1)
        for j in range(len(JOBS) + 1):
            new, old, ahead = j < len(JOBS), j > 0, j + 1 < len(JOBS)
            if old:
                chain_u(j - 1, 0)
            if new:
                gram(j, 1, 0)
            if old:
                chain_sa(j - 1, 0)
            if new:
                gram(j, 1, 1)
                inverse_start(j, 0)
                bonus(j)
                inverse_start(j, 1)
            if old:
                chain_out(j - 1, 0)
            if ahead:
                inputs(j + 1)
            for lv in range(5):
                chained = old and lv < 3
                if new:
                    for half in range(2):
                        invert_y(j, lv, half)
                if chained:
                    chain_u(j - 1, lv + 1)
                if new:
                    invert_xg(j, lv, 0)
                if chained:
                    chain_sa(j - 1, lv + 1)
                if new:
                    invert_xg(j, lv, 1)
                if chained:
                    chain_out(j - 1, lv + 1)
            if new:
                invert_last(j, 0)
            if ahead:
                tokens(j + 1)
                gram(j + 1, 0, 0)
            if new:
                invert_last(j, 1)
            if ahead:
                gram(j + 1, 0, 1)

        for hp in range(HT):
            ps = take("ym", hp)
            pe.wait_ge(*after("y", 2 * hp + 1))
            pe.matmul(ps, headones, yT[:, hp, :], start=True, stop=True).then_inc(*psum_full.did("psum", "ym", hp))
        for hp in range(HT):
            ps = take("yv", hp)
            pe.wait_ge(*after("y_sq", hp))
            pe.matmul(ps, headones, y_sq[:, hp, :], start=True, stop=True).then_inc(*psum_full.did("psum", "yv", hp))
        pe.wait_ge(*after("gd_sig"))
        for hp in range(HT):
            ps = take("g", hp)
            pe.matmul(ps, rw_g2[:, hp * P:(hp + 1) * P], gdT, start=True, stop=True).then_inc(
                *psum_full.did("psum", "g", hp))

        for b in range(6):
            linear("hy_in", b, x2T, "x2T", "hy")
        for what, dst in (("hvt", 0), ("hxt", 4)):
            for c in range(TT):
                ps = take(what, c)
                for i in range(HT):
                    pe.wait_ge(*after("hyT", dst + i))
                    first = (c % 2) * 2 * P + c // 2
                    mm = pe.transpose(ps[:, i * P:(i + 1) * P], hyT[:, dst + i, first:first + 2 * P - 1:2], ident)
                mm.then_inc(*psum_full.did("psum", what, c))
        pe.wait_ge(*after("dft"))
        for o in range(2):
            z, ready = xv_tok, (lambda k: ("xv_tok", k)) if o == 0 else (lambda k: ("z2", k))
            for q in range(2):
                for cs in range(2):
                    for e in range(2):
                        ps = take("Z", o, cs, q, e)
                        for k in range(2):
                            pe.wait_ge(*after(*ready(2 * e + k)))
                            mm = pe.matmul(ps, dft[:, cs, e, k, q * P:(q + 1) * P], z[:, 2 * e + k, :],
                                           start=k == 0, stop=k == 1)
                        mm.then_inc(*psum_full.did("psum", "Z", o, cs, q, e))
            linear("gates", o, x2T, "x2T", "gate")
            for tt in range(TT):
                ps = take("conv", o, tt)
                for e in range(2):
                    for cs in range(2):
                        for k in range(2):
                            pe.wait_ge(*after("Y", o, cs, 2 * e + k))
                            if o == 0 and e == tt // 2:
                                cols_of = slice((tt % 2) * P, (tt % 2 + 1) * P)
                                mm = pe.matmul(ps, dftT[:, cs, e, k, cols_of], Ycs[cs][:, 2 * e + k, :],
                                               start=cs == 0 and k == 0, stop=cs == 1 and k == 1)
                            if o == 1:
                                mm = pe.matmul(ps[:, e * 2 * P:(e + 1) * 2 * P],
                                               Ycs[cs][:, 2 * e + k, tt * P:(tt + 1) * P],
                                               dftT[:, cs, e, k, :], start=cs == 0 and k == 0, stop=cs == 1 and k == 1)
                mm.then_inc(*psum_full.did("psum", "conv", o, tt))

        for b in (2, 3):
            linear("gates", b, x2T, "x2T", "gate")
        for b in range(4, 8):
            split_linear("gates", b, out_hi, x2_hi, x2_lo, "x2T", "gate", 2 * b)

        def half_width(name, group, src, ready):
            for b in range(2):
                n = POSITION[name, b]
                pe.wait_ge(*after("block", n))
                w = ring[:, n % RING, :].rearrange("p (k c) -> p k c", c=2 * BLK)
                for j in range(4):
                    ps = take(group, 4 * b + j)
                    for k in range(HT):
                        pe.wait_ge(*after(ready, k))
                        mm = pe.matmul(ps, w[:, k, j * P:(j + 1) * P], src[:, k, :], start=k == 0, stop=k == HT - 1)
                    mm.then_inc(*psum_full.did("psum", group, 4 * b + j))
                weights_done(name, b, group, 4 * b + j)

        half_width("rw_out", "rwo", yT, "yT")
        half_width("hy_out", "hyo", zT, "zT")
        for b in range(4):
            split_linear("w_o2", b, out_hi, m2_hi, m2_lo, "merged2", "w_o2", 2 * b)
        tile_sum("lm0", res_sum, "res0_sum")
        feature_sum("lv0", lnsq, "lnsq0", ones)
        for b in range(FT // 2):
            split_linear("up2", 2 * b, up2_hi, x_hi, x_lo, "x3", "fg", 2 * b)
            split_linear("up2", 2 * b + 1, up2_hi, x_hi, x_lo, "x3", "fu", 2 * b)
        down("down2", up2_hi[2:], g2_hi, g2_lo, "gT2")
        tile_sum("lm1", res_sum, "res1_sum")
        feature_sum("lv1", lnsq, "lnsq1", ones)

    @block.vector
    def _(dve):
        V = nc.vector

        def mul(out, a, b):
            return V.tensor_tensor(out, a, b, ALU.mult)

        def stt(out, a, scalar, b, op0, op1):
            return V.scalar_tensor_tensor(out, a, scalar, b, op0, op1)

        def weights_left(name, n, parts):
            slot, left = [memory[:, POSITION[name, n] % RING, :] for memory in (ring, ring_split)]
            dve.wait_ge(*after("w_hi", name, n))
            V.tensor_tensor(left, slot, parts[n % len(parts)].bitcast(F32), ALU.subtract).then_inc(
                *now.did("w_lo", name, n))

        def tile_left(name, k, src, hi, lo):
            dve.wait_ge(*after(name + "_hi", k))
            V.tensor_tensor(lo[:, k, :], src[:, k, :], hi[:, k, :].bitcast(F32), ALU.subtract).then_inc(
                *now.did(name + "_lo", k))

        def gate_values(t):
            dve.wait_ge(*after("gelu", t))
            dve.wait_ge(*after("psum", "fv", t))
            mul(gT[:, t, :], bank("fv", t), acc[:, t % 4, :]).then_inc(*now.both(("gT", t), ("free", "fv", t)))

        now = dve_in["start"]
        V.memset(eps_cols[:, 0:1], EPS).then_inc(*now.did())
        V.memset(eps_cols[:, 1:2], LN_EPS).then_inc(*now.did())
        V.memset(eps_cols[:, 2:3], GN_EPS).then_inc(*now.did())
        V.memset(eps_cols[:, 3:4], 1.0).then_inc(*now.did())
        V.memset(ones_row, 1.0).then_inc(*now.both(("eps",), ("ones_row",)))
        dve.wait_ge(*after("cols"))
        dve.wait_ge(*after("cols"))
        mul(filt_sb[0:64, :], cols[0:64, COL["filt_b"]:COL["filt_b"] + 3],
            cols[0:64, COL["filt_sf"]:COL["filt_sf"] + 3]).then_inc(*now.did("filt_sb"))
        turn = 2.0 * math.pi
        parts = [6.28125, 0.0019340515136718750, turn - 6.28125 - 0.0019340515136718750]
        magic = 1.5 * 2.0 ** 23

        def sine_argument(n):
            dve.wait_ge(now.sem, now.count)
            dve.wait_ge(*after("filt_a", n))
            V.tensor_scalar(filt_k, filt_a, 1.0 / turn, magic, ALU.mult, ALU.add).then_inc(*now.did("fk", n))
            dve.wait_ge(*after("fk", n))
            V.tensor_scalar(filt_k, filt_k, -magic, None, ALU.add).then_inc(*now.did("fr", n, -1))
            dve.wait_ge(*after("fr", n, -1))
            for i, part in enumerate(parts):
                stt(filt_a, filt_k, -part, filt_a, ALU.mult, ALU.add).then_inc(*now.did("fr", n, i))
                dve.wait_ge(*after("fr", n, i))
            V.tensor_scalar(filt_a, filt_a, 3.1415925, -3.1415925, ALU.min, ALU.max).then_inc(*now.did("filt_r", n))

        def filters(o):
            for sd in range(2):
                for tt in range(TT):
                    dve.wait_ge(*after("psum", "hf", o, sd, tt))
                    dve.wait_ge(*after("window"))
                    mul(ht[o][sd][:, tt, :], bank("hf", o, sd, tt), window[:, tt, :]).then_inc(
                        *now.both(("ht0" if (sd, tt) == (0, 0) else "ht", o, sd, tt), ("free", "hf", o, sd, tt)))
                    if (sd, tt) == (0, 0):
                        dve.wait_ge(*after("ht0", o, 0, 0))
                        dve.wait_ge(*after("skip"))
                        first = ht[o][0][0:1, 0, :]
                        V.tensor_tensor(first, first, skip_row[:, o * HW:(o + 1) * HW], ALU.add).then_inc(
                            *now.both(("ht", o, 0, 0), ("skip_added", o)))

        def inverse_rms(which, i, n):
            dve.wait_ge(*after("rms", which))
            V.reciprocal(rstd[:, i, 0:n], rstd[:, i, 0:n]).then_inc(*now.did("rstd", which))

        def modulation_sums(name, b, vectors):
            n = POSITION[name, b]
            w = ring[:, n % RING, :].rearrange("p (k c) -> p k c", c=BLK)
            dve.wait_ge(*after("block", n))
            dve.wait_ge(*after("csil"))
            for k in range(DT):
                for i, sums in enumerate(vectors):
                    out = sums[sums_of(name, b)]
                    if k:
                        dve.wait_ge(*after(name + "_part", b, i, k - 1))
                        stt(out, w[:, k, :], csil[:, k, i:i + 1], out, ALU.mult, ALU.add).then_inc(
                            *now.did(*(name + "_sums", b, i) if k == DT - 1 else (name + "_part", b, i, k)))
                    else:
                        V.tensor_scalar(out, w[:, k, :], csil[:, k, i:i + 1], None, ALU.mult).then_inc(
                            *now.did(name + "_part", b, i, k))
            block_done[n] = (name + "_sums", b, len(vectors) - 1)

        def modulation_columns(name, b, outs, first):
            dve.wait_ge(*after("psum", name, b))
            t = 2 * b
            for i, (out, what) in enumerate(outs):
                V.tensor_tensor(out[:, first + t:first + t + 2], bank(name, b)[:, 2 * i:2 * i + 2],
                                cols[:, COL["b_ada"] + first + t:COL["b_ada"] + first + t + 2], ALU.add).then_inc(
                    *now.both((what, b), *([("free", name, b)] if i == len(outs) - 1 else [])))

        sine_argument(0)
        dve.wait_ge(*after("filters_out"))
        for o in range(2):
            V.tensor_tensor(fsd[:, o, 0, :], fw4[:, o, 0, :], fw4[:, o, 1, :], ALU.add).then_inc(
                *now.did("fsd", o, 0))
            V.tensor_tensor(fsd[:, o, 1, :], fw4[:, o, 0, :], fw4[:, o, 1, :], ALU.subtract).then_inc(
                *now.did("fsd", o, 1))
        sine_argument(1)
        sine_argument(2)
        filters(0)
        modulation_sums("ada1", 0, ada1_sums)
        modulation_sums("ada1", 1, ada1_sums)
        first_columns = (mod, "mod"), (modc, "modc")
        modulation_columns("ada1", 0, first_columns, 0)
        filters(1)
        dve.wait_ge(now.sem, now.count)
        V.memset(lrcT[32:33, :], 1.0).then_inc(*now.did())
        V.memset(lrT[32:33, :], 1.0).then_inc(*now.did("lr_ones"))
        modulation_columns("ada1", 2, first_columns, 0)
        modulation_sums("ada1", 3, ada1_sums)
        modulation_columns("ada1", 1, first_columns, 0)
        modulation_sums("ada1", 4, ada1_sums)
        inverse_rms("c", 1, LC)
        modulation_columns("ada1", 5, first_columns, 0)
        modulation_columns("ada1", 3, first_columns, 0)
        modulation_sums("ada1", 6, ada1_sums)
        inverse_rms("x", 0, L)
        modulation_columns("ada1", 4, first_columns, 0)
        modulation_sums("ada1", 7, ada1_sums)
        modulation_columns("ada1", 6, first_columns, 0)
        modulation_columns("ada1", 7, first_columns, 0)
        g1 = cols[:, COL["norm1_g"]:COL["norm1_g"] + 8]
        dve.wait_ge(*after("modc", ADA_FIRST - 1))
        stt(gs1c, modc[:, 8:16], 1.0, g1, ALU.add, ALU.mult).then_inc(*now.did("gs1c"))
        stt(gs1, mod[:, 8:16], 1.0, g1, ALU.add, ALU.mult).then_inc(*now.did("gs1"))
        dve.wait_ge(*after("gs1c"))
        dve.wait_ge(*after("rstd", "c"))
        dve.wait_ge(*after("ctx"))
        for k in range(DT):
            stt(hcT[:, k, :], ctxT[:, k, :], gs1c[:, k:k + 1], rstd[:, 1, 0:LC], ALU.mult, ALU.mult).then_inc(
                *now.did("hcT_scaled", k))
        dve.wait_ge(*after("gs1"))
        dve.wait_ge(*after("rstd", "x"))
        dve.wait_ge(*after("x"))
        for k in range(DT):
            stt(hT[:, k, :], xT[:, k, :], gs1[:, k:k + 1], rstd[:, 0, :], ALU.mult, ALU.mult).then_inc(
                *now.did("hT_scaled", k))

        def later_modulation(b):
            modulation_sums("ada2", b, [ada_sums])
            if b:
                modulation_columns("ada2", b - 1, ((mod, "mod2"),), 16)

        now = dve_in["gla"]
        def log_sigmoid(group, out, d, chunks, first):
            for tt in range(chunks):
                dve.wait_ge(*after("soft", group, d, tt))
                stt(out[d][:, tt, :], bank(group, d, tt), 0.0, soft[(first + tt) % 8], ALU.min, ALU.subtract).then_inc(
                    *now.both(("la" if group == "z" else "lac", d, tt), ("free", group, d, tt)))

        exp_count = [0]

        def decayed(group, d, cps):
            inc = slice(1, P + 1) if d == 0 else slice(0, P)
            for h in range(HEADS):
                for cp in range(cps):
                    e = exp_count[0]
                    exp_count[0] += 1
                    plus, minus = exps[:, e % 2], exps[:, 2 + e % 2]
                    dve.wait_ge(*after("exp", group, d, h, cp))
                    st = stats_c if group == "cumc" else stats_x
                    V.tensor_copy(st[:, d, h, 2 * cp:2 * cp + 2, :], plus[:, :, P + 1:CUM]).then_inc(
                        *now.did("stats", group, d, h, cp))
                    span = slice(2 * cp * P, 2 * (cp + 1) * P)
                    src, dst = (kcT, kc_inv) if group == "cumc" else (kT, k_inv)
                    dve.wait_ge(*after("kcT" if group == "cumc" else "kT", h))
                    if group == "cum":
                        dve.wait_ge(*after("qT", h))
                        mul(q_dec[d][:, h, span].rearrange("p (c t) -> p c t", c=2),
                            qT[:, h, span].rearrange("p (c t) -> p c t", c=2), plus[:, :, inc]).then_inc(
                            *now.did("q_dec", d, h, cp))
                    mul(dst[d][:, h, span].rearrange("p (c t) -> p c t", c=2),
                        src[:, h, span].rearrange("p (c t) -> p c t", c=2), minus[:, :, 0:P]).then_inc(
                        *now.both(("kc_inv" if group == "cumc" else "k_inv", d, h, cp), ("exp_used", e)))

        def states(step, hp):
            for d in range(2):
                if step < 2:
                    c, st, group = (step, 1 - step)[d], stats_c, "cumc"
                else:
                    c, st, group = order[d][step - 2], stats_x, "cum"
                dve.wait_ge(*after("psum", "su", step, d, hp))
                ps = bank("su", step, d, hp)
                for i in range(2):
                    h = 2 * hp + i
                    s = s_gla[4 * d + h]
                    add = ps[:, i * DV:(i + 1) * DV]
                    freed = [("free", "su", step, d, hp)] if i else []
                    dve.wait_ge(*after("stats", group, d, h, c // 2))
                    if step == 0:
                        V.tensor_scalar(s, add, st[:, d, h, c, 2:3], None, ALU.mult).then_inc(
                            *now.both(("s", step, d, h), *freed))
                    else:
                        if step >= 2:
                            dve.wait_ge(*after("sm", d, h, order[d][step - 2]))
                        t = work[0][:, i * DV:(i + 1) * DV]
                        dve.wait_ge(now.sem, now.count)
                        V.tensor_scalar(t, add, st[:, d, h, c, 2:3], None, ALU.mult).then_inc(
                            *now.both(("s_add", step, d, h), *freed))
                        dve.wait_ge(*after("s_add", step, d, h))
                        stt(s, s, st[:, d, h, c, 1:2], t, ALU.mult, ALU.add).then_inc(*now.did("s", step, d, h))

        def scores(c):
            for d in range(2):
                dve.wait_ge(now.sem, now.count)
                dve.wait_ge(*after("psum", "sc", d, c))
                V.tensor_scalar(work[0], bank("sc", d, c), BIG, -BIG, ALU.min, ALU.max).then_inc(
                    *now.both(("clamped", d, c), ("free", "sc", d, c)))
                dve.wait_ge(*after("clamped", d, c))
                out = sc[:, c, :] if d == 0 else work[1]
                mul(out.rearrange("p (h t) -> p h t", h=4), work[0].rearrange("p (h t) -> p h t", h=4),
                    incl[d].unsqueeze(1).to_broadcast([P, 4, P])).then_inc(*now.did("masked", d, c))
                dve.wait_ge(*after("masked", d, c))
            V.tensor_tensor(sc[:, c, :], sc[:, c, :], work[1], ALU.add).then_inc(*now.did("sc", c))
            dve.wait_ge(*after("sc", c))

        later_modulation(0)
        later_modulation(1)
        log_sigmoid("zc", lac, 0, TC, 0)
        log_sigmoid("zc", lac, 1, TC, 2)
        later_modulation(2)
        log_sigmoid("z", la, 0, TT, 4)
        later_modulation(3)
        log_sigmoid("z", la, 1, TT, 8)
        later_modulation(4)
        for d in range(2):
            decayed("cumc", d, 1)
        later_modulation(5)
        decayed("cum", 0, 2)
        later_modulation(6)
        decayed("cum", 1, 2)
        later_modulation(7)
        scores(0)
        scores(1)
        for step in range(2):
            states(step, 0)
            states(step, 1)
        states(2, 0)
        states(3, 0)
        scores(2)
        states(4, 0)
        states(2, 1)
        scores(3)
        modulation_columns("ada2", 7, ((mod, "mod2"),), 16)
        states(3, 1)
        states(4, 1)
        modulation_sums("ada2", 8, [ada_sums])
        for h in range(HEADS):
            dve.wait_ge(*after("o_rms", h))
            r = work[h % 2]
            V.reciprocal(r, r).then_inc(*now.did("o_rstd", h))
            dve.wait_ge(*after("o_rstd", h))
            for vt in range(2):
                t = 2 * h + vt
                dve.wait_ge(*after("oT", t))
                stt(oT[:, t, :], oT[:, t, :], col("gla_norm_g", t), r, ALU.mult, ALU.mult).then_inc(
                    *now.did("o_normed", t))

        now = dve_in["mix"]
        for t in range(DT):
            dve.wait_ge(*after("silu_r", t))
            dve.wait_ge(*after("o_normed", t))
            mul(oT[:, t, :], oT[:, t, :], silu_r[:, t, :]).then_inc(*now.did("ob", t))
            if t % 2 and t >= 1:
                later_modulation(9 + t // 2)
        for b in range(13, ADA_REST):
            later_modulation(b)
        modulation_columns("ada2", ADA_REST - 1, ((mod, "mod2"),), 16)
        dve.wait_ge(*after("mod2", ADA_REST - 1))
        stt(gs2, mod[:, 32:40], 1.0, cols[:, COL["norm2_g"]:COL["norm2_g"] + 8], ALU.add, ALU.mult).then_inc(
            *now.did("gs2"))
        for k in range(DT):
            tile_left("ob", k, oT, ob_hi, ob_lo)
        weights_left("br_b", 0, br_b_hi)
        weights_left("br_b", 1, br_b_hi)
        dve.wait_ge(*after("psum", "gb", DT - 1))
        for k in range(DT):
            tile_left("hm", k, hT, hm_hi, h_lo)
        for t in range(DT):
            dve.wait_ge(*after("psum", "br_b", t))
            dve.wait_ge(*after("sgb", t))
            mul(sgb[:, t, :], bank("br_b", t), sgb[:, t, :]).then_inc(*now.both(("mb", t), ("free", "br_b", t)))
            if t % 2:
                weights_left(*(("br_b", t // 2 + 2, br_b_hi) if t < 4 else ("ga", t // 2 - 2, ga_hi)))
        weights_left("ga", 2, ga_hi)
        weights_left("ga", 3, ga_hi)
        for b in range(4):
            weights_left("vs", b, ga_hi)
        weights_left("u", 0, u_hi)
        weights_left("u", 1, u_hi)
        for n in range(TT):
            for b in range(4):
                dve.wait_ge(*after("vs", b, n // 2))
            for half in range(2):
                V.bn_stats(bn[:, n, half, :], vs_tok[:, n, half * 512:(half + 1) * 512]).then_inc(
                    *now.did("bn", n, half))
            dve.wait_ge(*after("bn", n, 1))
            V.bn_aggr(mv[:, n, :], bn[:, n, :, :].rearrange("p h s -> p (h s)")).then_inc(*now.did("mv", n))
        weights_left("u", 2, u_hi)
        dve.wait_ge(*after("ln_std"))
        V.reciprocal(ln_r, ln_r).then_inc(*now.did("ln_r"))
        dve.wait_ge(*after("ln_r"))
        dve.wait_ge(*after("ln_g"))
        dve.wait_ge(*after("ln_b"))
        for n in range(TT):
            V.tensor_scalar(vs_tok[:, n, :], vs_tok[:, n, :], mv[:, n, 0:1], ln_r[:, n:n + 1], ALU.subtract,
                            ALU.mult).then_inc(*now.did("vn0", n))
            dve.wait_ge(*after("vn0", n))
            mul(vs_tok[:, n, :], vs_tok[:, n, :], ln_g).then_inc(*now.did("vn1", n))
            dve.wait_ge(*after("vn1", n))
            V.tensor_tensor(vs_tok[:, n, :], vs_tok[:, n, :], ln_b, ALU.add).then_inc(*now.did("vn", n))
            if n == 1:
                weights_left("u", 3, u_hi)
        weights_left("br_a", 0, br_a_hi)
        for g in range(SGU_G):
            dve.wait_ge(*after("psum", "s", g))
            dve.wait_ge(*after("guT", g))
            mul(guT[:, g, :], bank("s", g), guT[:, g, :]).then_inc(*now.both(("aT", g), ("free", "s", g)))
            if g:
                tile_left("aT", g - 1, guT, a_hi, a_lo)
            if g == 5:
                weights_left("br_a", 1, br_a_hi)
        tile_left("aT", SGU_G - 1, guT, a_hi, a_lo)
        for t in range(DT):
            dve.wait_ge(*after("psum", "br_a", t))
            dve.wait_ge(*after("sga", t))
            mul(sga[:, t, :], bank("br_a", t), sga[:, t, :]).then_inc(*now.both(("ma", t), ("free", "br_a", t)))
            dve.wait_ge(*after("ma", t))
            dve.wait_ge(*after("mb", t))
            V.tensor_tensor(sga[:, t, :], sga[:, t, :], sgb[:, t, :], ALU.add).then_inc(*now.did("merged", t))
            if t:
                tile_left("merged", t - 1, sga, m_hi, m_lo)
            if t in (1, 3, 5):
                weights_left(*(("br_a", t // 2 + 2) if t < 4 else ("w_o", 0)), br_a_hi)
        tile_left("merged", DT - 1, sga, m_hi, m_lo)
        weights_left("w_o", 1, br_a_hi)
        for t in range(DT):
            dve.wait_ge(*after("psum", "w_o", t))
            dve.wait_ge(*after("mod2", ADA_REST - 1))
            stt(xT[:, t, :], bank("w_o", t), mod[:, 16 + t:17 + t], xT[:, t, :], ALU.mult, ALU.add).then_inc(
                *now.both(("x1", t), ("free", "w_o", t)))
            if t in (1, 3):
                weights_left("w_o", t // 2 + 2, br_a_hi)
            if t == 5:
                weights_left("up", 0, up_hi)

        now = dve_in["ffn"]
        V.memset(pads, 0.0).then_inc(*now.did("pads"))
        dve.wait_ge(*after("rms", "2"))
        V.reciprocal(rstd2[:, 0, :], rstd2[:, 0, :]).then_inc(*now.did("rstd2"))
        dve.wait_ge(*after("rstd2"))
        dve.wait_ge(*after("gs2"))
        for k in range(DT):
            stt(hT[:, k, :], xT[:, k, :], gs2[:, k:k + 1], rstd2[:, 0, :], ALU.mult, ALU.mult).then_inc(
                *now.did("h2T_scaled", k))
        for k in range(DT):
            dve.wait_ge(*after("h2_hi", k))
            stt(h_lo[:, k, :], hT[:, k, :], mod[:, 24 + k:25 + k], h_hi[:, k, :].bitcast(F32), ALU.add,
                ALU.subtract).then_inc(*now.did("h2_lo", k))
        weights_left("up", 1, up_hi)
        for t in range(FT):
            a = acc[:, t % 4, :].rearrange("p (y x) -> p y x", x=GRID)
            dve.wait_ge(*after("conv", t, 0))
            for tap in range(1, 9):
                ky, kx = tap // 3, tap % 3
                stt(a, pads[:, t % 4, ky:ky + ROWS, kx:kx + GRID], col("conv_w", tap * FT + t), a, ALU.mult,
                    ALU.add).then_inc(*now.did("conv", t, tap))
                dve.wait_ge(*after("conv", t, tap))
            if t:
                gate_values(t - 1)
            if t + 2 < FT:
                weights_left("up", t + 2, up_hi)
            else:
                weights_left("down", t + 2 - FT, up_hi[2:])
        gate_values(FT - 1)

        def products_left(name, hi, src, lo):
            for k in range(FT):
                dve.wait_ge(*after(name, k))
                dve.wait_ge(*after(name + "_hi", k))
                V.tensor_tensor(lo[:, k, :], src[:, k, :], hi[k].bitcast(F32), ALU.subtract).then_inc(
                    *now.did(name + "_lo", k))

        products_left("gT", g_hi, gT, g_lo)
        weights_left("down", 2, up_hi[2:])
        weights_left("down", 3, up_hi[2:])
        for b in range(4):
            for t in (2 * b, 2 * b + 1):
                dve.wait_ge(*after("psum", "down", t))
                stt(xT[:, t, :], bank("down", t), mod[:, 40 + t:41 + t], xT[:, t, :], ALU.mult, ALU.add).then_inc(
                    *now.both(("x2", t), ("free", "down", t)))
            for n in range(3 * b + 4, min(3 * b + 7, 12)):
                weights_left("down", n, up_hi[2:])
        dve.wait_ge(*after("rms", "3"))
        V.reciprocal(rstd2[:, 1, :], rstd2[:, 1, :]).then_inc(*now.did("rstd3"))
        dve.wait_ge(*after("rstd3"))
        for k in range(DT):
            stt(x2T[:, k, :], xT[:, k, :], col("final_norm_g", k), rstd2[:, 1, :], ALU.mult, ALU.mult).then_inc(
                *now.did("x2T", k))

        now = dve_in["rwkv"]
        dve.wait_ge(dve_in["ffn"].sem, dve_in["ffn"].count)
        mu = cols[:, COL["rw_mu"]:COL["rw_mu"] + 15]
        ka = cols[:, COL["k_a"]:COL["k_a"] + 4]
        V.tensor_scalar(mix_half, mu, 0.5, None, ALU.mult).then_inc(*now.did("mix_half"))
        V.tensor_scalar(mix_one, mu, -1.0, 1.0, ALU.mult, ALU.add).then_inc(*now.did("mix_one"))
        V.tensor_scalar(half_ka, ka, 0.5, None, ALU.mult).then_inc(*now.did())
        V.tensor_scalar(rest_ka, ka, -0.5, 1.0, ALU.mult, ALU.add).then_inc(*now.did())
        V.tensor_scalar(half_a0, cols[:, COL["a0"]:COL["a0"] + 8], 0.5, None, ALU.mult).then_inc(*now.did("half"))
        V.memset(state_m, 0.0).then_inc(*now.did())
        V.memset(raw[:, :, 0:1], 0.0).then_inc(*now.did())
        V.memset(raw[:, :, L + 1:L + 2], 0.0).then_inc(*now.did("raw_zero"))
        dve.wait_ge(*after("mix_half"))
        def key_squares(hp):
            if hp >= 2:
                dve.wait_ge(*after("psum", "kk", hp - 2))
            V.tensor_scalar(nkkT[:, hp, :], rkT[:, hp, :], col("k_k", hp), None, ALU.mult).then_inc(
                *now.did("kk_raw", hp))
            dve.wait_ge(*after("kk_raw", hp))
            mul(kk_sq[:, hp % 2, :], nkkT[:, hp, :], nkkT[:, hp, :]).then_inc(*now.did("kk_sq", hp))

        def keys_normalised(hp):
            n = kk_n[:, hp % 2, :]
            dve.wait_ge(*after("kk_norm", hp))
            V.tensor_scalar(n, n, 1e-12, None, ALU.max).then_inc(*now.did("kk_max", hp))
            dve.wait_ge(*after("kk_max", hp))
            V.reciprocal(n, n).then_inc(*now.did("kk_inv", hp))
            dve.wait_ge(*after("kk_inv", hp))
            stt(nkkT[:, hp, :], nkkT[:, hp, :], -1.0, n, ALU.mult, ALU.mult).then_inc(*now.did("nkk", hp))

        def mix(i):
            t = RW_TILES[i]
            dve.wait_ge(*after("raw", t))
            V.tensor_tensor(pair_sum[:, i % 2, :], raw[:, i % 3, 0:L], raw[:, i % 3, 2:L + 2], ALU.add).then_inc(
                *now.did("pair_sum", t))
            dve.wait_ge(*after("pair_sum", t))
            dve.wait_ge(*after("mixed0", t))
            stt(mixed[t], pair_sum[:, i % 2, :], mix_half[:, t:t + 1], mixed[t], ALU.mult, ALU.add).then_inc(
                *now.did("mixed", t))
            dve.wait_ge(*after("mixed", t))
            if t == 7:
                key_squares(0)
                key_squares(1)
            if t == 0:
                key_squares(2)
                key_squares(3)
            if t in (1, 2, 3, 8):
                keys_normalised((1, 2, 3, 8).index(t))

        for i in range(14):
            mix(i)

        def as_chunks(ap):
            return ap.rearrange("p (c t) -> p c t", c=TT)

        def prepare(j, part):
            hp, d = JOBS[j]
            s = sets[j % 2]
            inc, exc = (slice(1, P + 1), slice(0, P)) if d == 0 else (slice(0, P), slice(1, P + 1))
            plus = exps[:, 0:2].rearrange("p a c j -> p (a c) j")
            minus = exps[:, 2:4].rearrange("p a c j -> p (a c) j")
            dve.wait_ge(now.sem, now.count)
            if part == 0:
                dve.wait_ge(*after("a", j))
                V.tensor_scalar(job_t, aT, half_ka[:, hp:hp + 1], rest_ka[:, hp:hp + 1], ALU.mult, ALU.add).then_inc(
                    *now.did("job_t", j))
                dve.wait_ge(*after("job_t", j))
                mul(kdT, job_t, rkT[:, hp, :]).then_inc(*now.did("kd", j))
            if part == 1:
                V.tensor_scalar(job_t, aT, -0.5, -0.5, ALU.mult, ALU.add).then_inc(*now.did("job_t2", j))
                dve.wait_ge(*after("job_t2", j))
                mul(job_t, job_t, nkkT[:, hp, :]).then_inc(*now.did("kka", j))
                if d == 0:
                    V.tensor_copy(kd_sum, kdT).then_inc(*now.did("kd_sum", hp))
                else:
                    V.tensor_tensor(kd_sum, kd_sum, kdT, ALU.add).then_inc(*now.did("kd_sum2", hp))
            if part == 2:
                dve.wait_ge(*after("rexp", j))
                mul(as_chunks(bkT[:, 0, :]), as_chunks(job_t), minus[:, :, 0:P]).then_inc(*now.did("job_b", j))
                mul(as_chunks(bkT[:, 1, :]), as_chunks(kdT), minus[:, :, 0:P]).then_inc(*now.did("job_k", j))
                if d == 1:
                    stt(kd_sum, kd_sum, col("r_k", hp), rT[:, hp, :], ALU.mult, ALU.mult).then_inc(
                        *now.did("bonus_in", hp))
            if part == 3:
                mul(s["ar"][:, :, 0, :], as_chunks(nkkT[:, hp, :]), plus[:, :, exc]).then_inc(*now.did("job_a", j))
                mul(s["ar"][:, :, 1, :], as_chunks(rT[:, hp, :]), plus[:, :, inc]).then_inc(*now.did("job_r", j))
                V.tensor_copy(job_stats[:, j % 2, :, :], plus[:, :, P + 1:CUM]).then_inc(*now.did("job_stats", j))

        def gram(j, i, cp):
            d = JOBS[j][1]
            dst = sets[j % 2][("nqb", "mqk")[i]]
            for h in range(2):
                dve.wait_ge(*after("psum", "gram", j, i, cp, h))
                mul(dst[:, 4 * cp + h:4 * cp + h + 3:2, :, :].rearrange("p n a t -> p n (a t)"),
                    bank("gram", j, i, cp, h).rearrange("p (n t) -> p n t", n=2),
                    pair_mask[d].unsqueeze(1).to_broadcast([P, 2, 2 * P])).then_inc(
                    *now.both(("gram", j, i, cp, h), ("free", "gram", j, i, cp, h)))

        def inverse_start(j):
            s = sets[j % 2]
            dve.wait_ge(*after("gram", j, 0, 1, 1))
            lt = s["nqb"][:, :, 0, :]
            V.tensor_tensor(lt, lt, ident.unsqueeze(1).to_broadcast([P, 8, P]), ALU.add).then_inc(*now.did("lt", j))
            dve.wait_ge(*after("lt", j))
            mul(s["g"], lt, level_mask[1 - JOBS[j][1]][0].unsqueeze(1).to_broadcast([P, 8, P])).then_inc(
                *now.did("g0", j))

        def bonus(j):
            hp, d = JOBS[j]
            if d == 1:
                dve.wait_ge(*after("psum", "bonus", hp))
                mul(rvT[:, hp, :], bank("bonus", hp), rvT[:, hp, :]).then_inc(
                    *now.both(("bonus", hp), ("free", "bonus", hp)))

        def invert_y(j, lv, half):
            dve.wait_ge(*after("psum", "iy", j, lv, half))
            dve.wait_ge(now.sem, now.count)
            mul(Y[:, 4 * half:4 * half + 4, :], bank("iy", j, lv, half).rearrange("p (s t) -> p s t", s=4),
                level_mask[JOBS[j][1]][lv + 1].unsqueeze(1).to_broadcast([P, 4, P])).then_inc(
                *now.both(("yi", j, lv, half), ("free", "iy", j, lv, half)))

        def chain_start(j, step):
            if step:
                c = order[JOBS[j][1]][step]
                dve.wait_ge(*after("state", j, step))
                for h, rows in enumerate((LO, HI)):
                    V.tensor_scalar(state_m[rows, h * RH:(h + 1) * RH], state[rows, j % 2, :],
                                    job_stats[rows, j % 2, c, 0:1], None, ALU.mult).then_inc(
                        *(now.did("state_m", j, step) if h else now.did()))

        def chain_sa(j, step):
            dve.wait_ge(now.sem, now.count)
            dve.wait_ge(*after("psum", "cs", j, step))
            V.tensor_copy(sab, bank("cs", j, step)[:, 0:P].rearrange("p (h v) -> p h v", h=2)).then_inc(
                *now.both(("sa", j, step), ("free", "cs", j, step)))

        def chain_end(j, step):
            hp, d = JOBS[j]
            c = order[d][step]
            dve.wait_ge(now.sem, now.count)
            if step < 3:
                dve.wait_ge(*after("psum", "ch", j, step))
                st = job_stats[:, j % 2, c, :]
                s = state[:, j % 2, :]
                if step == 0:
                    V.tensor_scalar(s, bank("ch", j, step)[:, 0:64], st[:, 2:3], None, ALU.mult).then_inc(
                        *now.both(("state", j, 1), ("free", "ch", j, step)))
                else:
                    V.tensor_scalar(state_t, bank("ch", j, step)[:, 0:64], st[:, 2:3], None, ALU.mult).then_inc(
                        *now.both(("state_t", j, step), ("free", "ch", j, step)))
                    dve.wait_ge(*after("state_t", j, step))
                    stt(s, s, st[:, 1:2], state_t, ALU.mult, ALU.add).then_inc(*now.did("state", j, step + 1))
            dve.wait_ge(*after("psum", "cy", j, step))
            y = yT[:, hp, c * P:(c + 1) * P]
            if d == 0:
                ins = V.tensor_copy(y, bank("cy", j, step)[:, 0:P])
            else:
                dve.wait_ge(*after("y_chunk", j - 1, c))
                ins = V.tensor_tensor(y, bank("cy", j, step)[:, 0:P], y, ALU.add)
            ins.then_inc(*now.both(("y_chunk", j, c), ("y", j), ("free", "cy", j, step)))

        for part in range(4):
            prepare(0, part)
        mix(14)
        gram(0, 0, 0)
        gram(0, 0, 1)
        inverse_start(0)
        for j in range(len(JOBS) + 1):
            new, old, ahead = j < len(JOBS), j > 0, j + 1 < len(JOBS)
            if new:
                gram(j, 1, 0)
            if old:
                chain_sa(j - 1, 0)
            if new:
                gram(j, 1, 1)
                bonus(j)
            if old:
                chain_end(j - 1, 0)
            for lv in range(5):
                chained = old and lv < 3
                if chained:
                    chain_start(j - 1, lv + 1)
                if new:
                    invert_y(j, lv, 0)
                    invert_y(j, lv, 1)
                if chained:
                    chain_sa(j - 1, lv + 1)
                    chain_end(j - 1, lv + 1)
                if ahead and lv < 4:
                    prepare(j + 1, lv)
            if new:
                first, second = (LO, HI) if JOBS[j][1] == 0 else (HI, LO)
                dve.wait_ge(*after("psum", "il", j, 0))
                V.tensor_copy(Y[second, :, first], bank("il", j, 0)[second, :].rearrange("p (s t) -> p s t", s=8)
                              ).then_inc(*now.both(("y_last", j), ("free", "il", j, 0)))
            if ahead:
                gram(j + 1, 0, 0)
            if new:
                dve.wait_ge(*after("psum", "il", j, 1))
                V.tensor_copy(sets[j % 2]["g"][first, :, second],
                              bank("il", j, 1)[first, :].rearrange("p (s t) -> p s t", s=8)).then_inc(
                    *now.both(("g_done", j), ("free", "il", j, 1)))
            if ahead:
                gram(j + 1, 0, 1)
                inverse_start(j + 1)

        dve.wait_ge(now.sem, now.count)
        for hp in range(HT):
            dve.wait_ge(*after("psum", "ym", hp))
            dve.wait_ge(*after("y", 2 * hp + 1))
            stt(yT[:, hp, :], bank("ym", hp), -1.0 / RH, yT[:, hp, :], ALU.mult, ALU.add).then_inc(
                *now.both(("yc", hp), ("free", "ym", hp)))
            dve.wait_ge(*after("yc", hp))
            mul(y_sq[:, hp, :], yT[:, hp, :], yT[:, hp, :]).then_inc(*now.did("y_sq", hp))
        for hp in range(HT):
            r = gn_s[:, hp % 2, :]
            dve.wait_ge(*after("gn_std", hp))
            V.reciprocal(r, r).then_inc(*now.did("gn_r", hp))
            dve.wait_ge(*after("gn_r", hp))
            stt(yT[:, hp, :], yT[:, hp, :], col("gn_w", hp), r, ALU.mult, ALU.mult).then_inc(*now.did("yn", hp))
            dve.wait_ge(*after("yn", hp))
            dve.wait_ge(*after("bonus", hp))
            stt(yT[:, hp, :], yT[:, hp, :], col("gn_b", hp), rvT[:, hp, :], ALU.add, ALU.add).then_inc(
                *now.did("yb", hp))
            dve.wait_ge(*after("yb", hp))
            dve.wait_ge(*after("psum", "g", hp))
            mul(yT[:, hp, :], bank("g", hp), yT[:, hp, :]).then_inc(*now.both(("yT", hp), ("free", "g", hp)))

        now = dve_in["hyena"]
        dve.wait_ge(dve_in["rwkv"].sem, dve_in["rwkv"].count)
        V.memset(raw_h[:, :, 0:1], 0.0).then_inc(*now.did())
        V.memset(raw_h[:, :, L + 1:L + 2], 0.0).then_inc(*now.did("raw_zero2"))
        for t in range(12):
            dve.wait_ge(*after("hy0", t))
            stt(hyT[:, t, :], raw_h[:, t % 3, 0:L], col("hy_conv_w", t), hyT[:, t, :], ALU.mult, ALU.add).then_inc(
                *now.did("hy1", t))
            dve.wait_ge(*after("hy1", t))
            stt(hyT[:, t, :], raw_h[:, t % 3, 2:L + 2], col("hy_conv_w", 24 + t), hyT[:, t, :], ALU.mult,
                ALU.add).then_inc(*now.did("hyT", t))
        for o in range(2):
            Hc, Hs = Hcs[o]
            for q in range(2):
                dve.wait_ge(now.sem, now.count)
                z = [[prod[:, 2 * cs + m, :] for m in range(2)] for cs in range(2)]
                y = [[prod[:, 4 + 2 * cs + m, :] for m in range(2)] for cs in range(2)]
                for cs in range(2):
                    dve.wait_ge(*after("Z_even", o, cs, q))
                    dve.wait_ge(*after("psum", "Z", o, cs, q, 1))
                    even, odd = z_even[:, cs, :], bank("Z", o, cs, q, 1)
                    V.tensor_tensor(z[cs][0], even, odd, ALU.add).then_inc(*now.did("z", o, q, cs, 0))
                    if cs == 0:
                        ins = V.tensor_tensor(z[cs][1], even, odd, ALU.subtract)
                    else:
                        ins = V.tensor_tensor(z[cs][1], odd, even, ALU.subtract)
                    ins.then_inc(*now.both(("z", o, q, cs, 1), ("free", "Z", o, cs, q, 1)))
                dve.wait_ge(*after("H", o))
                dve.wait_ge(now.sem, now.count)
                for m in range(2):
                    hc, hs = Hc[:, 2 * m + q, :], Hs[:, 2 * m + q, :]
                    mul(y[0][m], z[0][m], hc).then_inc(*now.did("zc_hc", o, q, m))
                    mul(y[1][m], z[1][m], hc).then_inc(*now.did("zs_hc", o, q, m))
                    dve.wait_ge(*after("zs_hc", o, q, m))
                    mul(z[0][m], z[0][m], hs).then_inc(*now.did("zc_hs", o, q, m))
                    mul(z[1][m], z[1][m], hs).then_inc(*now.did("zs_hs", o, q, m))
                    dve.wait_ge(*after("zs_hs", o, q, m))
                    V.tensor_tensor(y[0][m], y[0][m], z[1][m], ALU.subtract).then_inc(*now.did("yc", o, q, m))
                    V.tensor_tensor(y[1][m], y[1][m], z[0][m], ALU.add).then_inc(*now.did("ys", o, q, m))
                dve.wait_ge(*after("ys", o, q, 1))
                for cs in range(2):
                    for e in range(2):
                        op = ALU.add if cs == e else ALU.subtract
                        V.tensor_tensor(Ycs[cs][:, 2 * e + q, :], y[cs][0], y[cs][1], op).then_inc(
                            *now.did("Y", o, cs, 2 * e + q))
            for tt in range(TT):
                dve.wait_ge(*after("psum", "conv", o, tt))
                if o == 0:
                    dve.wait_ge(*after("x1_tok", tt))
                    out, gate, name = xv_tok[:, tt, :], x1_tok[:, tt, :], ("z2", tt)
                else:
                    out, gate, name = zT[:, tt, :], hyT[:, 8 + tt, :], ("zT", tt)
                src = bank("conv", o, tt)
                if o == 1:
                    out, gate = (a.rearrange("p (t e) -> p e t", e=2) for a in (out, gate))
                    src = src.rearrange("p (e t) -> p e t", e=2)
                stt(out, src, 1.0 / L, gate, ALU.mult, ALU.mult).then_inc(*now.both(name, ("free", "conv", o, tt)))

        now = dve_in["ffn2"]
        dve.wait_ge(dve_in["hyena"].sem, dve_in["hyena"].count)
        for k in range(DT):
            tile_left("x2T", k, x2T, x2_hi, x2_lo)
        for b in range(4, 8):
            weights_left("gates", b, out_hi)
        for t in range(DT):
            dve.wait_ge(*after("psum", "rwo", t))
            dve.wait_ge(*after("gate", 8 + t))
            mul(gate_r[:, t, :], bank("rwo", t), gate_r[:, t, :]).then_inc(*now.both(("mr", t), ("free", "rwo", t)))
        for t in range(DT):
            dve.wait_ge(*after("psum", "hyo", t))
            dve.wait_ge(*after("gate", t))
            mul(gate_h[:, t, :], bank("hyo", t), gate_h[:, t, :]).then_inc(*now.both(("mh", t), ("free", "hyo", t)))
            dve.wait_ge(*after("mh", t))
            dve.wait_ge(*after("mr", t))
            V.tensor_tensor(gate_h[:, t, :], gate_h[:, t, :], gate_r[:, t, :], ALU.add).then_inc(
                *now.did("merged2", t))
            if t:
                tile_left("merged2", t - 1, gate_h, m2_hi, m2_lo)
            if t in (1, 6):
                weights_left("w_o2", t // 6, out_hi)
        tile_left("merged2", DT - 1, gate_h, m2_hi, m2_lo)
        for n, group in enumerate(("w_o2", "down2")):
            for t in range(DT):
                dve.wait_ge(*after("psum", group, t))
                stt(x2T[:, t, :], x2T[:, t, :], ALPHA, bank(group, t), ALU.mult, ALU.add).then_inc(
                    *now.both(("res%d" % n, t), ("free", group, t)))
                if n == 0 and t in (1, 3):
                    weights_left("w_o2", t // 2 + 2, out_hi)
                if (n, t) == (0, 5):
                    weights_left("up2", 0, up2_hi)
                if n == 1 and t % 2:
                    for i in range(3 * (t // 2) + 4, min(3 * (t // 2) + 7, 12)):
                        weights_left("down2", i, up2_hi[2:])
            dve.wait_ge(now.sem, now.count)
            dve.wait_ge(*after("psum", "lm%d" % n))
            mean = norm_s[:, 1, :]
            V.tensor_scalar(mean, bank("lm%d" % n), 1.0 / D, None, ALU.mult).then_inc(
                *now.both(("mean", n), ("free", "lm%d" % n)))
            dve.wait_ge(*after("mean", n))
            for t in range(DT):
                V.tensor_tensor(lnc[:, t, :], x2T[:, t, :], mean, ALU.subtract).then_inc(*now.did("lnc", n, t))
            dve.wait_ge(*after("ln_std2", n))
            r = norm_s[:, 0, :]
            V.reciprocal(r, r).then_inc(*now.did("ln_rstd", n))
            dve.wait_ge(*after("ln_rstd", n))
            for t in range(DT):
                stt(lnc[:, t, :], lnc[:, t, :], col("ln%d_w" % (n + 1), t), r, ALU.mult, ALU.mult).then_inc(
                    *now.did("lnn", n, t))
            if n == 0:
                for k in range(DT):
                    dve.wait_ge(*after("x3_hi", k))
                    V.tensor_tensor(x_lo[:, k, :], x2T[:, k, :], x_hi[:, k, :].bitcast(F32), ALU.subtract).then_inc(
                        *now.did("x3_lo", k))
                weights_left("up2", 1, up2_hi)
                for t in range(FT):
                    dve.wait_ge(*after("psum", "fu", t))
                    dve.wait_ge(*after("silu_g", t))
                    mul(gT2[:, t, :], bank("fu", t), silu_g[:, t % 4, :]).then_inc(
                        *now.both(("gT2", t), ("free", "fu", t)))
                    if t + 2 < FT:
                        weights_left("up2", t + 2, up2_hi)
                    else:
                        weights_left("down2", t + 2 - FT, up2_hi[2:])
                products_left("gT2", g2_hi, gT2, g2_lo)
                weights_left("down2", 2, up2_hi[2:])
                weights_left("down2", 3, up2_hi[2:])

    @block.scalar
    def _(act):

        def run(out, src, func, **kw):
            return nc.scalar.activation(out, src, func, **kw)

        def tile_rounded(name, k, src, hi):
            act.wait_ge(*after(name, k))
            run(hi[:, k, :], src[:, k, :], ACT.Copy).then_inc(*now.did(name + "_hi", k))

        def weights_rounded(name, n, parts):
            at_block = POSITION[name, n]
            act.wait_ge(*after("block", at_block))
            if (n >= len(parts) and name != "gates") or name == "w_o":
                act.wait_ge(*after(*block_done[at_block - len(parts)]))
            run(parts[n % len(parts)], ring[:, at_block % RING, :], ACT.Copy).then_inc(*now.did("w_hi", name, n))

        def eps(i, rows=slice(0, P)):
            return eps_cols[rows, i:i + 1]

        now = act_in["start"]
        first = CONST["gla_cum"]
        act.dma_start(cols[:, :], io["cols"]).then_inc(*loads["cols"].loaded("cols"))
        act.dma_start(consts[:, 0:first], io["consts"][:, 0:first]).then_inc(*loads["consts"].loaded("consts"))
        act.dma_start(ctxT, io["ctxT"]).then_inc(*loads["ctx"].loaded("ctx"))
        act.dma_start(xT, io["xT"]).then_inc(*loads["x"].loaded("x"))
        act.dma_start(window, io["window"]).then_inc(*loads["window"].loaded("window"))
        act.dma_start(at(5, 2048), io["dft"][:, 0:2048]).then_inc(*loads["dft_first"].loaded("dft_first"))
        act.dma_start(consts[:, first:], io["consts"][:, first:]).then_inc(*loads["masks"].loaded("masks"))
        act.wait_ge(*after("cols"))
        run(csil[:, :, 0], cols[:, COL["c"]:COL["c"] + 8], ACT.Silu).then_inc(*now.did())
        run(csil[:, :, 1], cols[:, COL["c_ctx"]:COL["c_ctx"] + 8], ACT.Silu).then_inc(*now.did("csil"))
        def filter_layer(n, meanwhile=()):
            act.wait_ge(*after("filt_sb"))
            act.wait_ge(*after("psum", "filt", n))
            run(filt_a, bank("filt", n)[0:64, :], ACT.Identity, scale=col("filt_sf", n, slice(0, 64)),
                bias=filt_sb[0:64, n:n + 1]).then_inc(*now.both(("filt_a", n), ("free", "filt", n)))
            for src, dst, name, source in meanwhile:
                act.wait_ge(*after(source))
                for k in range(DT):
                    run(dst[:, k, :], src[:, k, :], ACT.Square).then_inc(*now.did(name, k))
            act.wait_ge(*after("filt_r", n))
            run(filt_h, filt_a, ACT.Sin).then_inc(*now.did("filt_h", n))

        filter_layer(0, [(ctxT, sqc, "sqc", "ctx")])
        filter_layer(1, [(xT, sq, "sq", "x")])
        filter_layer(2)

        def mean_square(which, n):
            act.wait_ge(*after("psum", "ss_" + which))
            act.wait_ge(*after("eps"))
            run(rstd[:, n, 0:(L, LC)[n]], bank("ss_" + which)[:, 0:(L, LC)[n]], ACT.Sqrt, scale=1.0 / D,
                bias=eps(0)).then_inc(*now.both(("rms", which), ("free", "ss_" + which)))

        mean_square("c", 1)
        mean_square("x", 0)
        for g in range(4):
            for q in range(2):
                n = 2 * g + q
                for e in range(2):
                    act.wait_ge(*after("psum", "H", g // 2, g % 2, q, e))
                    if n >= 2:
                        act.wait_ge(*after("spectrum", n - 2))
                    run(halves[:, 2 * (n % 2) + e, :], bank("H", g // 2, g % 2, q, e), ACT.Copy).then_inc(
                        *now.both(("half", n, e), ("free", "H", g // 2, g % 2, q, e)))
        for k in range(DT):
            act.wait_ge(*after("hcT_scaled", k))
            run(hcT[:, k, :], hcT[:, k, :], ACT.Identity, bias=modc[:, k:k + 1]).then_inc(*now.did("hcT", k))
        for k in range(DT):
            act.wait_ge(*after("hT_scaled", k))
            run(hT[:, k, :], hT[:, k, :], ACT.Identity, bias=mod[:, k:k + 1]).then_inc(*now.did("hT", k))

        now = act_in["gla"]
        def keys(b):
            for t in (2 * b, 2 * b + 1):
                act.wait_ge(*after("psum", "kc", t))
                run(kcT[:, t, :], bank("kc", t)[:, 0:LC], ACT.Copy).then_inc(*now.both(("kcT", t), ("free", "kc", t)))
                act.wait_ge(*after("psum", "k", t))
                run(kT[:, t, :], bank("k", t), ACT.Copy).then_inc(*now.both(("kT", t), ("free", "k", t)))

        def queries(b):
            for t in (2 * b, 2 * b + 1):
                act.wait_ge(*after("psum", "q", t))
                run(qT[:, t, :], bank("q", t), ACT.Copy, scale=DK ** -0.5).then_inc(
                    *now.both(("qT", t), ("free", "q", t)))

        def evacuate_tokens(group, b, half, dst, func, name):
            act.wait_ge(*after("psum", group, b, half))
            run(dst[:, 2 * half:2 * half + 2, b * BLK:(b + 1) * BLK],
                bank(group, b, half).rearrange("p (i c) -> p i c", i=2), func).then_inc(
                *now.both(name, ("free", group, b, half)))

        def values(b):
            evacuate_tokens("vc", b, 0, vc_tok, ACT.Copy, ("vc_tok", b))
            evacuate_tokens("v", b, 0, v_tok, ACT.Copy, ("v_tok0", b))
            evacuate_tokens("v", b, 1, v_tok, ACT.Copy, ("v_tok", b))

        zs = [("zc", d, tt) for d in range(2) for tt in range(TC)] + [("z", d, tt) for d in range(2) for tt in range(TT)]

        def log_sigmoid(first):
            batch = list(enumerate(zs))[first:first + 4]
            for i, (group, d, tt) in batch:
                act.wait_ge(*after("psum", group, d, tt))
                if i >= 8:
                    act.wait_ge(*after(*("free",) + zs[i - 8]))
                run(soft[i % 8], bank(group, d, tt), ACT.Abs).then_inc(*now.did("abs", i))
            for i, z in batch:
                act.wait_ge(*after("abs", i))
                run(soft[i % 8], soft[i % 8], ACT.Exp, scale=-1.0).then_inc(*now.did("exp_z", i))
            for i, z in batch:
                act.wait_ge(*after("exp_z", i))
                run(soft[i % 8], soft[i % 8], ACT.Ln, bias=eps(3)).then_inc(*now.did("soft", *z))

        exp_count = [0]

        def exponentials(group, d, cps):
            inc = slice(1, P + 1) if d == 0 else slice(0, P)
            for h in range(HEADS):
                for cp in range(cps):
                    e = exp_count[0]
                    exp_count[0] += 1
                    act.wait_ge(*after("psum", group, d, h, cp))
                    if e >= 2:
                        act.wait_ge(*after("exp_used", e - 2))
                    ps = bank(group, d, h, cp)[:, 0:2 * CUM].rearrange("p (c j) -> p c j", c=2)
                    run(exps[:, e % 2], ps, ACT.Exp).then_inc(*now.did())
                    run(exps[:, 2 + e % 2, :, 0:P], ps[:, :, inc], ACT.Exp, scale=-1.0).then_inc(
                        *now.both(("exp", group, d, h, cp), ("free", group, d, h, cp)))

        def key_tokens(group, dst, chunks, name):
            for d in range(2):
                for c in range(chunks):
                    act.wait_ge(*after("psum", group, d, c))
                    run(dst[d][:, c, :], bank(group, d, c), ACT.Copy).then_inc(
                        *now.both((name, d, c), ("free", group, d, c)))

        act.wait_ge(*after("psum", "lrc"))
        act.wait_ge(*after("lr_ones"))
        run(lrcT[0:32, :], bank("lrc")[0:32, 0:LC], ACT.Copy).then_inc(*now.both(("lrcT",), ("free", "lrc")))
        act.wait_ge(*after("psum", "lr"))
        run(lrT[0:32, :], bank("lr")[0:32, :], ACT.Copy).then_inc(*now.both(("lrT",), ("free", "lr")))
        keys(0)
        act.wait_ge(*after("spectrum", 7))
        act.wait_ge(*after("spectrum_stored", 2))
        act.wait_ge(*after("spectrum_stored", 3))
        log_sigmoid(0)
        keys(1)
        log_sigmoid(4)
        queries(0)
        log_sigmoid(8)
        queries(1)
        for d in range(2):
            exponentials("cumc", d, 1)
        values(0)
        exponentials("cum", 0, 2)
        values(1)
        exponentials("cum", 1, 2)
        values(2)
        key_tokens("ktc", kc_tok, TC, "kc_tok")
        evacuate_tokens("vc", 3, 0, vc_tok, ACT.Copy, ("vc_tok", 3))
        key_tokens("kt", k_tok, TT, "k_tok")

        def decayed_states(i, hp):
            for d in range(2):
                c = order[d][i]
                for h in (2 * hp, 2 * hp + 1):
                    act.wait_ge(*after("s", 1 + i, d, h))
                    run(sm[d][h][c], s_gla[4 * d + h], ACT.Copy, scale=stats_x[:, d, h, c, 0:1]).then_inc(
                        *now.did("sm", d, h, c))

        decayed_states(0, 0)
        decayed_states(0, 1)
        evacuate_tokens("v", 3, 0, v_tok, ACT.Copy, ("v_tok0", 3))
        decayed_states(1, 0)
        decayed_states(2, 0)
        evacuate_tokens("v", 3, 1, v_tok, ACT.Copy, ("v_tok", 3))
        decayed_states(3, 0)
        for i in range(1, TT):
            decayed_states(i, 1)

        def output_rms(h):
            act.wait_ge(*after("psum", "oss", h))
            if h >= 2:
                act.wait_ge(*after("o_normed", 2 * (h - 2) + 1))
            run(work[h % 2], bank("oss", h), ACT.Sqrt, scale=1.0 / DV, bias=eps(0)).then_inc(
                *now.both(("o_rms", h), ("free", "oss", h)))

        for h in range(HEADS):
            for t in (2 * h, 2 * h + 1):
                act.wait_ge(*after("psum", "o", t))
                run(oT[:, t, :], bank("o", t), ACT.Copy).then_inc(*now.did("oT", t))
                if h >= 2:
                    act.wait_ge(*after("psum", "oss", h - 2))
                run(osq[:, t % 4, :], bank("o", t), ACT.Square).then_inc(*now.both(("osq", t), ("free", "o", t)))
            if h >= 1:
                output_rms(h - 1)

        now = act_in["mix"]

        def evacuate(group, t, dst, func, name, **kw):
            act.wait_ge(*after("psum", group, t))
            run(dst, bank(group, t), func, **kw).then_inc(*now.both((name, t), ("free", group, t)))

        for t in range(DT):
            evacuate("r", t, silu_r[:, t, :], ACT.Silu, "silu_r")
            if t == 1:
                output_rms(HEADS - 1)
        for t in range(DT):
            evacuate("gb", t, sgb[:, t, :], ACT.Sigmoid, "sgb")
            if t < 4:
                tile_rounded("ob", 2 * t, oT, ob_hi)
                tile_rounded("ob", 2 * t + 1, oT, ob_hi)
            if t == 5:
                weights_rounded("br_b", 0, br_b_hi)
        weights_rounded("br_b", 1, br_b_hi)
        for k in range(DT):
            act.wait_ge(*after("hT", k))
            run(hm_hi[:, k, :], hT[:, k, :], ACT.Copy).then_inc(*now.did("hm_hi", k))
        weights_rounded("br_b", 2, br_b_hi)
        weights_rounded("br_b", 3, br_b_hi)
        weights_rounded("ga", 0, ga_hi)
        weights_rounded("ga", 1, ga_hi)
        for t in range(DT):
            evacuate("ga", t, sga[:, t, :], ACT.Sigmoid, "sga")
            if t % 2:
                weights_rounded(*(("ga", t // 2 + 2) if t < 4 else ("vs", t // 2 - 2)), ga_hi)
        for b in range(4):
            for half in range(2):
                evacuate_tokens("vs", b, half, vs_tok, ACT.Gelu, ("vs", b, half))
            if b < 2:
                weights_rounded("vs", b + 2, ga_hi)
            else:
                act.wait_ge(*after("ob", DT - 1))
                weights_rounded("u", b - 2, u_hi)
        for t in range(DT):
            evacuate("u", t, guT[:, t, :], ACT.Gelu, "guT")
            if t % 2:
                weights_rounded(*(("u", t // 2 + 2, u_hi) if t < 4 else ("br_a", t // 2 - 2, br_a_hi)))
            if t == 1:
                act.wait_ge(*after("mv", 3))
                run(ln_r, mv[:, :, 1], ACT.Sqrt, bias=eps(0)).then_inc(*now.did("ln_std"))
        for g in range(SGU_G):
            tile_rounded("aT", g, guT, a_hi)
        for b in range(4):
            if b < 3:
                weights_rounded(*(("br_a", b + 2) if b < 2 else ("w_o", 0)), br_a_hi)
            tile_rounded("merged", 2 * b, sga, m_hi)
            tile_rounded("merged", 2 * b + 1, sga, m_hi)
        weights_rounded("w_o", 1, br_a_hi)
        for k in range(DT):
            act.wait_ge(*after("x1", k))
            run(sq5[:, k, :], xT[:, k, :], ACT.Square).then_inc(*now.did("sq2", k))
            if k in (1, 3):
                weights_rounded("w_o", k // 2 + 2, br_a_hi)
            if k in (4, 6):
                weights_rounded("up", k // 2 - 2, up_hi)
        act.wait_ge(*after("psum", "ss2"))
        run(rstd2[:, 0, :], bank("ss2"), ACT.Sqrt, scale=1.0 / D, bias=eps(0)).then_inc(
            *now.both(("rms", "2"), ("free", "ss2")))

        now = act_in["ffn"]
        for k in range(DT):
            act.wait_ge(*after("h2T_scaled", k))
            run(h_hi[:, k, :], hT[:, k, :], ACT.Identity, bias=mod[:, 24 + k:25 + k]).then_inc(
                *now.did("h2_hi", k))
        act.wait_ge(*after("pads"))

        def gelu(t):
            act.wait_ge(*after("conv", t, 8))
            run(acc[:, t % 4, :], acc[:, t % 4, :], ACT.Gelu).then_inc(*now.did("gelu", t))

        for t in range(FT):
            act.wait_ge(*after("psum", "fa", t))
            if t >= 4:
                act.wait_ge(*after("conv", t - 4, 8))
            run(pads[:, t % 4, 1:1 + ROWS, 1:1 + GRID], bank("fa", t).rearrange("p (y x) -> p y x", x=GRID),
                ACT.Copy).then_inc(*now.both(("pad", t), ("free", "fa", t)))
            act.wait_ge(*after("pad", t))
            if t >= 4:
                act.wait_ge(*after("gT", t - 4))
            run(acc[:, t % 4, :].rearrange("p (y x) -> p y x", x=GRID), pads[:, t % 4, 0:ROWS, 0:GRID], ACT.Identity,
                scale=col("conv_w", t), bias=col("conv_b", t)).then_inc(*now.did("conv", t, 0))
            if t:
                gelu(t - 1)
            if t + 2 < FT:
                weights_rounded("up", t + 2, up_hi)
            else:
                weights_rounded("down", t + 2 - FT, up_hi[2:])
        gelu(FT - 1)

        def products_rounded(name, hi, src, last):
            for k in range(FT):
                act.wait_ge(*after(*last))
                act.wait_ge(*after(name, k))
                run(hi[k], src[:, k, :], ACT.Copy).then_inc(*now.did(name + "_hi", k))

        products_rounded("gT", g_hi, gT, ("psum", "fv", FT - 1))
        weights_rounded("down", 2, up_hi[2:])
        weights_rounded("down", 3, up_hi[2:])
        for b in range(4):
            for k in (2 * b, 2 * b + 1):
                act.wait_ge(*after("x2", k))
                run(sq1[:, k, :], xT[:, k, :], ACT.Square).then_inc(*now.did("sq3", k))
            for n in range(3 * b + 4, min(3 * b + 7, 12)):
                weights_rounded("down", n, up_hi[2:])
        act.wait_ge(*after("psum", "ss3"))
        run(rstd2[:, 1, :], bank("ss3"), ACT.Sqrt, scale=1.0 / D, bias=eps(0)).then_inc(
            *now.both(("rms", "3"), ("free", "ss3")))

        now = act_in["rwkv"]
        act.wait_ge(*after("raw_zero"))
        act.wait_ge(*after("mix_one"))
        def key_norm(hp):
            if hp >= 2:
                act.wait_ge(*after("nkk", hp - 2))
            evacuate("kk", hp, kk_n[:, hp % 2, :], ACT.Sqrt, "kk_norm")

        def project(i):
            t = RW_TILES[i]
            if i >= 3:
                act.wait_ge(*after("mixed", RW_TILES[i - 3]))
            evacuate("rw", t, raw[:, i % 3, 1:L + 1], ACT.Copy, "raw")
            act.wait_ge(*after("raw", t))
            run(mixed[t], raw[:, i % 3, 1:L + 1], ACT.Copy, scale=mix_one[:, t:t + 1]).then_inc(
                *now.did("mixed0", t))
            if t == 4:
                act.wait_ge(*after("mixed", 12))
                run(wdT, wdT, ACT.Tanh).then_inc(*now.did("wd_tanh"))
            if t == 1:
                key_norm(0)
                key_norm(1)
            if t in (7, 2):
                d = (7, 2).index(t)
                for tt in range(TT):
                    act.wait_ge(*after("psum", "w", d, tt))
                    run(lw[d][:, tt, :], bank("w", d, tt), ACT.Sigmoid).then_inc(
                        *now.both(("lw", d, tt), ("free", "w", d, tt)))
            if t in (2, 3):
                key_norm(t)

        for i in range(14):
            project(i)
        act.wait_ge(*after("half"))

        def inputs(j):
            hp, d = JOBS[j]
            inc = slice(1, P + 1) if d == 0 else slice(0, P)
            if j:
                act.wait_ge(*after("job_stats", j - 1))
            evacuate("a", j, aT, ACT.Tanh, "a", scale=0.5, bias=half_a0[:, 4 * d + hp:4 * d + hp + 1])
            for cp in range(2):
                act.wait_ge(*after("psum", "rcum", j, cp))
                ps = bank("rcum", j, cp)[:, 0:2 * CUM].rearrange("p (c j) -> p c j", c=2)
                run(exps[:, cp], ps, ACT.Exp).then_inc(*now.did())
                run(exps[:, 2 + cp, :, 0:P], ps[:, :, inc], ACT.Exp, scale=-1.0).then_inc(
                    *now.both(("rexp", j), ("free", "rcum", j, cp)))

        def tokens(j):
            for i, dst in ((0, "b_tok"), (1, "k_tok")):
                act.wait_ge(*after("psum", "tok", j, i))
                run(sets[j % 2][dst], bank("tok", j, i).rearrange("p (c f) -> p c f", c=4), ACT.Copy).then_inc(
                    *now.both(("tok", j, i), ("free", "tok", j, i)))

        def inverse_start(j, half):
            act.wait_ge(*after("psum", "x0", j, half))
            run(X[:, 4 * half:4 * half + 4, :], bank("x0", j, half).rearrange("p (s t) -> p s t", s=4),
                ACT.Copy).then_inc(*now.both(("x", j, 0, half), ("free", "x0", j, half)))

        def invert_xg(j, lv, half):
            for what, dst, name in (("ix", X, "x"), ("ig", sets[j % 2]["g"], "g")):
                act.wait_ge(*after("psum", what, j, lv, half))
                part = (LO, HI)[JOBS[j][1]] if (what, lv) == ("ix", 4) else slice(0, P)
                run(dst[:, 4 * half:4 * half + 4, part],
                    bank(what, j, lv, half).rearrange("p (s t) -> p s t", s=4)[:, :, part], ACT.Copy).then_inc(
                        *now.both((name, j, lv + 1, half), ("free", what, j, lv, half)))

        def chain_u(j, step):
            act.wait_ge(*after("psum", "cu", j, step))
            run(ub, bank("cu", j, step)[:, 0:P].rearrange("p (h v) -> p h v", h=2), ACT.Copy).then_inc(
                *now.both(("u", j, step), ("free", "cu", j, step)))

        inputs(0)
        project(14)
        for c in range(TT):
            evacuate("vt", c, rv_tok[:, c, :], ACT.Copy, "rv_tok")
        tokens(0)
        act.wait_ge(*after("mixed", 14))
        run(gdT, gdT, ACT.Sigmoid).then_inc(*now.did("gd_sig"))
        for j in range(len(JOBS) + 1):
            new, old, ahead = j < len(JOBS), j > 0, j + 1 < len(JOBS)
            if old:
                chain_u(j - 1, 0)
            if new:
                inverse_start(j, 0)
                inverse_start(j, 1)
            if ahead:
                inputs(j + 1)
            for lv in range(5):
                if old and lv < 3:
                    chain_u(j - 1, lv + 1)
                if new:
                    invert_xg(j, lv, 0)
                    invert_xg(j, lv, 1)
            if ahead:
                tokens(j + 1)
        for hp in range(HT):
            act.wait_ge(*after("psum", "yv", hp))
            if hp >= 2:
                act.wait_ge(*after("yn", hp - 2))
            run(gn_s[:, hp % 2, :], bank("yv", hp), ACT.Sqrt, scale=1.0 / RH, bias=eps(2)).then_inc(
                *now.both(("gn_std", hp), ("free", "yv", hp)))

        now = act_in["hyena"]
        act.wait_ge(*after("raw_zero2"))
        for t in range(12):
            if t >= 3:
                act.wait_ge(*after("hyT", t - 3))
            evacuate("hy", t, raw_h[:, t % 3, 1:L + 1], ACT.Copy, "hraw")
            act.wait_ge(*after("hraw", t))
            run(hyT[:, t, :], raw_h[:, t % 3, 1:L + 1], ACT.Identity, scale=col("hy_conv_w", 12 + t),
                bias=col("hy_conv_b", t)).then_inc(*now.did("hy0", t))
        for c in range(TT):
            evacuate("hvt", c, xv_tok[:, c, :], ACT.Copy, "xv_tok")
        for c in range(TT):
            evacuate("hxt", c, x1_tok[:, c, :], ACT.Copy, "x1_tok")
        for o in range(2):
            for q in range(2):
                for cs in range(2):
                    act.wait_ge(*after("psum", "Z", o, cs, q, 0))
                    if (o, q) > (0, 0):
                        act.wait_ge(*after("z", *((o, 0) if q else (o - 1, 1)), cs, 1))
                    run(z_even[:, cs, :], bank("Z", o, cs, q, 0), ACT.Copy).then_inc(
                        *now.both(("Z_even", o, cs, q), ("free", "Z", o, cs, q, 0)))
            for t in (2 * o, 2 * o + 1):
                evacuate("gate", t, gate_h[:, t, :], ACT.Sigmoid, "gate")

        now = act_in["ffn2"]
        for t in range(4, 2 * DT):
            evacuate("gate", t, (gate_h if t < DT else gate_r)[:, t % DT, :], ACT.Sigmoid, "gate")
            if t == 4:
                for k in range(DT):
                    tile_rounded("x2T", k, x2T, x2_hi)
            if t in (6, 7, 9, 11):
                weights_rounded("gates", (4, 5, 6, 7)[(6, 7, 9, 11).index(t)], out_hi)
        for t in range(DT):
            if t in (0, 4):
                weights_rounded("w_o2", t // 4, out_hi)
            tile_rounded("merged2", t, gate_h, m2_hi)
        weights_rounded("w_o2", 2, out_hi)
        weights_rounded("w_o2", 3, out_hi)
        weights_rounded("up2", 0, up2_hi)
        weights_rounded("up2", 1, up2_hi)
        for n in range(2):
            for t in range(DT):
                act.wait_ge(*after("lnc", n, t))
                run(lnsq[:, t, :], lnc[:, t, :], ACT.Square).then_inc(*now.did("lnsq%d" % n, t))
            act.wait_ge(*after("psum", "lv%d" % n))
            run(norm_s[:, 0, :], bank("lv%d" % n), ACT.Sqrt, scale=1.0 / D, bias=eps(1)).then_inc(
                *now.both(("ln_std2", n), ("free", "lv%d" % n)))
            for t in range(DT):
                act.wait_ge(*after("lnn", n, t))
                run(x2T[:, t, :], lnc[:, t, :], ACT.Identity, bias=col("ln%d_b" % (n + 1), t)).then_inc(
                    *now.did("x3T" if n == 0 else "out", t))
                if n == 0:
                    act.wait_ge(*after("x3T", t))
                    run(x_hi[:, t, :], x2T[:, t, :], ACT.Copy).then_inc(*now.did("x3_hi", t))
            if n == 0:
                for t in range(FT):
                    if t >= 4:
                        act.wait_ge(*after("gT2", t - 4))
                    evacuate("fg", t, silu_g[:, t % 4, :], ACT.Silu, "silu_g")
                    if t + 2 < FT:
                        weights_rounded("up2", t + 2, up2_hi)
                    else:
                        weights_rounded("down2", t + 2 - FT, up2_hi[2:])
                products_rounded("gT2", g2_hi, gT2, ("psum", "fu", FT - 1))
                for i in range(2, 12):
                    weights_rounded("down2", i, up2_hi[2:])

    @block.gpsimd
    def _(pool):

        def load(name, dst, src=None):
            pool.dma_start(dst, io[name] if src is None else src).then_inc(*loads[name].loaded(name))

        load("skip", skip_row)
        now = pool_in["start"]
        for g in range(4):
            half = spectra[:, 4 * (g % 2):4 * (g % 2) + 4, :]
            if g >= 2:
                pool.wait_ge(*after("spectrum_stored", g - 2))
            for q in range(2):
                n = 2 * g + q
                pool.wait_ge(*after("half", n, 1))
                even, odd = (halves[:, 2 * (n % 2) + e, :] for e in range(2))
                nc.gpsimd.tensor_tensor(half[:, q, :], even, odd, ALU.add).then_inc(*now.did("spectrum_low", n))
                a, b = (even, odd) if g % 2 == 0 else (odd, even)
                nc.gpsimd.tensor_tensor(half[:, 2 + q, :], a, b, ALU.subtract).then_inc(*now.did("spectrum", n))
            pool.wait_ge(*after("spectrum", n))
            pool.dma_start(io["spectra"][:, g], half).then_inc(*spectra_stored[g % 2].loaded("spectrum_stored", g))
        pool.wait_ge(*after("psum", "H", 1, 1, 1, 1))
        load("gla_w2", gla_w2)
        pool.wait_ge(*after("psum", "oss", HEADS - 1))
        load("ln_g", ln_g, io["ln_g"].partition_broadcast(P))
        load("ln_b", ln_b, io["ln_b"].partition_broadcast(P))
        load("w_s", w_sT)
        load("b_s", b_s)

        def add_tiles(out, tiles_in, ready):
            for k in range(1, DT):
                pool.wait_ge(*after(ready, k))
                if k > 1:
                    pool.wait_ge(*after(ready + "_part", k - 1))
                nc.gpsimd.tensor_tensor(out, tiles_in[:, 0, :] if k == 1 else out, tiles_in[:, k, :], ALU.add).then_inc(
                    *now.did(*((ready + "_part", k) if k < DT - 1 else (ready + "_sum",))))

        now = pool_in["ffn"]
        add_tiles(sq5[:, 0, :], sq5, "sq2")
        add_tiles(sq1[:, 0, :], sq1, "sq3")
        pool.wait_ge(*after("psum", "ss3"))
        load("rw_small", at(2, 2 * L, 2048).rearrange("p (n c) -> p n c", n=2))
        pool.dma_start(rw_w2, io["rw_w2"]).then_inc(*loads["rw_small"].loaded("rw_w2"))
        load("w0", w0_row)
        last = len(JOBS) - 1
        pool.wait_ge(*after("y", last))
        pool.wait_ge(*after("spectrum_stored", 2))
        pool.wait_ge(*after("spectrum_stored", 3))
        pool.dma_start(at(6, U), io["dft"]).then_inc(*loads["dft"].loaded("dft"))
        pool.dma_start(at(7, U).rearrange("p (s f n) -> p s f n", s=2, f=TT), io["spectra"][:, 0:2]).then_inc(
            *loads["H0"].loaded("H", 0))
        for c in range(TT):
            pool.wait_ge(*after("psum", "hvt", c))
            pool.wait_ge(*after("psum", "hxt", c))
        pool.dma_start(at(3, U).rearrange("p (s f n) -> p s f n", s=2, f=TT), io["spectra"][:, 2:4]).then_inc(
            *loads["H1"].loaded("H", 1))
        now = pool_in["ffn2"]
        add_tiles(res_sum, x2T, "res0")
        add_tiles(res_sum, x2T, "res1")

    @block.sync
    def _(sp):
        for name, dst in (("featsT", featsT), ("fw1", fw1), ("fw2", fw23[0]), ("fw3", fw23[1])):
            sp.dma_start(dst, io[name]).then_inc(*loads["filters"].loaded("filters"))
        sp.dma_start(fw4, io["fw4"]).then_inc(*loads["filters_out"].loaded("filters_out"))
        for n in range(NBLOCKS):
            if n == POSITION["hy_in", 1]:
                sp.wait_ge(*after("psum", "gram", len(JOBS) - 1, 1, 1, 1))
            if n >= RING:
                sp.wait_ge(*after(*block_done[n - RING]))
            sp.dma_start(ring[:, n % RING, :], io["weights"][n]).then_inc(*slot_loaded[n % RING].loaded("block", n))
        for t in range(DT):
            sp.wait_ge(*after("out", t))
            sp.dma_start(io["out"][:, t, :], x2T[:, t, :]).then_inc(*out_stored.loaded("stored", t))
        sp.wait_ge(*after("stored", DT - 1))



def _constants():
    eye = np.eye(P, dtype=np.float32)
    i, j = np.arange(P)[:, None], np.arange(P)[None, :]
    head = (i // RH == j // RH).astype(np.float32)

    def cumulative(d, unit):
        at = np.arange(P + 1)[None, :]
        if d == 0:
            upto, first = (i < at).astype(np.float64), (i < P // 2).astype(np.float64)
        else:
            upto, first = (i >= at).astype(np.float64), (i >= P // 2).astype(np.float64)
        one = np.ones_like(first)
        return np.concatenate([upto - first, first, one, one - first], 1) * unit

    def level(d, m):
        a, b = (i, j) if d == 0 else (j, i)
        return ((a // (2 * m) == b // (2 * m)) & (a // m > b // m)) | (i == j)

    later = [(j >= i), (j <= i)]
    strict = [(j > i), (j < i)]
    parts = [eye, np.ones((P, P)), head]
    parts += [cumulative(d, 1.0 / 16.0) for d in range(2)]
    parts += [cumulative(d, DECAY) for d in range(2)]
    parts += later
    parts += [x for d in range(2) for x in (strict[d], later[d])]
    parts += [level(d, m) for d in range(2) for m in [1] + LEVELS]
    table = np.concatenate([np.asarray(x, np.float64) for x in parts], 1).astype(np.float32)
    assert table.shape == (P, NCONST)

    tokens = np.concatenate([np.arange(0, L, 2), np.arange(1, L, 2)])
    t, f = tokens.reshape(2, L // 2, 1), np.arange(L // 2).reshape(1, 1, L // 2)
    angle = 2.0 * np.pi * ((t * (2 * f + 1)) % (4 * L)) / (4.0 * L)
    both = np.stack([np.cos(angle), np.sin(angle)])
    both = np.stack([both, both.transpose(0, 1, 3, 2)])
    dft = both.reshape(2, 2, 2, 2, P, L // 2).transpose(4, 0, 1, 2, 3, 5).reshape(P, U).astype(np.float32)
    time = np.linspace(0.0, 1.0, L, dtype=np.float32)[:, None]
    w = (2.0 * math.pi * np.arange(L, dtype=np.float32) / L).astype(np.float32)
    bands = np.linspace(1e-4, 15, 16, dtype=np.float32)
    ang = (w[:, None] * bands[None, :]).astype(np.float32)
    feats = np.concatenate([time, np.cos(ang), -np.sin(ang)], 1).astype(np.float32)
    deltas = np.abs(np.linspace(math.log(1e-2) / 1.5, math.log(1e-2) / 0.3, HW, dtype=np.float32))
    window = np.exp(-time * deltas[None, :]).astype(np.float32)
    return table, dft, np.ascontiguousarray(feats[tokens].T), window[tokens].reshape(TT, P, HW).transpose(1, 0, 2)


def _blocks(w, width=BLK):
    k, n = w.shape
    kt = 2048 // width
    rows, colsn = -(-k // (kt * P)) * kt * P, -(-n // width) * width
    if (rows, colsn) != (k, n):
        padded = np.zeros((rows, colsn), w.dtype)
        padded[:k, :n] = w
        w = padded
    w = w.reshape(rows // (kt * P), kt, P, colsn // width, width)
    return w.transpose(3, 0, 2, 1, 4).reshape(-1, P, kt * width)


def kernel(**inputs):
    import concourse.bacc as bacc
    from concourse.bass_utils import run_bass_kernel_spmd

    a = {k: np.asarray(v) for k, v in inputs.items()}
    m = {k: (v[0] if v.shape[:1] == (1,) else v) for k, v in a.items()}

    offs = np.cumsum([0, 1024, 1024, 512, 1024, 1024, 1024, 512, 1024, 32])
    u, vs, q, r, ga, gb, k, v, lr = (m["w_in"][:, offs[i]:offs[i + 1]] for i in range(9))
    up, up2g, up2u = (_blocks(w) for w in (m["ffn_w_up"], m["ffn_w_gate_2"], m["ffn_w_up_2"]))
    half = FT // 2
    w_in2 = m["w_in_2"]
    streams = {
        "ada1": _blocks(m["w_ada"][:, :2048]), "ada2": _blocks(m["w_ada"][:, 2048:]),
        "k": _blocks(k), "v": _blocks(v), "lr": _blocks(lr), "q": _blocks(q), "r": _blocks(r), "gb": _blocks(gb),
        "br_b": _blocks(m["w_br_b"]), "ga": _blocks(ga), "vs": _blocks(vs), "u": _blocks(u),
        "br_a": _blocks(m["w_br_a"]), "w_o": _blocks(m["w_o"]),
        "up": np.stack([up[:half], up[half:]], 1).reshape(-1, P, 2048), "down": _blocks(m["ffn_w_down"]),
        "rw_in": _blocks(w_in2[:, 1536:3456])[list(RW_ORDER)], "hy_in": _blocks(w_in2[:, :1536]),
        "gates": _blocks(w_in2[:, 3456:]),
        "rw_out": _blocks(m["w_rw_out_2"], 2 * BLK), "hy_out": _blocks(m["w_hy_out_2"], 2 * BLK),
        "w_o2": _blocks(m["w_o_2"]), "up2": np.stack([up2g, up2u], 1).reshape(-1, P, 2048),
        "down2": _blocks(m["ffn_w_down_2"]),
    }
    assert all(len(streams[name]) == n for name, n in STREAM)
    weights = np.stack([streams[name][i] for name, i in BLOCK_ORDER])

    def tile_columns(x, width=P):
        x = x.reshape(-1, width)
        return np.concatenate([x, np.zeros((len(x), P - width), x.dtype)], 1) if width < P else x

    source = {
        "c": m["c"], "c_ctx": a["c_ctx"], "b_ada": m["b_ada"], "norm1_g": m["norm1_g"], "norm2_g": m["norm2_g"],
        "gla_norm_g": m["gla_norm_g"], "final_norm_g": a["final_norm_g"], "conv_w": m["ffn_conv_w"],
        "conv_b": m["ffn_conv_b"], "hy_conv_w": m["hy_conv_w_2"], "hy_conv_b": m["hy_conv_b_2"],
        "rw_mu": m["rw_mu_2"], "a0": m["rw_a0_2"], "k_k": m["rw_k_k_2"], "k_a": m["rw_k_a_2"],
        "r_k": m["rw_r_k_2"], "gn_w": m["rw_gn_w_2"], "gn_b": m["rw_gn_b_2"], "ln1_w": m["ln1_w_2"],
        "ln1_b": m["ln1_b_2"], "ln2_w": m["ln2_w_2"], "ln2_b": m["ln2_b_2"],
        "filt_b": np.stack([m["hy_filt_b1_2"], m["hy_filt_b2_2"], m["hy_filt_b3_2"]]),
        "filt_sf": m["hy_sin_freq_2"],
    }
    table = np.concatenate([tile_columns(source[name], 64 if name.startswith("filt") else P) for name, _ in COLUMNS])
    consts, dft, featsT, window = _constants()

    def feature_major(x):
        return x.T.reshape(DT, P, -1).transpose(1, 0, 2)

    gla_w2 = np.zeros((33, 2, HW), np.float32)
    for d in range(2):
        gla_w2[d * RANK:(d + 1) * RANK, d] = m["gla_w2"][d]
        gla_w2[32, d] = m["gla_b2"][d]
    rw_w2 = np.zeros((P, 2, HW), np.float32)
    for d in range(2):
        rw_w2[d * 64:(d + 1) * 64, d] = m["rw_w2_2"][d]
    arrays = {
        "weights": weights, "cols": table.T, "consts": consts,
        "xT": feature_major(m["x"]), "ctxT": feature_major(m["ctx"]), "gla_w2": gla_w2,
        "ln_g": m["sgu_ln_g"], "ln_b": m["sgu_ln_b"], "w_s": m["sgu_w"].transpose(2, 0, 1),
        "b_s": m["sgu_b"].reshape(1, D),
        "rw_small": np.stack([m["rw_a2_2"].reshape(P, HW), m["rw_g2_2"]], 1), "rw_w2": rw_w2,
        "w0": m["rw_w0_2"].reshape(1, D), "featsT": featsT, "fw1": m["hy_filt_w1_2"], "fw2": m["hy_filt_w2_2"],
        "fw3": m["hy_filt_w3_2"], "fw4": m["hy_filt_w4_2"].reshape(64, 2, 2, HW), "skip": m["hy_skip_2"].reshape(1, D),
        "window": window, "dft": dft,
    }
    arrays = {f"{k}_dram": np.ascontiguousarray(x) for k, x in arrays.items()}

    def declare():
        nc = bacc.Bacc("TRN2", target_bir_lowering=False, num_devices=1)
        io = {k[:-5]: nc.dram_tensor(k, x.shape, F32, kind="ExternalInput").ap() for k, x in arrays.items()}
        io["spectra"] = nc.dram_tensor("spectra_dram", (P, 4, TT, HW), F32, kind="Internal").ap()
        io["out"] = nc.dram_tensor("out_dram", (P, DT, L), F32, kind="ExternalOutput").ap()
        return nc, io

    announced = build(*declare(), None)
    nc, io = declare()
    build(nc, io, announced)
    result = run_bass_kernel_spmd(nc, [arrays], core_ids=[0]).results[0]["out_dram"]
    return np.ascontiguousarray(result.transpose(1, 0, 2).reshape(D, L).T).reshape(1, L, D)
```
